# Optimizing a Trainium2 kernel written in Bass

```python
import jax, jax.numpy as jnp
from jax import lax
import numpy as np

D_MODEL = 1024
BATCH = 1
SEQ = 512
DEPTH = 2
DEC_BATCH = 8
DEC_SEQ = 8
PAST_LEN = 2048
PAGE_SIZE = 128

N_A_LAYERS = DEPTH // 2
N_B_LAYERS = DEPTH - N_A_LAYERS
A_EXPAND = 128
A_HEADS = D_MODEL // A_EXPAND
A_DK = A_EXPAND
A_DV = D_MODEL // A_HEADS
A_CHUNK = 64
B_HEADS = 16
B_HEAD_DIM = D_MODEL // B_HEADS
Q_BLOCK = 128
D_FF = ((8 * D_MODEL // 3 + 255) // 256) * 256
RMS_EPS = 1e-6
MASK_VALUE = -1e30
MIN_F = 1e-30

kernel_name = 'hgrn2_fox_yoco_step'

F32 = jnp.float32

def rmsnorm(x, g):
    xf = x.astype(F32)
    y = xf * lax.rsqrt(jnp.mean(xf * xf, axis=-1, keepdims=True) + RMS_EPS)
    return (y * g.astype(F32)).astype(x.dtype)

def swiglu_ffn(x, g, w_gu, w_down):
    h = rmsnorm(x, g) @ w_gu
    a, b = jnp.split(h, 2, axis=-1)
    return (jax.nn.silu(a) * b) @ w_down

def gla_chunked(q, k, logf, v, s0):
    B, L, H, DK = q.shape
    DV = v.shape[-1]
    c = min(A_CHUNK, L)
    n = -(-L // c)
    pad = n * c - L
    if pad:
        pw = ((0, 0), (0, pad), (0, 0), (0, 0))
        q, k, logf, v = (jnp.pad(t, pw) for t in (q, k, logf, v))

    def chunks(t):
        return t.reshape(B, n, c, H, t.shape[-1]).transpose(1, 0, 3, 2, 4)

    causal = jnp.tril(jnp.ones((c, c), dtype=bool))[None, None, :, :, None]

    def step(S, inp):
        qc, kc, gc, vc = inp
        b = jnp.cumsum(gc, axis=2)
        diff = b[:, :, :, None, :] - b[:, :, None, :, :]
        decay = jnp.where(causal, jnp.exp(jnp.where(causal, diff, 0.0)), 0.0)
        att = jnp.sum(qc[:, :, :, None, :] * kc[:, :, None, :, :] * decay, axis=-1)
        o = jnp.einsum('bhts,bhsv->bhtv', att, vc) + jnp.einsum('bhtd,bhdv->bhtv', qc * jnp.exp(b), S)
        b_last = b[:, :, -1]
        S = jnp.exp(b_last)[..., None] * S + jnp.einsum(
            'bhsd,bhsv->bhdv', kc * jnp.exp(b_last[:, :, None, :] - b), vc)
        return S, o

    s_fin, o = lax.scan(step, s0, (chunks(q), chunks(k), chunks(logf), chunks(v)))
    o = o.transpose(1, 0, 3, 2, 4).reshape(B, n * c, H, DV)[:, :L]
    return o, s_fin

def hgrn2_mixer(x, s0, norm_g, w_in, lb, o_g, w_out):
    B, L, _ = x.shape
    kd = A_HEADS * A_DK
    vd = A_HEADS * A_DV
    h = rmsnorm(x, norm_g) @ w_in
    q, fz, inp, gate = jnp.split(h, [kd, 2 * kd, 2 * kd + vd], axis=-1)
    q = q.reshape(B, L, A_HEADS, A_DK).astype(F32)
    fz = fz.reshape(B, L, A_HEADS, A_DK).astype(F32)
    v = inp.reshape(B, L, A_HEADS, A_DV).astype(F32)
    lb = lb.reshape(A_HEADS, A_DK).astype(F32)
    f = lb + (1.0 - lb) * jax.nn.sigmoid(fz)
    logf = jnp.log(jnp.maximum(f, MIN_F))
    k = (1.0 - lb) * jax.nn.sigmoid(-fz)
    o, s_new = gla_chunked(q, k, logf, v, s0.astype(F32))
    o = rmsnorm(o, o_g).reshape(B, L, vd).astype(x.dtype) * jax.nn.silu(gate)
    return o @ w_out, s_new

def shared_kv(x, kv_g, w_kvf, b_f, k_g):
    B, L, _ = x.shape
    hd = B_HEADS * B_HEAD_DIM
    h = rmsnorm(x, kv_g) @ w_kvf
    k, v, fz = jnp.split(h, [hd, 2 * hd], axis=-1)
    k = rmsnorm(k.reshape(B, L, B_HEADS, B_HEAD_DIM), k_g)
    v = v.reshape(B, L, B_HEADS, B_HEAD_DIM)
    logf = jax.nn.log_sigmoid(fz.astype(F32) + b_f.astype(F32))
    return k, v, logf

def fox_attention(q, k, v, cq, ck, q_pos, k_pos):
    B, Lq, H, Dh = q.shape
    blk = min(Q_BLOCK, Lq)
    nb = -(-Lq // blk)
    pad = nb * blk - Lq
    if pad:
        q = jnp.pad(q, ((0, 0), (0, pad), (0, 0), (0, 0)))
        cq = jnp.pad(cq, ((0, 0), (0, pad), (0, 0)), mode='edge')
        q_pos = jnp.pad(q_pos, (0, pad), mode='edge')
    qb = q.reshape(B, nb, blk, H, Dh).transpose(1, 0, 2, 3, 4)
    cb = cq.reshape(B, nb, blk, H).transpose(1, 0, 3, 2)
    pb = q_pos.reshape(nb, blk)
    ckt = ck.transpose(0, 2, 1)
    scale = Dh ** -0.5

    def block(args):
        qi, ci, pi = args
        s = jnp.einsum('bqhd,bkhd->bhqk', qi, k).astype(F32) * scale
        s = s + ci[..., None] - ckt[:, :, None, :]
        s = jnp.where(k_pos[None, :] <= pi[:, None], s, MASK_VALUE)
        p = jax.nn.softmax(s, axis=-1).astype(v.dtype)
        return jnp.einsum('bhqk,bkhd->bqhd', p, v)

    o = lax.map(block, (qb, cb, pb))
    return o.transpose(1, 0, 2, 3, 4).reshape(B, nb * blk, H, Dh)[:, :Lq]

def run_trunk(x, a_states, past_k, past_v, past_logf,
              a_norm, a_w_in, a_lb_eff, a_onorm, a_w_out,
              kv_norm, w_kvf, b_f, k_norm,
              b_norm, b_wq, q_norm, b_wo,
              ffn_norm, w_gate_up, w_down):
    B, L, _ = x.shape
    past_len = 0 if past_k is None else past_k.shape[1]
    new_a = []
    for layer in range(DEPTH):
        if layer < N_A_LAYERS:
            o, s = hgrn2_mixer(x, a_states[layer], a_norm[layer], a_w_in[layer],
                               a_lb_eff[layer], a_onorm[layer], a_w_out[layer])
            new_a.append(s)
            x = x + o
        else:
            j = layer - N_A_LAYERS
            if j == 0:
                k_new, v_new, logf_new = shared_kv(x, kv_norm, w_kvf, b_f, k_norm)
                if past_k is None:
                    k_all, v_all = k_new, v_new
                    c_all = jnp.cumsum(logf_new, axis=1)
                else:
                    k_all = jnp.concatenate([past_k, k_new.astype(past_k.dtype)], axis=1)
                    v_all = jnp.concatenate([past_v, v_new.astype(past_v.dtype)], axis=1)
                    c_all = jnp.cumsum(jnp.concatenate([past_logf.astype(F32), logf_new], axis=1), axis=1)
                cq = c_all[:, past_len:]
                q_pos = past_len + jnp.arange(L, dtype=jnp.int32)
                k_pos = jnp.arange(past_len + L, dtype=jnp.int32)
            h = rmsnorm(x, b_norm[j])
            q = rmsnorm((h @ b_wq[j]).reshape(B, L, B_HEADS, B_HEAD_DIM), q_norm[j])
            o = fox_attention(q, k_all.astype(q.dtype), v_all.astype(q.dtype), cq, c_all, q_pos, k_pos)
            x = x + o.reshape(B, L, B_HEADS * B_HEAD_DIM) @ b_wo[j]
        x = x + swiglu_ffn(x, ffn_norm[layer], w_gate_up[layer], w_down[layer])
    return x, jnp.stack(new_a), k_new, v_new, logf_new

def setup_inputs(seed: int = 0) -> dict:
    key = jax.random.key(seed)
    ks = jax.random.split(key, 24)
    n_pages = PAST_LEN // PAGE_SIZE
    n_used = DEC_BATCH * n_pages
    n_pool = (5 * n_used + 3) // 4
    res = (2 * DEPTH) ** -0.5
    sd = D_MODEL ** -0.5

    def nrm(k, shape, s):
        return s * jax.random.normal(k, shape, F32)

    def gain(k, shape):
        return 1.0 + 0.05 * jax.random.normal(k, shape, F32)

    page_table = jax.random.permutation(ks[6], n_pool)[:n_used].reshape(DEC_BATCH, n_pages).astype(jnp.int32)
    return {
        'x_prompt': nrm(ks[0], (BATCH, SEQ, D_MODEL), 1.0),
        'x_sample': nrm(ks[1], (DEC_BATCH, DEC_SEQ, D_MODEL), 1.0),
        'state_hgrn': nrm(ks[2], (N_A_LAYERS, DEC_BATCH, A_HEADS, A_DK, A_DV), 0.5),
        'cache_k': nrm(ks[3], (n_pool, PAGE_SIZE, B_HEADS, B_HEAD_DIM), 1.0),
        'cache_v': nrm(ks[4], (n_pool, PAGE_SIZE, B_HEADS, B_HEAD_DIM), 1.0),
        'cache_logf': jax.nn.log_sigmoid(3.0 + jax.random.normal(ks[5], (n_pool, PAGE_SIZE, B_HEADS), F32)),
        'page_table': page_table,
        'a_norm': gain(ks[7], (N_A_LAYERS, D_MODEL)),
        'a_w_in': nrm(ks[8], (N_A_LAYERS, D_MODEL, 2 * A_HEADS * A_DK + 2 * A_HEADS * A_DV), sd),
        'a_lb': nrm(ks[9], (N_A_LAYERS, A_HEADS * A_DK), 0.5),
        'a_onorm': gain(ks[10], (N_A_LAYERS, A_DV)),
        'a_w_out': nrm(ks[11], (N_A_LAYERS, A_HEADS * A_DV, D_MODEL), sd * res),
        'kv_norm': gain(ks[12], (D_MODEL,)),
        'w_kvf': nrm(ks[13], (D_MODEL, 2 * B_HEADS * B_HEAD_DIM + B_HEADS), sd),
        'b_f': 3.0 + nrm(ks[14], (B_HEADS,), 0.1),
        'k_norm': gain(ks[15], (B_HEAD_DIM,)),
        'b_norm': gain(ks[16], (N_B_LAYERS, D_MODEL)),
        'b_wq': nrm(ks[17], (N_B_LAYERS, D_MODEL, B_HEADS * B_HEAD_DIM), sd),
        'q_norm': gain(ks[18], (N_B_LAYERS, B_HEAD_DIM)),
        'b_wo': nrm(ks[19], (N_B_LAYERS, B_HEADS * B_HEAD_DIM, D_MODEL), sd * res),
        'ffn_norm': gain(ks[20], (DEPTH, D_MODEL)),
        'w_gate_up': nrm(ks[21], (DEPTH, D_MODEL, 2 * D_FF), sd),
        'w_down': nrm(ks[22], (DEPTH, D_FF, D_MODEL), (D_FF ** -0.5) * res),
    }

def reference(x_prompt, x_sample, state_hgrn, cache_k, cache_v, cache_logf, page_table,
              a_norm, a_w_in, a_lb, a_onorm, a_w_out,
              kv_norm, w_kvf, b_f, k_norm,
              b_norm, b_wq, q_norm, b_wo,
              ffn_norm, w_gate_up, w_down):
    p = jax.nn.softmax(a_lb.astype(F32), axis=0)
    lb_eff = jnp.cumsum(p, axis=0) - p[:1]
    weights = (a_norm, a_w_in, lb_eff, a_onorm, a_w_out, kv_norm, w_kvf, b_f, k_norm,
               b_norm, b_wq, q_norm, b_wo, ffn_norm, w_gate_up, w_down)

    s0_prompt = jnp.zeros((N_A_LAYERS, x_prompt.shape[0], A_HEADS, A_DK, A_DV), F32)
    y_prompt, hgrn_prompt, k_prompt, v_prompt, logf_prompt = run_trunk(
        x_prompt, s0_prompt, None, None, None, *weights)

    db, n_pages = page_table.shape
    past_len = n_pages * cache_k.shape[1]
    past_k = cache_k[page_table].reshape(db, past_len, B_HEADS, B_HEAD_DIM)
    past_v = cache_v[page_table].reshape(db, past_len, B_HEADS, B_HEAD_DIM)
    past_logf = cache_logf[page_table].reshape(db, past_len, B_HEADS)
    y_sample, hgrn_sample, k_sample, v_sample, logf_sample = run_trunk(
        x_sample, state_hgrn, past_k, past_v, past_logf, *weights)

    return (y_prompt, y_sample, hgrn_prompt, k_prompt, v_prompt, logf_prompt,
            hgrn_sample, k_sample, v_sample, logf_sample)


_drawn_inputs = setup_inputs


def setup_inputs(seed=0):
    import zlib

    import numpy as np

    out = dict(_drawn_inputs(seed))
    spreads = {}
    factors = {'cache_logf': 2.934, 'a_onorm': 3.198, 'b_norm': 8.0, 'q_norm': 8.0}
    for name, (base, spread) in spreads.items():
        noise = np.random.default_rng([zlib.crc32(name.encode()), seed]).standard_normal(out[name].shape)
        drawn = base * np.exp(spread * noise) if base else spread * noise
        out[name] = __import__('jax').numpy.asarray(drawn.astype(out[name].dtype))
    for name, factor in factors.items():
        out[name] = (out[name] * factor).astype(out[name].dtype)
    return out
```

```python
from contextlib import ExitStack

import numpy as np

import concourse.bass as bass
from concourse import mybir

F32 = mybir.dt.float32
F32R = mybir.dt.float32r
I32 = mybir.dt.int32
ACT = mybir.ActivationFunctionType
ALU = mybir.AluOpType
AX = mybir.AxisListType

P = 128
D = 1024
KD = D // P
SEQ = 512
NB, NQ = 8, 8
NS = NB * NQ
T = SEQ + NS
HALF = T // 2
H = 8
BH, DH = 16, 64
FF = 2816
KF = FF // P
PAGES, PAGE = 16, 128
PAST = PAGES * PAGE
EPS = 1e-6
MIN_F = 1e-30
MASK = -1e30
LEVELS = 7
SLEVELS = 3
LN_LIFT = 50


def decay_sums(n, levels, chunk):
    i, t = np.arange(n)[:, None], np.arange(n)[None, :]
    out = []
    for l in range(levels):
        mid = ((t >> (l + 1)) << (l + 1)) + (1 << l)
        late = (t >> l) & 1
        out.append(np.where(late == 1, (i >= mid) & (i <= t), (i > t) & (i < mid)))
    same = i // chunk == t // chunk
    out.append(same & (i <= t))
    out.append(same & (i > t))
    return np.stack(out, axis=1).astype(np.float32)


def split_masks(n, levels):
    s, t = np.arange(n)[:, None], np.arange(n)[None, :]
    out = [(s >> (l + 1) == t >> (l + 1)) & ((s >> l) & 1 == 0) & ((t >> l) & 1 == 1) for l in range(levels)]
    out.append(s == t)
    return np.stack(out, axis=1).astype(np.float32)


def shape_constants():
    i = np.arange(P)
    hq = i[:, None]
    c = {
        "c_ident": np.eye(P),
        "c_ones": np.ones((1, PAST + NQ)),
        "c_mean": np.full((P, P), 1.0 / P),
        "c_headmean": (i[:, None] // DH == i[None, :] // DH) / DH,
        "c_decay": decay_sums(P, LEVELS, P).reshape(P, -1),
        "c_sdecay": decay_sums(NS, SLEVELS, NQ).reshape(NS, -1),
        "c_tri": (i[:, None] <= i[None, :]),
        "c_causal": np.where(i[None, :] <= i[:, None], 0.0, MASK),
        "c_scausal": np.where(np.arange(NQ)[None, :] <= hq % NQ, 0.0, MASK),
        "c_headrow": (np.arange(BH)[:, None] == i[None, :] // NQ),
        "c_pickq": (hq % NQ == np.arange(NQ)[None, :]),
        "c_rowhead": np.repeat(hq // NQ == np.arange(BH)[None, :], DH, axis=1),
        "c_batch": np.repeat(np.arange(NS)[:, None] // NQ == np.arange(NB)[None, :], P, axis=1),
        "c_newtri": ((i[:NS, None] // NQ == i[None, :NS] // NQ) & (i[:NS, None] <= i[None, :NS])),
    }
    c = {k: np.ascontiguousarray(v, dtype=np.float32) for k, v in c.items()}
    c["c_split"] = split_masks(P, LEVELS).reshape(P, -1)
    c["c_ssplit"] = split_masks(NS, SLEVELS).reshape(NS, -1)
    return c


class Core:

    def __init__(self, nc, stack):
        self.nc, self.stack, self.open = nc, stack, []

    def sb(self, stack, name, shape, dt=F32):
        return stack.enter_context(self.nc.sbuf_tensor(name, shape, dt))

    def sem(self, name):
        self.open.append(self.nc.alloc_semaphore(name=name))
        return self.open[-1]

    def retire(self):
        self.nc.clear_and_free_semaphores(self.open)
        self.nc.all_engine_barrier()
        self.open = []


def halves(ap):
    return ap.rearrange("p (a n) -> p a n", a=2)


def load_inputs(k):
    nc, x = k.nc, k.xT
    with ExitStack() as st:
        rows = k.sb(st, "x_rows", [P, 5, D])
        loaded, xrows, turned, stored = (k.sem(n) for n in ("consts_loaded", "x_loaded", "x_turned", "x_stored"))
        n_const = len(k.const_loads)
        with nc.Block() as block:
            @block.sync
            def _(sp):
                sp.dma_start(rows[:, 0:4, :], k.x_prompt.rearrange("b (c p) d -> p (b c) d", p=P)).then_inc(xrows, 16)
                sp.dma_start(rows[0:NS, 4, :], k.x_sample.rearrange("b q d -> (b q) d")).then_inc(xrows, 16)
                for dst, src in k.const_loads:
                    sp.dma_start(dst, src, allow_slow_non_contiguous=True).then_inc(loaded, 16)
                sp.wait_ge(loaded, 16 * n_const)

            @block.tensor
            def _(pe):
                pe.wait_ge(loaded, 16 * n_const)
                pe.wait_ge(xrows, 32)
                for f in range(KD):
                    if f >= 2:
                        pe.wait_ge(stored, f - 1)
                    for c in range(4):
                        nc.tensor.transpose(k.ps[:, 2 * (f % 2), c * P:(c + 1) * P], rows[:, c, f * P:(f + 1) * P], k.ident[:])
                    nc.tensor.transpose(k.ps[:, 2 * (f % 2) + 1, 0:NS], rows[0:NS, 4, f * P:(f + 1) * P],
                                        k.ident[0:NS, 0:NS]).then_inc(turned, 1)

            @block.vector
            def _(dve):
                for f in range(KD):
                    dve.wait_ge(turned, f + 1)
                    nc.vector.tensor_copy(x[:, f, 0:SEQ], k.ps[:, 2 * (f % 2), :])
                    nc.vector.tensor_copy(x[:, f, SEQ:T], k.ps[:, 2 * (f % 2) + 1, 0:NS]).then_inc(stored, 1)


def norm(k, name, gain):
    nc, x = k.nc, k.xT
    with ExitStack() as st:
        sq = k.sb(st, name + "_sq", [P, 2, T])
        rstd = k.sb(st, name + "_rstd", [P, T])
        y = k.sb(st, name + "_y", [P, 2, T])
        squared, summed, logged, scaled, normed, high, low = (
            k.sem(name + s) for s in ("_squared", "_summed", "_logged", "_scaled", "_normed", "_high", "_low"))
        with nc.Block() as block:
            @block.scalar
            def _(act):
                for f in range(KD):
                    if f >= 2:
                        act.wait_ge(summed, f - 1)
                    nc.scalar.activation(sq[:, f % 2, :], x[:, f, :], ACT.Square).then_inc(squared, 1)
                act.wait_ge(summed, KD)
                nc.scalar.activation(halves(rstd[:]), k.ps[:, 0:2, 0:HALF], ACT.Ln, scale=1.0 / KD,
                                     bias=k.eps[:, 0:1]).then_inc(logged, 1)
                act.wait_ge(logged, 1)
                nc.scalar.activation(rstd[:], rstd[:], ACT.Exp, scale=-0.5).then_inc(scaled, 1)
                for f in range(KD):
                    act.wait_ge(normed, f + 1)
                    nc.scalar.activation(k.xh[:, f, :], y[:, f % 2, :], ACT.Copy).then_inc(high, 1)

            @block.tensor
            def _(pe):
                for f in range(KD):
                    pe.wait_ge(squared, f + 1)
                    for a in range(2):
                        mm = nc.tensor.matmul(k.ps[:, a, 0:HALF], k.mean[:], sq[:, f % 2, a * HALF:(a + 1) * HALF],
                                              start=f == 0, stop=f == KD - 1)
                    mm.then_inc(summed, 1)

            @block.vector
            def _(dve):
                dve.wait_ge(scaled, 1)
                for f in range(KD):
                    if f >= 2:
                        dve.wait_ge(low, f - 1)
                    nc.vector.scalar_tensor_tensor(y[:, f % 2, :], x[:, f, :], gain[:, f:f + 1], rstd[:],
                                                   ALU.mult, ALU.mult).then_inc(normed, 1)
                    dve.wait_ge(high, f + 1)
                    nc.vector.tensor_tensor(k.xl[:, f, :], y[:, f % 2, :], k.xh[:, f, :].bitcast(F32),
                                            ALU.subtract).then_inc(low, 1)


def dense(k, name, weight, kt, chunks, ah, al, pairs, col_of, evacuate, swiglu=None):
    nc = k.nc
    w = weight.rearrange("(k p) n -> p k n", p=P)
    loaded = [k.sem(f"{name}_loaded{s}") for s in range(2)]
    free = [k.sem(f"{name}_free{u}") for u in range(2)]
    high, low, used, gated, mixed, parted = (
        k.sem(f"{name}_{s}") for s in ("high", "low", "used", "gated", "mixed", "parted"))
    units = 2 * chunks
    with ExitStack() as st:
        wraw = k.sb(st, name + "_wraw", [P, 2, kt, P])
        wh, wl = (k.sb(st, name + n, [P, 2, kt, P], F32R) for n in ("_wh", "_wl"))
        gate = k.sb(st, name + "_gate", [P, T]) if swiglu else None
        prod = k.sb(st, name + "_prod", [P, T]) if swiglu else None
        with nc.Block() as block:
            @block.sync
            def _(sp):
                sp.sem_inc(low, 2)
                with sp.Fori(0, pairs) as i:
                    for v in range(units):
                        u, c = divmod(v, chunks)
                        sp.wait_ge(low, i * units + v + 1)
                        sp.dma_start(wraw[:, v % 2, :, :], w[:, c * kt:(c + 1) * kt, bass.ds(col_of(i, u), P)]
                                     ).then_inc(loaded[v % 2], 16)

            @block.scalar
            def _(act):
                act.sem_inc(used, 2)
                if swiglu:
                    act.sem_inc(gated, 1)
                with act.Fori(0, pairs) as i:
                    for v in range(units):
                        act.wait_ge(loaded[v % 2], (i * (units // 2) + v // 2) * 16 + 16)
                        act.wait_ge(used, i * units + v + 1)
                        act.activation(wh[:, v % 2, :, :], wraw[:, v % 2, :, :], ACT.Copy).then_inc(high, 1)
                    if swiglu:
                        act.wait_ge(used, i * units + chunks + 2)
                        act.wait_ge(mixed, i + 1)
                        act.activation(halves(gate[:]), k.ps[:, 0:2, 0:HALF], ACT.Silu).then_inc(gated, 1)

            @block.gpsimd
            def _(pool):
                with pool.Fori(0, pairs) as i:
                    for v in range(units):
                        pool.wait_ge(high, i * units + v + 1)
                        pool.tensor_tensor(wl[:, v % 2, :, :], wraw[:, v % 2, :, :],
                                           wh[:, v % 2, :, :].bitcast(F32), ALU.subtract).then_inc(low, 1)

            @block.tensor
            def _(pe):
                with pe.Fori(0, pairs) as i:
                    for v in range(units):
                        u, c = divmod(v, chunks)
                        if c == 0 and swiglu:
                            pe.wait_ge(gated if u == 0 else mixed, i + 1)
                        elif c == 0:
                            pe.wait_ge(free[u], i + 1)
                        pe.wait_ge(low, i * units + v + 3)
                        for t in range(kt):
                            for n, (wt, at) in enumerate(((wh, ah), (wh, al), (wl, ah))):
                                for a in range(2):
                                    mm = pe.matmul(k.ps[:, 2 * u + a, 0:HALF], wt[:, v % 2, t, :],
                                                   at[:, c * kt + t, a * HALF:(a + 1) * HALF],
                                                   start=c == 0 and t == 0 and n == 0,
                                                   stop=c == chunks - 1 and t == kt - 1 and n == 2)
                        mm.then_inc(used, 1)

            @block.vector
            def _(dve):
                if swiglu:
                    dve.sem_inc(mixed, 1)
                else:
                    dve.sem_inc(free[0], 1)
                    dve.sem_inc(free[1], 1)
                with dve.Fori(0, pairs) as i:
                    if not swiglu:
                        for u in range(2):
                            dve.wait_ge(used, i * units + (u + 1) * chunks + 2)
                            evacuate(dve, i, u, k.ps[:, 2 * u:2 * u + 2, 0:HALF]).then_inc(free[u], 1)
                    else:
                        dh, dl = swiglu
                        dve.wait_ge(gated, i + 2)
                        dve.wait_ge(used, i * units + units + 2)
                        dve.tensor_tensor(halves(prod[:]), halves(gate[:]), k.ps[:, 2:4, 0:HALF],
                                          ALU.mult).then_inc(mixed, 1)
                        dve.wait_ge(mixed, i + 2)
                        dve.tensor_copy(dh[:, bass.ds(i * T, T)], prod[:]).then_inc(parted, 1)
                        dve.wait_ge(parted, i * 2 + 1)
                        dve.tensor_tensor(dl[:, bass.ds(i * T, T)], prod[:], dh[:, bass.ds(i * T, T)].bitcast(F32),
                                          ALU.subtract).then_inc(parted, 1)
                        dve.wait_ge(parted, i * 2 + 2)


def hgrn(k):
    nc, ps = k.nc, k.ps
    names = ("staged", "sigmoids", "floored", "lifted", "logged", "logf", "turned", "high", "low", "valued", "summed",
             "decayed", "queries", "keys", "scored", "picked", "attended", "keyed", "keyrows", "read", "copied", "grown", "state",
             "vmasked", "sgrown", "squared", "meant", "rlog", "rstd", "gained", "gated", "ohigh", "olow", "stored", "stored_y", "free")
    e = {n: k.sem("hgrn_" + n) for n in names}
    TILES = 5
    with ExitStack() as st:
        z = k.sb(st, "hg_z", [P, 4, T])
        s0 = k.sb(st, "hg_s0", [P, NB, P])
        lb = k.sb(st, "hg_lb", [P, 2])
        f, kk, gt = (k.sb(st, "hg_" + n, [P, T]) for n in ("f", "k", "gate"))
        tiny = k.sb(st, "hg_tiny", [P, T])
        lf = k.sb(st, "hg_lf", [P, T + NS])
        picked = k.sb(st, "hg_picked", [P, (LEVELS + 1) * P])
        lth, ltl = (k.sb(st, "hg_" + n, [P, P], F32R) for n in ("lth", "ltl"))
        vt = k.sb(st, "hg_vt", [P, P])
        ex = k.sb(st, "hg_ex", [P, LEVELS + 2, P])
        sx = k.sb(st, "hg_sx", [P, SLEVELS + 3, NS])
        att = k.sb(st, "hg_att", [P, P])
        satt = k.sb(st, "hg_satt", [NS, NS])
        kt = k.sb(st, "hg_kt", [P, P])
        vm = k.sb(st, "hg_vm", [NS, NB, P])
        S = k.sb(st, "hg_S", [P, P])
        snew = k.sb(st, "hg_snew", [P, NB, P])
        o = k.sb(st, "hg_o", [P, T])
        osq = k.sb(st, "hg_osq", [P, T])
        orstd = k.sb(st, "hg_orstd", [P, T])
        y = k.sb(st, "hg_y", [P, T])

        def dims(c):
            return (c * P, P, LEVELS, ex) if c < 4 else (SEQ, NS, SLEVELS, sx)

        with nc.Block() as block:
            @block.sync
            def _(sp):
                sp.sem_inc(e["olow"], 1)
                sp.sem_inc(e["free"], 1)
                with sp.Fori(0, H) as h:
                    sp.wait_ge(e["olow"], h + 1)
                    sp.dma_start(z[:], k.z[:].rearrange("p (j h) n -> p j h n", j=4)[:, :, bass.ds(h, 1), :]
                                 .rearrange("p j h n -> p j (h n)")).then_inc(e["staged"], 16)
                    sp.dma_start(s0[:], k.state_hgrn[0].rearrange("b h d v -> h d b v")[bass.ds(h, 1)]
                                 .rearrange("h d b v -> (h d) b v")).then_inc(e["staged"], 16)
                    sp.dma_start(lb[:], k.lb[:, bass.ds(h, 1), :].rearrange("p h c -> p (h c)")).then_inc(e["staged"], 16)
                    sp.wait_ge(e["state"], 5 * h + 4)
                    sp.dma_start(k.out["hgrn_prompt"][0, 0][bass.ds(h, 1)].rearrange("h d v -> (h d) v"), S[:]
                                 ).then_inc(e["stored"], 16)
                    sp.wait_ge(e["state"], 5 * h + 5)
                    sp.dma_start(k.out["hgrn_sample"][0].rearrange("b h d v -> h d b v")[bass.ds(h, 1)]
                                 .rearrange("h d b v -> (h d) b v"), snew[:]).then_inc(e["stored"], 16)
                    sp.wait_ge(e["stored"], 32 * h + 32)
                    sp.sem_inc(e["free"], 1)

            @block.scalar
            def _(act):
                with act.Fori(0, H) as h:
                    act.wait_ge(e["staged"], 48 * h + 48)
                    act.activation(f[:], z[:, 1, :], ACT.Sigmoid)
                    act.activation(kk[:], z[:, 1, :], ACT.Sigmoid, scale=-1.0)
                    act.activation(gt[:], z[:, 3, :], ACT.Silu).then_inc(e["sigmoids"], 1)
                    act.wait_ge(e["lifted"], h + 1)
                    act.activation(lf[:, 0:T], f[:], ACT.Ln).then_inc(e["logged"], 1)
                    for c in range(TILES):
                        t0, n, levels, x = dims(c)
                        m = 5 * h + c + 1
                        act.wait_ge(e["turned"], m)
                        act.activation(lth[0:n, :], ps[0:n, 0, 0:P], ACT.Copy).then_inc(e["high"], 1)
                        act.wait_ge(e["valued"], m)
                        act.wait_ge(e["summed"], m)
                        if c < 4:
                            for g in range(3):
                                ins = act.activation(x[:, 3 * g:3 * g + 3, :], ps[:, 1 + g, 0:3 * P].rearrange(
                                    "p (a b) -> p a b", a=3), ACT.Exp)
                        else:
                            ins = act.activation(x[:, 0:SLEVELS + 2, :], ps[:, 1, 0:5 * NS].rearrange("p (a b) -> p a b", a=5), ACT.Exp)
                        ins.then_inc(e["decayed"], 1)
                        act.wait_ge(e["keyed"], m)
                        act.activation(kt[0:n, :], ps[0:n, 0, 2 * P:3 * P], ACT.Copy).then_inc(e["keyrows"], 1)
                    act.wait_ge(e["copied"], 5 * h + 5)
                    act.activation(osq[:], o[:], ACT.Square).then_inc(e["squared"], 1)
                    act.wait_ge(e["meant"], h + 1)
                    act.activation(halves(orstd[:]), ps[:, 4:6, 0:HALF], ACT.Ln, bias=k.eps[:, 0:1]).then_inc(e["rlog"], 1)
                    act.wait_ge(e["rlog"], h + 1)
                    act.activation(orstd[:], orstd[:], ACT.Exp, scale=-0.5).then_inc(e["rstd"], 1)
                    act.wait_ge(e["gated"], h + 1)
                    act.activation(k.xh[:].rearrange("p k n -> p (k n)")[:, bass.ds(h * T, T)], y[:], ACT.Copy
                                   ).then_inc(e["ohigh"], 1)

            @block.gpsimd
            def _(pool):
                with pool.Fori(0, H) as h:
                    pool.wait_ge(e["sigmoids"], h + 1)
                    for c in range(TILES):
                        t0, n, levels, x = dims(c)
                        m = 5 * h + c + 1
                        pool.wait_ge(e["decayed"], m)
                        pool.wait_ge(e["floored"], h + 1)
                        for l in range(levels):
                            b = 1 << l
                            xv = x[:, l, :].rearrange("p (a r b) -> p a r b", r=2, b=b)[:, :, 0, :]
                            kv = kk[:, t0:t0 + n].rearrange("p (a r b) -> p a r b", r=2, b=b)[:, :, 0, :]
                            pool.tensor_tensor(xv, xv, kv, ALU.mult)
                        pool.tensor_tensor(x[:, levels + 1, :], x[:, levels + 1, :], kk[:, t0:t0 + n], ALU.mult
                                           ).then_inc(e["keys"], 1)
                        if c == 4:
                            pool.wait_ge(e["valued"], m)
                            pool.tensor_tensor(vm[:], vt[0:NS, :].unsqueeze(1).broadcast_to([NS, NB, P]),
                                               k.batch[:].rearrange("p (b v) -> p b v", b=NB), ALU.mult
                                               ).then_inc(e["vmasked"], 1)

            @block.tensor
            def _(pe):
                with pe.Fori(0, H) as h:
                    pe.wait_ge(e["logf"], h + 1)
                    for c in range(TILES):
                        t0, n, levels, x = dims(c)
                        m = 5 * h + c + 1
                        decay, width = (k.decay, LEVELS + 2) if c < 4 else (k.sdecay, SLEVELS + 2)
                        pe.transpose(ps[:, 0, 0:P], lf[:, t0:t0 + P], k.ident[:])
                        pe.transpose(ps[:, 0, P:2 * P], z[:].rearrange("p j n -> p (j n)")[:, 2 * T + t0:2 * T + t0 + P], k.ident[:]).then_inc(e["turned"], 1)
                        pe.wait_ge(e["low"], m)
                        for g in range(3 if c < 4 else 1):
                            cols = slice(g * 3 * P, (g + 1) * 3 * P) if c < 4 else slice(0, width * NS)
                            w = cols.stop - cols.start
                            pe.matmul(ps[:, 1 + g, 0:w], lth[0:n, :], decay[0:n, cols], start=True, stop=False)
                            mm = pe.matmul(ps[:, 1 + g, 0:w], ltl[0:n, :], decay[0:n, cols], start=False, stop=True)
                        mm.then_inc(e["summed"], 1)
                        pe.wait_ge(e["keys"], m)
                        pe.wait_ge(e["queries"], m)
                        pe.wait_ge(e["valued"], m)
                        pe.transpose(ps[:, 0, 2 * P:3 * P], x[:].rearrange("p l n -> p (l n)")[:, (levels + 1) * n:(levels + 1) * n + P], k.ident[:]).then_inc(e["keyed"], 1)
                        for l in range(levels):
                            pe.matmul(ps[0:n, 4 + l // 4, (l % 4) * n:(l % 4 + 1) * n], x[:, l, :], x[:, l, :],
                                      start=True, stop=True)
                        pe.matmul(ps[0:n, 4 + levels // 4, 3 * n:4 * n], kk[:, t0:t0 + n], z[:, 0, t0:t0 + n],
                                  start=True, stop=True).then_inc(e["scored"], 1)
                        pe.wait_ge(e["attended"], m)
                        pe.wait_ge(e["keyrows"], m)
                        if c < 4:
                            pe.matmul(ps[:, 6, 0:P], vt[:], att[:], start=True, stop=c == 0)
                            if c > 0:
                                pe.wait_ge(e["state"], m - 1)
                                mm = pe.matmul(ps[:, 6, 0:P], S[:], x[:, levels, :], start=False, stop=True)
                            else:
                                mm = None
                            pe.matmul(ps[:, 7, 0:P], kt[:], vt[:], start=True, stop=True).then_inc(e["read"], 1)
                        else:
                            pe.matmul(ps[:, 6, 0:NS], vt[0:NS, :], satt[:], start=True, stop=True)
                            for b in range(NB):
                                pe.matmul(ps[:, 6, b * NQ:(b + 1) * NQ], s0[:, b, :], x[:, levels, b * NQ:(b + 1) * NQ],
                                          start=False, stop=True, skip_group_check=True)
                            pe.wait_ge(e["vmasked"], h + 1)
                            for g in range(2):
                                mm = pe.matmul(ps[:, 1 + g, :], kt[0:NS, :], vm[:, 4 * g:4 * g + 4, :].rearrange(
                                    "p b v -> p (b v)"), start=True, stop=True)
                            mm.then_inc(e["read"], 1)
                        pe.wait_ge(e["state"], m)
                    pe.wait_ge(e["squared"], h + 1)
                    for a in range(2):
                        mm = pe.matmul(ps[:, 4 + a, 0:HALF], k.mean[:], osq[:, a * HALF:(a + 1) * HALF], start=True, stop=True)
                    mm.then_inc(e["meant"], 1)

            @block.vector
            def _(dve):
                dve.memset(lf[:, T:T + NS], 0.0)
                dve.memset(sx[:, SLEVELS + 2, :], 0.0)
                with dve.Fori(0, H) as h:
                    dve.wait_ge(e["sigmoids"], h + 1)
                    dve.tensor_scalar(kk[:], kk[:], lb[:, 1:2], None, ALU.mult)
                    dve.tensor_scalar(f[:], f[:], lb[:, 1:2], lb[:, 0:1], ALU.mult, ALU.add).then_inc(e["floored"], 1)
                    dve.wait_ge(e["floored"], h + 1)
                    dve.tensor_scalar(f[:], f[:], MIN_F, None, ALU.max).then_inc(e["gained"], 1)
                    dve.wait_ge(e["gained"], 7 * h + 1)
                    dve.tensor_scalar(tiny[:], f[:], 2.0 ** -30, 2.0 ** LN_LIFT - 1.0, ALU.is_lt, ALU.mult).then_inc(e["gained"], 1)
                    dve.wait_ge(e["gained"], 7 * h + 2)
                    dve.scalar_tensor_tensor(f[:], tiny[:], 1.0, f[:], ALU.add, ALU.mult).then_inc(e["lifted"], 1)
                    dve.wait_ge(e["logged"], h + 1)
                    dve.scalar_tensor_tensor(lf[:, 0:T], tiny[:], -LN_LIFT * float(np.log(2.0)) / (2.0 ** LN_LIFT - 1.0), lf[:, 0:T],
                                             ALU.mult, ALU.add).then_inc(e["logf"], 1)
                    for c in range(TILES):
                        t0, n, levels, x = dims(c)
                        m = 5 * h + c + 1
                        a = att if c < 4 else satt
                        masks = (k.split if c < 4 else k.ssplit)[:].rearrange("p (l n) -> p l n", n=n)
                        dve.wait_ge(e["high"], m)
                        dve.tensor_tensor(ltl[0:n, :], ps[0:n, 0, 0:P], lth[0:n, :].bitcast(F32), ALU.subtract
                                          ).then_inc(e["low"], 1)
                        dve.tensor_copy(vt[0:n, :], ps[0:n, 0, P:2 * P]).then_inc(e["valued"], 1)
                        dve.wait_ge(e["decayed"], m)
                        for l in range(levels):
                            b = 1 << l
                            xv = x[:, l, :].rearrange("p (a r b) -> p a r b", r=2, b=b)[:, :, 1, :]
                            qv = z[:, 0, t0:t0 + n].rearrange("p (a r b) -> p a r b", r=2, b=b)[:, :, 1, :]
                            dve.tensor_tensor(xv, xv, qv, ALU.mult)
                        if c < 4:
                            dve.tensor_copy(k.dlast[:, 0:1], x[:, levels, n - 1:n]).then_inc(e["gained"], 1)
                        else:
                            dve.tensor_copy(k.dlast[:, 0:NB], x[:, levels, NQ - 1:n:NQ]).then_inc(e["gained"], 1)
                        dve.wait_ge(e["gained"], 7 * h + 3 + c)
                        dve.tensor_tensor(x[:, levels, :], x[:, levels, :], z[:, 0, t0:t0 + n], ALU.mult
                                          ).then_inc(e["queries"], 1)
                        dve.wait_ge(e["scored"], m)
                        w = levels + 1
                        pairs = picked[0:n, 0:w * n].rearrange("p (l n) -> p l n", l=w)
                        if c < 4:
                            scores = ps[:, 4:6, :].rearrange("p a n -> p (a n)").rearrange("p (l n) -> p l n", l=w)
                        else:
                            scores = ps[0:n, 4, 0:w * n].rearrange("p (l n) -> p l n", l=w)
                        dve.tensor_tensor(pairs, scores, masks, ALU.mult).then_inc(e["picked"], 1)
                        dve.wait_ge(e["picked"], m)
                        dve.tensor_reduce(a[:], pairs.rearrange("p l n -> p n l"), AX.X, ALU.add).then_inc(e["attended"], 1)
                        dve.wait_ge(e["read"], m)
                        dve.tensor_copy(o[:, t0:t0 + n], ps[:, 6, 0:n]).then_inc(e["copied"], 1)
                        if c == 0:
                            dve.wait_ge(e["free"], h + 1)
                            dve.tensor_copy(S[:], ps[:, 7, 0:P]).then_inc(e["state"], 1)
                            dve.wait_ge(e["state"], m)
                        elif c < 4:
                            dve.scalar_tensor_tensor(S[:], S[:], k.dlast[:, 0:1], ps[:, 7, 0:P], ALU.mult, ALU.add
                                                     ).then_inc(e["state"], 1)
                            dve.wait_ge(e["state"], m)
                        else:
                            for b in range(NB):
                                ins = dve.scalar_tensor_tensor(
                                    snew[:, b, :], s0[:, b, :], k.dlast[:, b:b + 1],
                                    ps[:, 1 + b // 4, (b % 4) * P:(b % 4 + 1) * P], ALU.mult, ALU.add)
                            ins.then_inc(e["state"], 1)
                    dve.wait_ge(e["rstd"], h + 1)
                    dve.scalar_tensor_tensor(y[:], o[:], k.onorm[:, 0:1], orstd[:], ALU.mult, ALU.mult).then_inc(e["stored_y"], 1)
                    dve.wait_ge(e["stored_y"], h + 1)
                    dve.tensor_tensor(y[:], y[:], gt[:], ALU.mult).then_inc(e["gated"], 1)
                    dve.wait_ge(e["ohigh"], h + 1)
                    dve.tensor_tensor(k.xl[:].rearrange("p k n -> p (k n)")[:, bass.ds(h * T, T)], y[:],
                                      k.xh[:].rearrange("p k n -> p (k n)")[:, bass.ds(h * T, T)].bitcast(F32),
                                      ALU.subtract).then_inc(e["olow"], 1)


def lower_bound(k):
    nc = k.nc
    top, ex, tot, done, scaled = (k.sem("lb_" + n) for n in ("top", "exp", "total", "done", "scaled"))
    with ExitStack() as st:
        d, p, r, q = (k.sb(st, "lb_" + n, [P, KD]) for n in ("d", "p", "r", "q"))
        with nc.Block() as block:
            @block.vector
            def _(dve):
                dve.tensor_scalar(k.qn8[:], k.qn[:], DH ** -0.5, None, ALU.mult).then_inc(scaled, 1)
                dve.tensor_tensor(d[:], k.a_lb[:], k.a_lb[:], ALU.subtract).then_inc(top, 1)
                dve.wait_ge(ex, 1)
                dve.reciprocal(r[:], p[:]).then_inc(tot, 1)
                dve.wait_ge(tot, 1)
                dve.tensor_tensor(q[:], p[:], r[:], ALU.mult).then_inc(tot, 1)
                dve.wait_ge(tot, 2)
                dve.tensor_tensor(k.lb[:, :, 0], q[:], q[:], ALU.subtract).then_inc(tot, 1)
                dve.wait_ge(tot, 3)
                dve.tensor_scalar(k.lb[:, :, 1], k.lb[:, :, 0], -1.0, 1.0, ALU.mult, ALU.add).then_inc(done, 1)

            @block.scalar
            def _(act):
                act.wait_ge(top, 1)
                act.activation(p[:], d[:], ACT.Exp).then_inc(ex, 1)


def forget_values(k, xh, xl):
    nc, ps = k.nc, k.ps
    e = {n: k.sem("fv_" + n) for n in ("loaded", "high", "low", "summed", "z", "abs", "exp", "ln", "logf", "turned", "rows",
                                       "stored", "cum", "c", "cstored")}
    with ExitStack() as tmp:
        lfrows = k.sb(tmp, "lf_rows", [P, 5, BH])
        w = k.sb(tmp, "fv_w", [P, KD, BH])
        wh, wl = (k.sb(tmp, n, [P, KD, BH], F32R) for n in ("fv_wh", "fv_wl"))
        bf = k.sb(tmp, "fv_bf", [BH, 1])
        tri, ones = k.sb(tmp, "fv_tri", [P, P]), k.sb(tmp, "fv_ones", [P, P])
        z, ab, lf = (k.sb(tmp, n, [BH, T]) for n in ("fv_z", "fv_ab", "fv_lf"))
        c2 = k.sb(tmp, "fv_c", [BH, 2, SEQ])
        with nc.Block() as block:
            @block.sync
            def _(sp):
                sp.dma_start(w[:], k.w["w_kvf"].rearrange("(k p) n -> p k n", p=P)[:, :, 2 * D:2 * D + BH]).then_inc(e["loaded"], 16)
                sp.dma_start(bf[:], k.w["b_f"].rearrange("(p o) -> p o", o=1), allow_slow_non_contiguous=True).then_inc(e["loaded"], 16)
                sp.dma_start(tri[:], k.w["c_tri"]).then_inc(e["loaded"], 16)
                sp.wait_ge(e["rows"], 1)
                sp.dma_start(k.out["logf_prompt"].rearrange("b (c p) h -> p (b c) h", p=P), lfrows[:, 0:4, :]).then_inc(e["stored"], 16)
                sp.dma_start(k.out["logf_sample"].rearrange("b q h -> (b q) h"), lfrows[0:NS, 4, :]).then_inc(e["stored"], 16)
                sp.wait_ge(e["c"], 2)
                sp.dma_start(k.cum_prompt.rearrange("s h n -> h s n"), c2[:]).then_inc(e["cstored"], 16)
                sp.wait_ge(e["stored"], 32)
                sp.wait_ge(e["cstored"], 16)

            @block.scalar
            def _(act):
                act.wait_ge(e["loaded"], 48)
                act.activation(wh[:], w[:], ACT.Copy).then_inc(e["high"], 1)
                act.wait_ge(e["summed"], 1)
                act.activation(halves(z[:]), ps[0:BH, 0:2, 0:HALF], ACT.Identity, bias=bf[:, 0:1]).then_inc(e["z"], 1)
                act.wait_ge(e["z"], 1)
                act.activation(ab[:], z[:], ACT.Abs).then_inc(e["abs"], 1)
                act.wait_ge(e["abs"], 1)
                act.activation(ab[:], ab[:], ACT.Exp, scale=-1.0).then_inc(e["exp"], 1)
                act.wait_ge(e["exp"], 1)
                act.activation(ab[:], ab[:], ACT.Ln, bias=1.0).then_inc(e["ln"], 1)
                act.wait_ge(e["cum"], 1)
                act.activation(c2[:, 0, :], ps[0:BH, 3, :], ACT.Copy).then_inc(e["c"], 1)
                act.activation(c2[:, 1, :], ps[0:BH, 3, :], ACT.Copy, scale=-1.0).then_inc(e["c"], 1)

            @block.vector
            def _(dve):
                dve.memset(ones[:], 1.0)
                dve.wait_ge(e["high"], 1)
                dve.tensor_tensor(wl[:], w[:], wh[:].bitcast(F32), ALU.subtract).then_inc(e["low"], 1)
                dve.wait_ge(e["ln"], 1)
                dve.scalar_tensor_tensor(lf[:], z[:], 0.0, ab[:], ALU.min, ALU.subtract).then_inc(e["logf"], 1)
                dve.wait_ge(e["turned"], 1)
                dve.tensor_copy(lfrows[:, 0:4, :], ps[:, 2, 0:4 * BH].rearrange("p (c h) -> p c h", c=4))
                dve.tensor_copy(lfrows[0:NS, 4, :], ps[0:NS, 2, 4 * BH:5 * BH]).then_inc(e["rows"], 1)

            @block.tensor
            def _(pe):
                pe.wait_ge(e["low"], 1)
                for t in range(KD):
                    for n, (wt, at) in enumerate(((wh, xh), (wh, xl), (wl, xh))):
                        for a in range(2):
                            mm = pe.matmul(ps[0:BH, a, 0:HALF], wt[:, t, :], at[:, t, a * HALF:(a + 1) * HALF],
                                           start=t == 0 and n == 0, stop=t == KD - 1 and n == 2)
                mm.then_inc(e["summed"], 1)
                pe.wait_ge(e["logf"], 1)
                for c in range(5):
                    n = P if c < 4 else NS
                    mm = pe.transpose(ps[0:n, 2, c * BH:(c + 1) * BH], lf[:, c * P:c * P + n], k.ident[0:BH, 0:BH])
                mm.then_inc(e["turned"], 1)
                pe.wait_ge(e["rows"], 1)
                for c in range(4):
                    for i in range(c + 1):
                        mm = pe.matmul(ps[0:BH, 3, c * P:(c + 1) * P], lfrows[:, i, :], (tri if i == c else ones)[:],
                                       start=i == 0, stop=i == c)
                mm.then_inc(e["cum"], 1)


def head_rows(k, name, flat, first, gain=None, rows=None):
    nc, ps = k.nc, k.ps
    e = {n: k.sem(name + "_" + n) for n in ("squared", "summed", "logged", "rstd", "y", "kept", "turned", "rows")}
    with ExitStack() as tmp:
        sq, rstd, y = (k.sb(tmp, name + n, [P, T]) for n in ("_sq", "_rstd", "_y"))
        tile = lambda j: flat[:, bass.ds((j + first) * T, T)]
        with nc.Block() as block:
            @block.scalar
            def _(act):
                with act.Fori(0, KD) as j:
                    if gain is not None:
                        act.activation(sq[:], tile(j), ACT.Square).then_inc(e["squared"], 1)
                        act.wait_ge(e["summed"], j + 1)
                        act.activation(halves(rstd[:]), ps[:, 0:2, 0:HALF], ACT.Ln, bias=k.eps[:, 0:1]).then_inc(e["logged"], 1)
                        act.wait_ge(e["logged"], j + 1)
                        act.activation(rstd[:], rstd[:], ACT.Exp, scale=-0.5).then_inc(e["rstd"], 1)
                        act.wait_ge(e["y"], j + 1)
                    if rows is not None:
                        act.wait_ge(e["turned"], j + 1)
                        act.activation(rows[:, 0:4, bass.ds(j * P, P)], ps[:, 4, :].rearrange("p (c n) -> p c n", c=4), ACT.Copy)
                        act.activation(rows[0:NS, 4, bass.ds(j * P, P)], ps[0:NS, 5, 0:P], ACT.Copy).then_inc(e["rows"], 1)

            @block.vector
            def _(dve):
                if rows is not None:
                    dve.sem_inc(e["rows"], 1)
                if gain is not None:
                    dve.sem_inc(e["kept"], 1)
                with dve.Fori(0, KD) as j:
                    if rows is not None:
                        dve.wait_ge(e["rows"], j + 1)
                    if gain is not None:
                        dve.wait_ge(e["kept"], j + 1)
                        dve.wait_ge(e["rstd"], j + 1)
                        dve.scalar_tensor_tensor(y[:], tile(j), gain, rstd[:], ALU.mult, ALU.mult).then_inc(e["y"], 1)
                    else:
                        dve.tensor_copy(y[:], tile(j)).then_inc(e["y"], 1)

            @block.gpsimd
            def _(pool):
                if gain is not None:
                    with pool.Fori(0, KD) as j:
                        pool.wait_ge(e["y"], j + 1)
                        pool.tensor_copy(tile(j), y[:]).then_inc(e["kept"], 1)

            @block.tensor
            def _(pe):
                with pe.Fori(0, KD) as j:
                    if gain is not None:
                        pe.wait_ge(e["squared"], j + 1)
                        for a in range(2):
                            mm = pe.matmul(ps[:, a, 0:HALF], k.headmean[:], sq[:, a * HALF:(a + 1) * HALF], start=True, stop=True)
                        mm.then_inc(e["summed"], 1)
                    if rows is not None:
                        pe.wait_ge(e["y"], j + 1)
                        pe.wait_ge(e["rows"], j + 1)
                        for c in range(4):
                            pe.transpose(ps[:, 4, c * P:(c + 1) * P], y[:, c * P:(c + 1) * P], k.ident[:])
                        pe.transpose(ps[0:NS, 5, 0:P], y[:, SEQ:T], k.ident[:]).then_inc(e["turned"], 1)


def prompt_attention(k, kf, qf, vrows, oT):
    nc, ps = k.nc, k.ps
    e = {n: k.sem("pa_" + n) for n in ("const", "staged", "scored", "max", "exp", "inv", "scaled", "turned", "rows", "mixed", "done")}
    U = 8
    with ExitStack() as st:
        kj, qj, vj = k.sb(st, "pa_k", [P, SEQ]), k.sb(st, "pa_q", [P, SEQ]), k.sb(st, "pa_v", [P, 4, P])
        bl, br = k.sb(st, "pa_bl", [2, 2, SEQ]), k.sb(st, "pa_br", [2, 2, SEQ])
        causal = k.sb(st, "pa_causal", [P, P])
        nm, tot, inv = (k.sb(st, n, [P, 2]) for n in ("pa_nm", "pa_tot", "pa_inv"))
        pr, pt = k.sb(st, "pa_pr", [P, 2, SEQ]), k.sb(st, "pa_pt", [P, 2, SEQ])

        with nc.Block() as block:
            @block.sync
            def _(sp):
                sp.dma_start(causal[:], k.w["c_causal"]).then_inc(e["const"], 16)
                for a in range(2):
                    sp.dma_start(bl[0:1, a, :], k.w["c_ones"][0:1, 0:SEQ]).then_inc(e["const"], 16)
                    sp.dma_start(br[1:2, a, :], k.w["c_ones"][0:1, 0:SEQ]).then_inc(e["const"], 16)
                sp.sem_inc(e["done"], 1)
                with sp.Fori(0, KD) as j:
                    sp.wait_ge(e["done"], j + 1)
                    sp.dma_start(kj[:], kf[:, bass.ds(j * T, SEQ)]).then_inc(e["staged"], 16)
                    sp.dma_start(qj[:], qf[:, bass.ds(j * T, SEQ)]).then_inc(e["staged"], 16)
                    sp.dma_start(vj[:], vrows[:, 0:4, bass.ds(j * P, P)]).then_inc(e["staged"], 16)
                    sp.dma_start(bl[1:2, :, :], k.cum_prompt[0][bass.ds(2 * j, 2)].unsqueeze(0)).then_inc(e["staged"], 16)
                    sp.dma_start(br[0:1, :, :], k.cum_prompt[1][bass.ds(2 * j, 2)].unsqueeze(0)).then_inc(e["staged"], 16)

            @block.tensor
            def _(pe):
                def score(j, u):
                    a, i = divmod(u, 4)
                    n = (i + 1) * P
                    if u >= 2:
                        pe.wait_ge(e["exp"], U * j + u - 1)
                    r = slice(DH * a, DH * (a + 1))
                    out = ps[:, u % 2, 0:n]
                    pe.matmul(out, qj[r, i * P:(i + 1) * P], kj[r, 0:n], start=True, stop=False)
                    pe.matmul(ps[:, u % 2, i * P:n], k.ident[:], causal[:], start=False, stop=False)
                    pe.matmul(out, bl[:, a, i * P:(i + 1) * P], br[:, a, 0:n], start=False, stop=True
                              ).then_inc(e["scored"], 1)

                def turn(j, u):
                    pe.wait_ge(e["scaled"], U * j + u + 1)
                    if u >= 2:
                        pe.wait_ge(e["rows"], U * j + u - 1)
                    for c in range(u % 4 + 1):
                        mm = pe.transpose(ps[:, 2 + u % 2, c * P:(c + 1) * P], pr[:, u % 2, c * P:(c + 1) * P], k.ident[:])
                    mm.then_inc(e["turned"], 1)

                def mix(j, u):
                    a, i = divmod(u, 4)
                    pe.wait_ge(e["rows"], U * j + u + 1)
                    for c in range(i + 1):
                        mm = pe.matmul(ps[DH * a:DH * (a + 1), 4, i * P:(i + 1) * P], vj[:, c, DH * a:DH * (a + 1)],
                                       pt[:, u % 2, c * P:(c + 1) * P], start=c == 0, stop=c == i)
                    mm.then_inc(e["mixed"], 1)

                pe.wait_ge(e["const"], 80)
                with pe.Fori(0, KD) as j:
                    pe.wait_ge(e["staged"], 80 * j + 80)
                    pe.wait_ge(e["done"], j + 1)
                    for u in range(U + 2):
                        if u < U:
                            score(j, u)
                        if 1 <= u <= U:
                            turn(j, u - 1)
                        if u >= 2:
                            mix(j, u - 2)

            @block.scalar
            def _(act):
                with act.Fori(0, KD) as j:
                    for u in range(U):
                        n = (u % 4 + 1) * P
                        act.wait_ge(e["max"], U * j + u + 1)
                        if u >= 2:
                            act.wait_ge(e["turned"], U * j + u - 1)
                        act.activation(pr[:, u % 2, 0:n], ps[:, u % 2, 0:n], ACT.Exp, bias=nm[:, u % 2:u % 2 + 1],
                                       accum_out=tot[:, u % 2:u % 2 + 1]).then_inc(e["exp"], 1)

            @block.vector
            def _(dve):
                def rows(j, u):
                    n = (u % 4 + 1) * P
                    dve.wait_ge(e["turned"], U * j + u + 1)
                    if u >= 2:
                        dve.wait_ge(e["mixed"], U * j + u - 1)
                    dve.tensor_copy(pt[:, u % 2, 0:n], ps[:, 2 + u % 2, 0:n]).then_inc(e["rows"], 1)

                with dve.Fori(0, KD) as j:
                    for u in range(U):
                        n = (u % 4 + 1) * P
                        s = slice(u % 2, u % 2 + 1)
                        dve.wait_ge(e["scored"], U * j + u + 1)
                        if u >= 2:
                            dve.wait_ge(e["exp"], U * j + u - 1)
                        dve.tensor_reduce(nm[:, s], ps[:, u % 2, 0:n], AX.X, ALU.max, negate=True).then_inc(e["max"], 1)
                        if u >= 1:
                            rows(j, u - 1)
                        dve.wait_ge(e["exp"], U * j + u + 1)
                        dve.reciprocal(inv[:, s], tot[:, s]).then_inc(e["inv"], 1)
                        dve.wait_ge(e["inv"], U * j + u + 1)
                        dve.tensor_scalar(pr[:, u % 2, 0:n], pr[:, u % 2, 0:n], inv[:, s], None, ALU.mult).then_inc(e["scaled"], 1)
                    rows(j, U - 1)
                    dve.wait_ge(e["mixed"], U * j + U)
                    dve.tensor_copy(oT[:, bass.ds(j * T, SEQ)], ps[:, 4, :]).then_inc(e["done"], 1)


def past_decay(k):
    nc, ps = k.nc, k.ps
    e = {n: k.sem("pd_" + n) for n in ("pages", "gathered", "summed", "off", "neg", "new", "stored")}
    with ExitStack() as st:
        pages = k.sb(st, "pd_pages", [1, NB * PAGES], I32)
        lf = k.sb(st, "pd_lf", [P, PAGES, NB * BH])
        lnew = k.sb(st, "pd_new", [P, NQ])
        tri = k.sb(st, "pd_tri", [P, P])
        off = k.sb(st, "pd_off", [P, PAGES + 1])
        cnew = k.sb(st, "pd_cnew", [P, NQ])
        neg = k.sb(st, "pd_neg", [P, PAST + NQ])
        with nc.Block() as block:
            @block.sync
            def _(sp):
                sp.dma_start(pages[:], k.w["page_table"].rearrange("b p -> (b p)").unsqueeze(0)).then_inc(e["pages"], 16)
                sp.dma_start(tri[:], k.w["c_tri"]).then_inc(e["gathered"], 16)
                for b in range(NB):
                    sp.dma_start(lnew[b * BH:(b + 1) * BH, :], k.out["logf_sample"][b].rearrange("q h -> h q"),
                                 allow_slow_non_contiguous=True).then_inc(e["gathered"], 16)
                sp.wait_ge(e["pages"], 16)
                with sp.Fori(0, NB) as b:
                    for p in range(PAGES):
                        page = sp.value_load(pages[0:1, bass.ds(b * PAGES + p, 1)], min_val=0, max_val=k.n_pool - 1)
                        sp.dma_start(lf[:, p, bass.ds(b * BH, BH)], k.w["cache_logf"][bass.ds(page, 1)]
                                     .rearrange("o t h -> t (o h)")).then_inc(e["gathered"], 16)
                sp.wait_ge(e["neg"], PAGES + 1)
                sp.wait_ge(e["new"], NQ)
                sp.dma_start(k.neg_decay, neg[:]).then_inc(e["stored"], 16)
                sp.dma_start(k.new_decay.rearrange("b (h q) -> (b h) q", h=BH), cnew[:]).then_inc(e["stored"], 16)
                sp.wait_ge(e["stored"], 32)

            @block.tensor
            def _(pe):
                pe.wait_ge(e["gathered"], 16 * (1 + NB + NB * PAGES))
                for p in range(PAGES):
                    mm = pe.matmul(ps[:, p // 4, (p % 4) * P:(p % 4 + 1) * P], lf[:, p, :], tri[:], start=True, stop=True)
                mm.then_inc(e["summed"], 1)

            @block.vector
            def _(dve):
                dve.memset(off[:, 0:1], 0.0).then_inc(e["off"], 1)
                dve.wait_ge(e["summed"], 1)
                for p in range(PAGES):
                    local = ps[:, p // 4, (p % 4) * P:(p % 4 + 1) * P]
                    dve.wait_ge(e["off"], p + 1)
                    dve.tensor_tensor(off[:, p + 1:p + 2], off[:, p:p + 1], local[:, P - 1:P], ALU.add).then_inc(e["off"], 1)
                    dve.tensor_scalar(neg[:, p * P:(p + 1) * P], local, off[:, p:p + 1], -1.0, ALU.add, ALU.mult).then_inc(e["neg"], 1)
                for q in range(NQ):
                    before = off[:, PAGES:PAGES + 1] if q == 0 else cnew[:, q - 1:q]
                    dve.wait_ge(e["off"], PAGES + 1)
                    if q > 0:
                        dve.wait_ge(e["new"], q)
                    dve.tensor_tensor(cnew[:, q:q + 1], before, lnew[:, q:q + 1], ALU.add).then_inc(e["new"], 1)
                dve.wait_ge(e["new"], NQ)
                dve.tensor_scalar(neg[:, PAST:PAST + NQ], cnew[:], -1.0, None, ALU.mult).then_inc(e["neg"], 1)


def sample_attention(k, ks, qs, oT):
    nc, ps = k.nc, k.ps
    e = {n: k.sem("sa_" + n) for n in (
        "const", "zero", "staged", "pages", "q", "qh", "ql", "turned", "kh", "kl", "used", "scored", "mx", "max", "exp", "sum",
        "inv", "pturned", "ph", "pl", "tailt", "tail", "vh", "vl", "pv", "mixed", "om", "picked", "done")}
    kload = [k.sem(f"sa_kload{s}") for s in range(2)]
    vload = [k.sem(f"sa_vload{s}") for s in range(2)]
    G, J = 4, KD
    with ExitStack() as st:
        sb = lambda n, shape, dt=F32: k.sb(st, "sa_" + n, shape, dt)
        pages = sb("pages", [1, NB * PAGES], I32)
        kp, vp = sb("kp", [P, 2, 4, D]), sb("vp", [P, 2, 4, D])
        kh, kl = sb("kh", [P, 2, SEQ], F32R), sb("kl", [P, 2, SEQ], F32R)
        vh, vl = sb("vh", [P, 2, D], F32R), sb("vl", [P, 2, D], F32R)
        q0, qz = sb("q0", [P, J, NQ]), sb("qz", [P, J * P])
        qh, ql = sb("qh", [P, J, P], F32R), sb("ql", [P, J, P], F32R)
        kn, vn = sb("kn", [P, J, NQ]), sb("vn", [NQ, D])
        rowl, rowr = sb("rowl", [BH + 1, P]), sb("rowr", [BH + 1, PAST + NQ])
        scausal, pickq, rowhead = sb("scausal", [P, NQ]), sb("pickq", [P, NQ]), sb("rowhead", [P, D])
        mx, tot, nm, inv = sb("mx", [P, 2]), sb("tot", [P, 2]), sb("nm", [P, 1]), sb("inv", [P, 2])
        pr, ptail, ptt = sb("pr", [P, PAST]), sb("ptail", [P, NQ]), sb("ptt", [NQ, P])
        ph, pl = sb("ph", [P, PAGES, P], F32R), sb("pl", [P, PAGES, P], F32R)
        om = sb("om", [P, D])
        cache = {"k": k.w["cache_k"].rearrange("n t h d -> n t (h d)"), "v": k.w["cache_v"].rearrange("n t h d -> n t (h d)")}

        with nc.Block() as block:
            @block.sync
            def _(sp):
                sp.dma_start(pages[:], k.w["page_table"].rearrange("b p -> (b p)").unsqueeze(0)).then_inc(e["pages"], 16)
                for dst, src in ((rowl[0:BH, :], "c_headrow"), (scausal[:], "c_scausal"), (pickq[:], "c_pickq"),
                                 (rowhead[:], "c_rowhead")):
                    sp.dma_start(dst, k.w[src]).then_inc(e["const"], 16)
                sp.dma_start(rowr[BH:BH + 1, :], k.w["c_ones"]).then_inc(e["const"], 16)
                sp.wait_ge(e["pages"], 16)
                sp.sem_inc(e["done"], 1)
                sp.sem_inc(e["turned"], 2 * J)
                sp.sem_inc(e["vl"], 8)

                def load(b, g, which, ring, sems, free, value):
                    numbers = [sp.value_load(pages[0:1, bass.ds(b * PAGES + g * 4 + p, 1)], min_val=0, max_val=k.n_pool - 1)
                               for p in range(4)]
                    sp.wait_ge(free, value)
                    for p, page in enumerate(numbers):
                        sp.dma_start(ring[:, g % 2, p, :], cache[which][bass.ds(page, 1)].rearrange("o t n -> t (o n)")
                                     ).then_inc(sems[g % 2], 16)

                with sp.Fori(0, NB) as b:
                    for g in range(G):
                        load(b, g, "k", kp, kload, e["turned"], b * G * J + (g + 1) * J)
                        if g == 0:
                            sp.wait_ge(e["done"], b + 1)
                            sp.dma_start(rowr[0:BH, :], k.neg_decay[bass.ds(b * BH, BH), :]).then_inc(e["staged"], 16)
                            sp.dma_start(rowl[BH:BH + 1, :], k.new_decay[bass.ds(b, 1), :]).then_inc(e["staged"], 16)
                            sp.dma_start(q0[:], qs[:, :, bass.ds(b * NQ, NQ)]).then_inc(e["staged"], 16)
                            sp.dma_start(kn[:], ks[:, :, bass.ds(b * NQ, NQ)]).then_inc(e["staged"], 16)
                            sp.dma_start(vn[:], k.out["v_sample"].rearrange("b q h d -> b q (h d)")[bass.ds(b, 1)]
                                         .rearrange("b q n -> (b q) n")).then_inc(e["staged"], 16)
                    for g in range(G):
                        load(b, g, "v", vp, vload, e["vl"], b * PAGES + (g + 1) * 4)

            @block.tensor
            def _(pe):
                pe.wait_ge(e["const"], 80)

                def turn(b, i):
                    g, j = divmod(i, J)
                    if j == 0:
                        pe.wait_ge(kload[g % 2], (b * 2 + g // 2 + 1) * 64)
                    if i >= 2:
                        pe.wait_ge(e["kl"], b * G * J + i - 1)
                    for p in range(4):
                        mm = pe.transpose(ps[:, 4 + i % 2, p * P:(p + 1) * P], kp[:, g % 2, p, j * P:(j + 1) * P], k.ident[:])
                    mm.then_inc(e["turned"], 1)

                def score(b, i):
                    g, j = divmod(i, J)
                    pe.wait_ge(e["kl"], b * G * J + i + 1)
                    if j == 0:
                        pe.matmul(ps[:, g, :], rowl[:], rowr[:, g * SEQ:(g + 1) * SEQ], start=True, stop=False)
                    for n, (qt, kt) in enumerate(((qh, kh), (ql, kh), (qh, kl))):
                        mm = pe.matmul(ps[:, g, :], qt[:, j, :], kt[:, i % 2, :], start=False, stop=j == J - 1 and n == 2)
                    mm.then_inc(e["used"], 1)

                with pe.Fori(0, NB) as b:
                    pe.wait_ge(e["staged"], b * 80 + 80)
                    pe.wait_ge(e["ql"], b + 1)
                    for i in range(G * J + 1):
                        if i < G * J:
                            turn(b, i)
                        if i >= 1:
                            score(b, i - 1)
                    pe.matmul(ps[:, 6, 0:NQ], rowl[:], rowr[:, PAST:PAST + NQ], start=True, stop=False)
                    pe.matmul(ps[:, 6, 0:NQ], k.ident[:], scausal[:], start=False, stop=False)
                    for j in range(J):
                        mm = pe.matmul(ps[:, 6, 0:NQ], qz[:, j * P:(j + 1) * P], kn[:, j, :], start=False, stop=j == J - 1)
                    mm.then_inc(e["scored"], 1)
                    pe.wait_ge(e["exp"], b + 1)
                    for p in range(PAGES):
                        mm = pe.transpose(ps[:, p // 4, (p % 4) * P:(p % 4 + 1) * P], pr[:, p * P:(p + 1) * P], k.ident[:])
                        if p % 4 == 3:
                            mm.then_inc(e["pturned"], 1)
                    pe.transpose(ps[0:NQ, 4, 0:P], ptail[:], k.ident[:]).then_inc(e["tailt"], 1)
                    pe.wait_ge(e["tail"], b + 1)
                    for a in range(2):
                        mm = pe.matmul(ps[:, 6 + a, :], ptt[:], vn[:, a * SEQ:(a + 1) * SEQ], start=True, stop=False)
                    for p in range(PAGES):
                        pe.wait_ge(e["vl"], b * PAGES + p + 9)
                        if p % 4 == 0:
                            pe.wait_ge(e["pl"], b * 4 + p // 4 + 1)
                        for n, (pp, vv) in enumerate(((ph, vh), (pl, vh), (ph, vl))):
                            for a in range(2):
                                mm = pe.matmul(ps[:, 6 + a, :], pp[:, p, :], vv[:, p % 2, a * SEQ:(a + 1) * SEQ],
                                               start=False, stop=p == PAGES - 1 and n == 2)
                        mm.then_inc(e["pv"], 1)
                    pe.wait_ge(e["om"], b + 1)
                    for j in range(J):
                        mm = pe.matmul(ps[:, 5, j * NQ:(j + 1) * NQ], om[:, j * P:(j + 1) * P], pickq[:], start=True, stop=True)
                    mm.then_inc(e["picked"], 1)
                    pe.wait_ge(e["done"], b + 2)

            @block.scalar
            def _(act):
                with act.Fori(0, NB) as b:
                    act.wait_ge(e["q"], 2 * b + 2)
                    act.activation(qh[:].rearrange("p j n -> p (j n)"), qz[:], ACT.Copy).then_inc(e["qh"], 1)
                    for i in range(G * J):
                        act.wait_ge(e["turned"], b * G * J + 2 * J + i + 1)
                        if i >= 2:
                            act.wait_ge(e["used"], b * G * J + i - 1)
                        act.activation(kh[:, i % 2, :], ps[:, 4 + i % 2, :], ACT.Copy).then_inc(e["kh"], 1)
                    act.wait_ge(e["max"], b + 1)
                    act.activation(ptail[:], ps[:, 6, 0:NQ], ACT.Exp, bias=nm[:, 0:1], accum_out=tot[:, 1:2])
                    act.activation(pr[:], ps[:, 0:4, :].rearrange("p a n -> p (a n)"), ACT.Exp, bias=nm[:, 0:1],
                                   accum_out=tot[:, 0:1]).then_inc(e["exp"], 1)
                    for g in range(4):
                        act.wait_ge(e["pturned"], b * 4 + g + 1)
                        act.activation(ph[:, 4 * g:4 * g + 4, :].rearrange("p a n -> p (a n)"), ps[:, g, :], ACT.Copy
                                       ).then_inc(e["ph"], 1)
                    for p in range(PAGES):
                        g = p // 4
                        act.wait_ge(vload[g % 2], (b * 2 + g // 2 + 1) * 64)
                        if p >= 2:
                            act.wait_ge(e["pv"], b * PAGES + p - 1)
                        act.activation(vh[:, p % 2, :], vp[:, g % 2, p % 4, :], ACT.Copy).then_inc(e["vh"], 1)

            @block.vector
            def _(dve):
                dve.memset(qz[:], 0.0).then_inc(e["zero"], 1)
                dve.wait_ge(e["zero"], 1)
                with dve.Fori(0, NB) as b:
                    dve.wait_ge(e["staged"], b * 80 + 80)
                    for a in range(2):
                        r = slice(DH * a, DH * (a + 1))
                        dst = blocks(qz[r, :], J, 2 * NQ, a * NQ, NQ)
                        dve.tensor_copy(dst, q0[r, :, :]).then_inc(e["q"], 1)
                    dve.wait_ge(e["qh"], b + 1)
                    dve.tensor_tensor(ql[:].rearrange("p j n -> p (j n)"), qz[:],
                                      qh[:].rearrange("p j n -> p (j n)").bitcast(F32), ALU.subtract).then_inc(e["ql"], 1)
                    for i in range(G * J):
                        dve.wait_ge(e["kh"], b * G * J + i + 1)
                        dve.tensor_tensor(kl[:, i % 2, :], ps[:, 4 + i % 2, :], kh[:, i % 2, :].bitcast(F32),
                                          ALU.subtract).then_inc(e["kl"], 1)
                    dve.wait_ge(e["scored"], b + 1)
                    dve.tensor_reduce(mx[:, 0:1], ps[:, 0:4, :].rearrange("p a n -> p (a n)"), AX.X, ALU.max)
                    dve.tensor_reduce(mx[:, 1:2], ps[:, 6, 0:NQ], AX.X, ALU.max).then_inc(e["mx"], 1)
                    dve.wait_ge(e["mx"], b + 1)
                    dve.tensor_reduce(nm[:], mx[:], AX.X, ALU.max, negate=True).then_inc(e["max"], 1)
                    dve.wait_ge(e["exp"], b + 1)
                    dve.tensor_tensor(inv[:, 0:1], tot[:, 0:1], tot[:, 1:2], ALU.add).then_inc(e["sum"], 1)
                    dve.wait_ge(e["sum"], b + 1)
                    dve.reciprocal(inv[:, 1:2], inv[:, 0:1]).then_inc(e["inv"], 1)
                    for g in range(4):
                        dve.wait_ge(e["ph"], b * 4 + g + 1)
                        dve.tensor_tensor(pl[:, 4 * g:4 * g + 4, :].rearrange("p a n -> p (a n)"), ps[:, g, :],
                                          ph[:, 4 * g:4 * g + 4, :].rearrange("p a n -> p (a n)").bitcast(F32),
                                          ALU.subtract).then_inc(e["pl"], 1)
                    dve.wait_ge(e["tailt"], b + 1)
                    dve.tensor_copy(ptt[:], ps[0:NQ, 4, 0:P]).then_inc(e["tail"], 1)
                    for p in range(PAGES):
                        dve.wait_ge(e["vh"], b * PAGES + p + 1)
                        dve.tensor_tensor(vl[:, p % 2, :], vp[:, (p // 4) % 2, p % 4, :], vh[:, p % 2, :].bitcast(F32),
                                          ALU.subtract).then_inc(e["vl"], 1)
                    dve.wait_ge(e["inv"], b + 1)
                    dve.wait_ge(e["pv"], b * PAGES + PAGES)
                    dve.scalar_tensor_tensor(om[:], ps[:, 6:8, :].rearrange("p a n -> p (a n)"), inv[:, 1:2], rowhead[:],
                                             ALU.mult, ALU.mult).then_inc(e["om"], 1)
                    dve.wait_ge(e["picked"], b + 1)
                    dve.tensor_copy(oT[:].rearrange("p (j n) -> p j n", j=J)[:, :, bass.ds(b * NQ + SEQ, NQ)],
                                    ps[:, 5, 0:J * NQ].rearrange("p (j n) -> p j n", j=J)).then_inc(e["done"], 1)


def blocks(ap, count, step, first, n):
    pattern = [list(ap.ap[0]), [P + step, count], [1, n]]
    return bass.AP(ap.tensor, ap.offset + first, pattern)


def split_rows(k, oT):
    high, low = k.sem("sr_high"), k.sem("sr_low")
    flat = [t[:].rearrange("p k n -> p (k n)") for t in (k.xh, k.xl)]
    with k.nc.Block() as block:
        @block.scalar
        def _(act):
            act.activation(flat[0], oT[:], ACT.Copy).then_inc(high, 1)

        @block.vector
        def _(dve):
            dve.wait_ge(high, 1)
            dve.tensor_tensor(flat[1], oT[:], flat[0].bitcast(F32), ALU.subtract).then_inc(low, 1)


def with_split(k, name):
    st = ExitStack()
    k.xh, k.xl = k.sb(st, name + "_xh", [P, KD, T], F32R), k.sb(st, name + "_xl", [P, KD, T], F32R)
    return st


def fox(k, gains):
    nc = k.nc
    with ExitStack() as so:
        oT = k.sb(so, "oT", [P, KD * T])
        ks, qs = k.sb(so, "k_new", [P, KD, NS]), k.sb(so, "q_new", [P, KD, NS])
        with ExitStack() as st:
            kv, q = k.sb(st, "kv", [P, 2 * KD * T]), k.sb(st, "qf", [P, KD * T])
            with with_split(k, "kvx"):
                norm(k, "kvn", gains["kv_norm"])
                dense(k, "kvf", k.w["w_kvf"], KD, 1, k.xh, k.xl, KD, lambda i, u: (i * 2 + u) * P, store_to(kv[:]))
                forget_values(k, k.xh, k.xl)
                norm(k, "bn", gains["b_norm"])
                dense(k, "wq", k.w["b_wq"][0], KD, 1, k.xh, k.xl, KD // 2, lambda i, u: (i * 2 + u) * P, store_to(q[:]))
            vrows = k.sb(st, "v_rows", [P, 5, D])
            head_rows(k, "vr", kv, KD, rows=vrows)
            store_rows(k, "v", vrows)
            with ExitStack() as kr:
                krows = k.sb(kr, "k_rows", [P, 5, D])
                head_rows(k, "kr", kv, 0, gain=k.kn[:, 0:1], rows=krows)
                store_rows(k, "k", krows)
            k.retire()
            head_rows(k, "qr", q, 0, gain=k.qn8[:, 0:1])
            prompt_attention(k, kv, q, vrows, oT)
            copied = k.sem("new_copied")
            with nc.Block() as block:
                @block.vector
                def _(dve):
                    dve.tensor_copy(ks[:], kv[:, 0:KD * T].rearrange("p (j n) -> p j n", j=KD)[:, :, SEQ:T]).then_inc(copied, 1)
                    dve.tensor_copy(qs[:], q[:].rearrange("p (j n) -> p j n", j=KD)[:, :, SEQ:T]).then_inc(copied, 1)
        past_decay(k)
        sample_attention(k, ks, qs, oT)
        k.retire()
        with with_split(k, "ox"):
            split_rows(k, oT)
            dense(k, "wo", k.w["b_wo"][0], KD, 1, k.xh, k.xl, KD // 2, lambda i, u: (i * 2 + u) * P, add_to_stream(k))


def store_rows(k, which, rows):
    done = k.sem(which + "_stored")
    with k.nc.Block() as block:
        @block.sync
        def _(sp):
            sp.dma_start(k.out[which + "_prompt"].rearrange("b (c p) h d -> p (b c) (h d)", p=P), rows[:, 0:4, :]).then_inc(done, 16)
            sp.dma_start(k.out[which + "_sample"].rearrange("b q h d -> (b q) (h d)"), rows[0:NS, 4, :]).then_inc(done, 16)
            sp.wait_ge(done, 32)


def store_y(k):
    nc = k.nc
    turned, copied, stored = (k.sem("y_" + n) for n in ("turned", "copied", "stored"))
    with ExitStack() as st:
        rows = k.sb(st, "y_rows", [P, 5, D])
        with nc.Block() as block:
            @block.tensor
            def _(pe):
                for f in range(KD):
                    b = 2 * (f % 2)
                    if f >= 2:
                        pe.wait_ge(copied, f - 1)
                    for c in range(4):
                        pe.transpose(k.ps[:, b, c * P:(c + 1) * P], k.xT[:, f, c * P:(c + 1) * P], k.ident[:])
                    pe.transpose(k.ps[0:NS, b + 1, 0:P], k.xT[:, f, SEQ:T], k.ident[:]).then_inc(turned, 1)

            @block.vector
            def _(dve):
                for f in range(KD):
                    b = 2 * (f % 2)
                    dve.wait_ge(turned, f + 1)
                    dve.tensor_copy(rows[:, 0:4, f * P:(f + 1) * P], k.ps[:, b, :].rearrange("p (c n) -> p c n", c=4))
                    dve.tensor_copy(rows[0:NS, 4, f * P:(f + 1) * P], k.ps[0:NS, b + 1, 0:P]).then_inc(copied, 1)

            @block.sync
            def _(sp):
                sp.wait_ge(copied, KD)
                sp.dma_start(k.out["y_prompt"].rearrange("b (c p) d -> p (b c) d", p=P), rows[:, 0:4, :]).then_inc(stored, 16)
                sp.dma_start(k.out["y_sample"].rearrange("b q d -> (b q) d"), rows[0:NS, 4, :]).then_inc(stored, 16)
                sp.wait_ge(stored, 32)


OUTS = [("y_prompt", (1, SEQ, D)), ("y_sample", (NB, NQ, D)), ("hgrn_prompt", (1, 1, H, P, P)),
        ("k_prompt", (1, SEQ, BH, DH)), ("v_prompt", (1, SEQ, BH, DH)), ("logf_prompt", (1, SEQ, BH)),
        ("hgrn_sample", (1, NB, H, P, P)), ("k_sample", (NB, NQ, BH, DH)), ("v_sample", (NB, NQ, BH, DH)),
        ("logf_sample", (NB, NQ, BH))]


def ffn(k, name, layer, gain):
    with ExitStack() as st:
        st.enter_context(with_split(k, name))
        norm(k, name + "n", gain)
        fh, fl = (k.sb(st, name + n, [P, KF, T], F32R) for n in ("_fh", "_fl"))
        dense(k, name + "gu", k.w["w_gate_up"][layer], KD, 1, k.xh, k.xl, KF, lambda i, u: i * P + u * FF, None,
              swiglu=(fh[:].rearrange("p k n -> p (k n)"), fl[:].rearrange("p k n -> p (k n)")))
        dense(k, name + "dn", k.w["w_down"][layer], KF // 2, 2, fh, fl, KD // 2, lambda i, u: (i * 2 + u) * P,
              add_to_stream(k))


def add_to_stream(k):
    flat = k.xT[:].rearrange("p k n -> p (k n)")

    def evacuate(dve, i, u, ps):
        x = halves(flat[:, bass.ds((i * 2 + u) * T, T)])
        return dve.tensor_tensor(x, x, ps, ALU.add)
    return evacuate


def store_to(flat, first=0):
    def evacuate(dve, i, u, ps):
        return dve.tensor_copy(halves(flat[:, bass.ds((i * 2 + u + first) * T, T)]), ps)
    return evacuate


def program(nc, a, outs, stop_after=99):
    with ExitStack() as stack:
        k = Core(nc, stack)
        k.w, k.out = a, outs
        k.x_prompt, k.x_sample, k.state_hgrn = a["x_prompt"], a["x_sample"], a["state_hgrn"]
        sb = lambda name, shape, dt=F32: k.sb(stack, name, shape, dt)
        k.ps = stack.enter_context(nc.psum_tensor("ps", [P, 8, 512], F32))
        k.xT = sb("xT", [P, KD, T])
        k.ident, k.mean, k.headmean = sb("ident", [P, P]), sb("mean", [P, P]), sb("headmean", [P, P])
        k.eps = sb("eps", [P, 1])
        k.lb, k.a_lb = sb("lb", [P, KD, 2]), sb("a_lbT", [P, KD])
        k.dlast = sb("dlast", [P, NB])
        k.n_pool = a["cache_k"].shape[0]
        k.cum_prompt = nc.dram_tensor("cum_prompt", [2, BH, SEQ], F32).ap()
        k.neg_decay = nc.dram_tensor("neg_decay", [NB * BH, PAST + NQ], F32).ap()
        k.new_decay = nc.dram_tensor("new_decay", [NB, BH * NQ], F32).ap()
        k.qn8 = sb("qn8", [P, 1])
        gains = {n: sb("g_" + n, [P, KD]) for n in ("a_norm", "kv_norm", "b_norm", "ffn0", "ffn1")}
        k.onorm, k.qn, k.kn = sb("onorm", [P, 1]), sb("qn", [P, 1]), sb("kn", [P, 1])
        k.const_loads = [(k.ident[:], a["c_ident"]), (k.mean[:], a["c_mean"]), (k.headmean[:], a["c_headmean"]),
                         (k.eps[:], a["c_eps"]),
                         (k.a_lb[:], a["a_lb"][0].rearrange("(k p) -> p k", p=P)),
                         (gains["a_norm"][:], a["a_norm"][0].rearrange("(k p) -> p k", p=P)),
                         (gains["kv_norm"][:], a["kv_norm"].rearrange("(k p) -> p k", p=P)),
                         (gains["b_norm"][:], a["b_norm"][0].rearrange("(k p) -> p k", p=P)),
                         (gains["ffn0"][:], a["ffn_norm"][0].rearrange("(k p) -> p k", p=P)),
                         (gains["ffn1"][:], a["ffn_norm"][1].rearrange("(k p) -> p k", p=P)),
                         (k.onorm[:], a["a_onorm"][0].rearrange("(p o) -> p o", o=1))]
        for half in range(2):
            k.const_loads += [(k.qn[half * DH:(half + 1) * DH, :], a["q_norm"][0].rearrange("(p o) -> p o", o=1)),
                              (k.kn[half * DH:(half + 1) * DH, :], a["k_norm"].rearrange("(p o) -> p o", o=1))]
        load_inputs(k)
        if stop_after < 1:
            return
        lower_bound(k)
        with with_split(k, "hx"), ExitStack() as hg:
            norm(k, "an", gains["a_norm"])
            k.z = k.sb(hg, "z", [P, 4 * H, T])
            if stop_after != 1.5:
                dense(k, "win", a["a_w_in"][0], KD, 1, k.xh, k.xl, 2 * H, lambda i, u: (i * 2 + u) * P,
                      store_to(k.z[:].rearrange("p k n -> p (k n)")))
            if stop_after < 2:
                return
            hgrn_constants(k, hg)
            hgrn(k)
            if stop_after < 3:
                return
            hg.close()
            dense(k, "wout", a["a_w_out"][0], KD, 1, k.xh, k.xl, KD // 2, lambda i, u: (i * 2 + u) * P, add_to_stream(k))
        k.retire()
        ffn(k, "f0", 0, gains["ffn0"])
        if stop_after < 4:
            return
        k.retire()
        fox(k, gains)
        ffn(k, "f1", 1, gains["ffn1"])
        store_y(k)


def hgrn_constants(k, st):
    nc = k.nc
    k.decay = k.sb(st, "decay", [P, (LEVELS + 2) * P], F32R)
    k.sdecay = k.sb(st, "sdecay", [NS, (SLEVELS + 2) * NS], F32R)
    k.split = k.sb(st, "split", [P, (LEVELS + 1) * P])
    k.ssplit = k.sb(st, "ssplit", [NS, (SLEVELS + 1) * NS])
    k.batch = k.sb(st, "batch", [NS, NB * P])
    got, done = k.sem("hc_loaded"), k.sem("hc_done")
    with ExitStack() as tmp:
        raw = k.sb(tmp, "decay_raw", [P, (LEVELS + 2) * P])
        sraw = k.sb(tmp, "sdecay_raw", [NS, (SLEVELS + 2) * NS])
        with nc.Block() as block:
            @block.sync
            def _(sp):
                for dst, src in ((raw, "c_decay"), (sraw, "c_sdecay"), (k.split, "c_split"), (k.ssplit, "c_ssplit"),
                                 (k.batch, "c_batch")):
                    sp.dma_start(dst[:], k.w[src]).then_inc(got, 16)
                sp.wait_ge(got, 80)

            @block.vector
            def _(dve):
                dve.wait_ge(got, 80)
                dve.tensor_copy(k.decay[:], raw[:]).then_inc(done, 1)
                dve.tensor_copy(k.sdecay[:], sraw[:]).then_inc(done, 1)


_INS = ["x_prompt", "x_sample", "state_hgrn", "cache_k", "cache_v", "cache_logf", "page_table", "a_norm", "a_w_in", "a_lb",
        "a_onorm", "a_w_out", "kv_norm", "w_kvf", "b_f", "k_norm", "b_norm", "b_wq", "q_norm", "b_wo", "ffn_norm",
        "w_gate_up", "w_down"]


def kernel(**inputs):
    from concourse import bacc
    from concourse.bass_utils import run_bass_kernel_spmd

    nc = bacc.Bacc("TRN2", target_bir_lowering=False, num_devices=1)
    arrays = {n: np.ascontiguousarray(inputs[n]) for n in _INS}
    arrays.update(shape_constants())
    arrays["c_eps"] = np.full((P, 1), EPS, np.float32)
    aps = {n: nc.dram_tensor("in_" + n, v.shape, mybir.dt.from_np(v.dtype), kind="ExternalInput").ap()
           for n, v in arrays.items()}
    outs = {n: nc.dram_tensor("out_" + n, s, F32, kind="ExternalOutput").ap() for n, s in OUTS}
    program(nc, aps, outs)
    r = run_bass_kernel_spmd(nc, [{"in_" + n: v for n, v in arrays.items()}], core_ids=[0])
    return tuple(r.results[0]["out_" + n] for n, _ in OUTS)
```

```python
from contextlib import ExitStack

import numpy as np

import concourse.bass as bass
from concourse import mybir

F32 = mybir.dt.float32
F32R = mybir.dt.float32r
I32 = mybir.dt.int32
ACT = mybir.ActivationFunctionType
ALU = mybir.AluOpType
AX = mybir.AxisListType

P = 128
D = 1024
KD = D // P
SEQ = 512
NB, NQ = 8, 8
NS = NB * NQ
T = SEQ + NS
HALF = T // 2
H = 8
BH, DH = 16, 64
FF = 2816
KF = FF // P
PAGES, PAGE = 16, 128
PAST = PAGES * PAGE
EPS = 1e-6
MIN_F = 1e-30
MASK = -1e30
LEVELS = 7
SLEVELS = 3
LN_LIFT = 50


def decay_sums(n, levels, chunk):
    i, t = np.arange(n)[:, None], np.arange(n)[None, :]
    out = []
    for l in range(levels):
        mid = ((t >> (l + 1)) << (l + 1)) + (1 << l)
        late = (t >> l) & 1
        out.append(np.where(late == 1, (i >= mid) & (i <= t), (i > t) & (i < mid)))
    same = i // chunk == t // chunk
    out.append(same & (i <= t))
    out.append(same & (i > t))
    return np.stack(out, axis=1).astype(np.float32)


def split_masks(n, levels):
    s, t = np.arange(n)[:, None], np.arange(n)[None, :]
    out = [(s >> (l + 1) == t >> (l + 1)) & ((s >> l) & 1 == 0) & ((t >> l) & 1 == 1) for l in range(levels)]
    out.append(s == t)
    return np.stack(out, axis=1).astype(np.float32)


def shape_constants():
    i = np.arange(P)
    hq = i[:, None]
    c = {
        "c_ident": np.eye(P),
        "c_ones": np.ones((1, PAST + NQ)),
        "c_mean": np.full((P, P), 1.0 / P),
        "c_headmean": (i[:, None] // DH == i[None, :] // DH) / DH,
        "c_decay": decay_sums(P, LEVELS, P).reshape(P, -1),
        "c_sdecay": decay_sums(NS, SLEVELS, NQ).reshape(NS, -1),
        "c_tri": (i[:, None] <= i[None, :]),
        "c_causal": np.where(i[None, :] <= i[:, None], 0.0, MASK),
        "c_scausal": np.where(np.arange(NQ)[None, :] <= hq % NQ, 0.0, MASK),
        "c_headrow": (np.arange(BH)[:, None] == i[None, :] // NQ),
        "c_pickq": (hq % NQ == np.arange(NQ)[None, :]),
        "c_rowhead": np.repeat(hq // NQ == np.arange(BH)[None, :], DH, axis=1),
        "c_batch": np.repeat(np.arange(NS)[:, None] // NQ == np.arange(NB)[None, :], P, axis=1),
        "c_newtri": ((i[:NS, None] // NQ == i[None, :NS] // NQ) & (i[:NS, None] <= i[None, :NS])),
    }
    c = {k: np.ascontiguousarray(v, dtype=np.float32) for k, v in c.items()}
    c["c_split"] = split_masks(P, LEVELS).reshape(P, -1)
    c["c_ssplit"] = split_masks(NS, SLEVELS).reshape(NS, -1)
    return c


class Core:

    def __init__(self, nc, stack):
        self.nc, self.stack, self.open = nc, stack, []

    def sb(self, stack, name, shape, dt=F32):
        return stack.enter_context(self.nc.sbuf_tensor(name, shape, dt))

    def sem(self, name):
        self.open.append(self.nc.alloc_semaphore(name=name))
        return self.open[-1]

    def retire(self):
        self.nc.clear_and_free_semaphores(self.open)
        self.nc.all_engine_barrier()
        self.open = []


def halves(ap):
    return ap.rearrange("p (a n) -> p a n", a=2)


def load_inputs(k):
    nc, x = k.nc, k.xT
    with ExitStack() as st:
        rows = k.sb(st, "x_rows", [P, 5, D])
        loaded, xrows, turned, stored = (k.sem(n) for n in ("consts_loaded", "x_loaded", "x_turned", "x_stored"))
        n_const = len(k.const_loads)
        with nc.Block() as block:
            @block.sync
            def _(sp):
                sp.dma_start(rows[:, 0:4, :], k.x_prompt.rearrange("b (c p) d -> p (b c) d", p=P)).then_inc(xrows, 16)
                sp.dma_start(rows[0:NS, 4, :], k.x_sample.rearrange("b q d -> (b q) d")).then_inc(xrows, 16)
                for dst, src in k.const_loads:
                    sp.dma_start(dst, src, allow_slow_non_contiguous=True).then_inc(loaded, 16)
                sp.wait_ge(loaded, 16 * n_const)

            @block.tensor
            def _(pe):
                pe.wait_ge(loaded, 16 * n_const)
                pe.wait_ge(xrows, 32)
                for f in range(KD):
                    if f >= 2:
                        pe.wait_ge(stored, f - 1)
                    for c in range(4):
                        nc.tensor.transpose(k.ps[:, 2 * (f % 2), c * P:(c + 1) * P], rows[:, c, f * P:(f + 1) * P], k.ident[:])
                    nc.tensor.transpose(k.ps[:, 2 * (f % 2) + 1, 0:NS], rows[0:NS, 4, f * P:(f + 1) * P],
                                        k.ident[0:NS, 0:NS]).then_inc(turned, 1)

            @block.vector
            def _(dve):
                for f in range(KD):
                    dve.wait_ge(turned, f + 1)
                    nc.vector.tensor_copy(x[:, f, 0:SEQ], k.ps[:, 2 * (f % 2), :])
                    nc.vector.tensor_copy(x[:, f, SEQ:T], k.ps[:, 2 * (f % 2) + 1, 0:NS]).then_inc(stored, 1)


def norm(k, name, gain):
    nc, x = k.nc, k.xT
    with ExitStack() as st:
        sq = k.sb(st, name + "_sq", [P, 2, T])
        rstd = k.sb(st, name + "_rstd", [P, T])
        y = k.sb(st, name + "_y", [P, 2, T])
        squared, summed, logged, scaled, normed, high, low = (
            k.sem(name + s) for s in ("_squared", "_summed", "_logged", "_scaled", "_normed", "_high", "_low"))
        with nc.Block() as block:
            @block.scalar
            def _(act):
                for f in range(KD):
                    if f >= 2:
                        act.wait_ge(summed, f - 1)
                    nc.scalar.activation(sq[:, f % 2, :], x[:, f, :], ACT.Square).then_inc(squared, 1)
                act.wait_ge(summed, KD)
                nc.scalar.activation(halves(rstd[:]), k.ps[:, 0:2, 0:HALF], ACT.Ln, scale=1.0 / KD,
                                     bias=k.eps[:, 0:1]).then_inc(logged, 1)
                act.wait_ge(logged, 1)
                nc.scalar.activation(rstd[:], rstd[:], ACT.Exp, scale=-0.5).then_inc(scaled, 1)
                for f in range(KD):
                    act.wait_ge(normed, f + 1)
                    nc.scalar.activation(k.xh[:, f, :], y[:, f % 2, :], ACT.Copy).then_inc(high, 1)

            @block.tensor
            def _(pe):
                for f in range(KD):
                    pe.wait_ge(squared, f + 1)
                    for a in range(2):
                        mm = nc.tensor.matmul(k.ps[:, a, 0:HALF], k.mean[:], sq[:, f % 2, a * HALF:(a + 1) * HALF],
                                              start=f == 0, stop=f == KD - 1)
                    mm.then_inc(summed, 1)

            @block.vector
            def _(dve):
                dve.wait_ge(scaled, 1)
                for f in range(KD):
                    if f >= 2:
                        dve.wait_ge(low, f - 1)
                    nc.vector.scalar_tensor_tensor(y[:, f % 2, :], x[:, f, :], gain[:, f:f + 1], rstd[:],
                                                   ALU.mult, ALU.mult).then_inc(normed, 1)
                    dve.wait_ge(high, f + 1)
                    nc.vector.tensor_tensor(k.xl[:, f, :], y[:, f % 2, :], k.xh[:, f, :].bitcast(F32),
                                            ALU.subtract).then_inc(low, 1)


def dense(k, name, weight, kt, chunks, ah, al, pairs, col_of, evacuate, swiglu=None):
    nc = k.nc
    w = weight.rearrange("(k p) n -> p k n", p=P)
    loaded = [k.sem(f"{name}_loaded{s}") for s in range(2)]
    free = [k.sem(f"{name}_free{u}") for u in range(2)]
    high, low, used, gated, mixed, parted = (
        k.sem(f"{name}_{s}") for s in ("high", "low", "used", "gated", "mixed", "parted"))
    units = 2 * chunks
    with ExitStack() as st:
        wraw = k.sb(st, name + "_wraw", [P, 2, kt, P])
        wh, wl = (k.sb(st, name + n, [P, 2, kt, P], F32R) for n in ("_wh", "_wl"))
        gate = k.sb(st, name + "_gate", [P, T]) if swiglu else None
        prod = k.sb(st, name + "_prod", [P, T]) if swiglu else None
        with nc.Block() as block:
            @block.sync
            def _(sp):
                sp.sem_inc(low, 2)
                with sp.Fori(0, pairs) as i:
                    for v in range(units):
                        u, c = divmod(v, chunks)
                        sp.wait_ge(low, i * units + v + 1)
                        sp.dma_start(wraw[:, v % 2, :, :], w[:, c * kt:(c + 1) * kt, bass.ds(col_of(i, u), P)]
                                     ).then_inc(loaded[v % 2], 16)

            @block.scalar
            def _(act):
                act.sem_inc(used, 2)
                if swiglu:
                    act.sem_inc(gated, 1)
                with act.Fori(0, pairs) as i:
                    for v in range(units):
                        act.wait_ge(loaded[v % 2], (i * (units // 2) + v // 2) * 16 + 16)
                        act.wait_ge(used, i * units + v + 1)
                        act.activation(wh[:, v % 2, :, :], wraw[:, v % 2, :, :], ACT.Copy).then_inc(high, 1)
                    if swiglu:
                        act.wait_ge(used, i * units + chunks + 2)
                        act.wait_ge(mixed, i + 1)
                        act.activation(halves(gate[:]), k.ps[:, 0:2, 0:HALF], ACT.Silu).then_inc(gated, 1)

            @block.gpsimd
            def _(pool):
                with pool.Fori(0, pairs) as i:
                    for v in range(units):
                        pool.wait_ge(high, i * units + v + 1)
                        pool.tensor_tensor(wl[:, v % 2, :, :], wraw[:, v % 2, :, :],
                                           wh[:, v % 2, :, :].bitcast(F32), ALU.subtract).then_inc(low, 1)

            @block.tensor
            def _(pe):
                with pe.Fori(0, pairs) as i:
                    for v in range(units):
                        u, c = divmod(v, chunks)
                        if c == 0 and swiglu:
                            pe.wait_ge(gated if u == 0 else mixed, i + 1)
                        elif c == 0:
                            pe.wait_ge(free[u], i + 1)
                        pe.wait_ge(low, i * units + v + 3)
                        for t in range(kt):
                            for n, (wt, at) in enumerate(((wh, ah), (wh, al), (wl, ah))):
                                for a in range(2):
                                    mm = pe.matmul(k.ps[:, 2 * u + a, 0:HALF], wt[:, v % 2, t, :],
                                                   at[:, c * kt + t, a * HALF:(a + 1) * HALF],
                                                   start=c == 0 and t == 0 and n == 0,
                                                   stop=c == chunks - 1 and t == kt - 1 and n == 2)
                        mm.then_inc(used, 1)

            @block.vector
            def _(dve):
                if swiglu:
                    dve.sem_inc(mixed, 1)
                else:
                    dve.sem_inc(free[0], 1)
                    dve.sem_inc(free[1], 1)
                with dve.Fori(0, pairs) as i:
                    if not swiglu:
                        for u in range(2):
                            dve.wait_ge(used, i * units + (u + 1) * chunks + 2)
                            evacuate(dve, i, u, k.ps[:, 2 * u:2 * u + 2, 0:HALF]).then_inc(free[u], 1)
                    else:
                        dh, dl = swiglu
                        dve.wait_ge(gated, i + 2)
                        dve.wait_ge(used, i * units + units + 2)
                        dve.tensor_tensor(halves(prod[:]), halves(gate[:]), k.ps[:, 2:4, 0:HALF],
                                          ALU.mult).then_inc(mixed, 1)
                        dve.wait_ge(mixed, i + 2)
                        dve.tensor_copy(dh[:, bass.ds(i * T, T)], prod[:]).then_inc(parted, 1)
                        dve.wait_ge(parted, i * 2 + 1)
                        dve.tensor_tensor(dl[:, bass.ds(i * T, T)], prod[:], dh[:, bass.ds(i * T, T)].bitcast(F32),
                                          ALU.subtract).then_inc(parted, 1)
                        dve.wait_ge(parted, i * 2 + 2)


def hgrn(k):
    nc, ps = k.nc, k.ps
    names = ("turned", "high", "low", "valued", "summed", "decayed", "queries", "keys", "last", "scored", "picked", "attended",
             "keyrows", "vmasked", "read", "copied", "state", "sigmoids", "scaled", "floored", "tiny", "lifted", "logged",
             "logf", "squared", "meant", "rlog", "rstd", "gate", "normed", "gated", "ohigh", "olow", "free", "stored", "zero",
             "staged0", "staged1", "pstored")
    e = {n: k.sem("hgrn_" + n) for n in names}
    staged = [e["staged0"], e["staged1"]]
    C = 5
    W = 2 * C
    N = H * C
    with ExitStack() as st:
        sb = lambda n, shape, dt=F32: k.sb(st, "hg_" + n, shape, dt)
        v = sb("v", [P, 2, T + NS])
        s0 = sb("s0", [P, 2, NB, P])
        kk, lf = sb("k", [P, 2, T]), sb("lf", [P, 2, T + NS])
        f, tiny = sb("f", [P, T]), sb("tiny", [P, T])
        lth, ltl = sb("lth", [P, P], F32R), sb("ltl", [P, P], F32R)
        vt = sb("vt", [P, C, P])
        ex = sb("ex", [P, 2, LEVELS, P])
        qd, kd = sb("qd", [P, 2, P]), sb("kd", [P, 2, P])
        last = sb("last", [P, 2, NB])
        picked = sb("picked", [P, (LEVELS + 1) * P])
        att, kt = sb("att", [P, P]), sb("kt", [P, P])
        vm, snew = sb("vm", [NS, NB, P]), sb("snew", [P, NB, P])
        S = sb("S", [P, 2, P])
        o, y = sb("o", [P, 2, T]), sb("y", [P, T])
        orstd, gate = sb("orstd", [P, T]), sb("gate", [P, T])
        zf = k.z[:].rearrange("p k n -> p (k n)")
        xh, xl = (t[:].rearrange("p k n -> p (k n)") for t in (k.xh, k.xl))

        class Tile:

            def __init__(self, i, t):
                self.t = t
                self.done = i * W + (t + 1)
                self.pair = i + t // W
                self.c = t % C
                self.head = i * 2 + t // C
                self.hs = (t // C) % 2
                self.s = t % 2
                self.sample = self.c == C - 1
                self.t0 = self.c * P
                self.n, self.levels = (NS, SLEVELS) if self.sample else (P, LEVELS)
                self.cols = slice(self.t0, self.t0 + self.n)

            def z(self, j):
                return zf[:, bass.ds((j * H + self.head) * T + self.t0, self.n)]

            def ex(self):
                return ex[:, self.s].rearrange("p l n -> p (l n)")[:, 0:self.levels * self.n].rearrange("p (l n) -> p l n", n=self.n)

            def scores(self):
                w = self.levels + 1
                if self.sample:
                    return ps[0:self.n, 3, 0:w * self.n].rearrange("p (l n) -> p l n", l=w)
                return ps[:, 3:5, :].rearrange("p a n -> p (a n)").rearrange("p (l n) -> p l n", l=w)

        def steps(eng, stage, head_work, order):
            ahead = {"turn": 3, "sum": 2, "score": 1, "advance": 0}

            for name, t in (("turn", 0), ("sum", 0), ("turn", 1), ("sum", 1), ("turn", 2), ("score", 0)):
                stage[name](Tile(0, t))

            def body(i, rest):
                for t in range(W):
                    for name in order:
                        if t + ahead[name] < rest:
                            stage[name](Tile(i, t + ahead[name]))
                        if name == "advance":
                            head_work(i, t, rest)
                head_work(i, W, rest)

            with eng.Fori(0, H // 2 - 1) as i:
                body(i, W + 3)
            body(H // 2 - 1, W)

        none = lambda *a: None

        with nc.Block() as block:
            @block.sync
            def _(sp):
                def stage_head(i, s):
                    head = i * 2 + s
                    sp.dma_start(v[:, s, 0:T], zf[:, bass.ds((2 * H + head) * T, T)]).then_inc(staged[s], 16)
                    sp.dma_start(s0[:, s], k.state_hgrn[0].rearrange("b h d v -> h d b v")[bass.ds(head, 1)]
                                 .rearrange("h d b v -> (h d) b v")).then_inc(staged[s], 16)

                def put(i, s):
                    head = i * 2 + s
                    sp.wait_ge(e["state"], i * W + (C * s + 4))
                    sp.dma_start(k.out["hgrn_prompt"][0, 0][bass.ds(head, 1)].rearrange("h d v -> (h d) v"), S[:, s]
                                 ).then_inc(e["pstored"], 16)
                    sp.wait_ge(e["state"], i * W + (C * s + 5))
                    sp.dma_start(k.out["hgrn_sample"][0].rearrange("b h d v -> h d b v")[bass.ds(head, 1)]
                                 .rearrange("h d b v -> (h d) b v"), snew[:]).then_inc(e["stored"], 16)
                    sp.wait_ge(e["pstored"], head * 16 + 16)
                    sp.wait_ge(e["stored"], head * 16 + 16)
                    sp.sem_inc(e["free"], 1)

                sp.sem_inc(e["free"], 2)
                stage_head(0, 0)
                stage_head(0, 1)
                with sp.Fori(0, H // 2 - 1) as i:
                    for s in range(2):
                        put(i, s)
                        stage_head(i + 1, s)
                put(H // 2 - 1, 0)
                put(H // 2 - 1, 1)

            @block.tensor
            def _(pe):
                def turn(a):
                    if a.c == 0:
                        pe.wait_ge(e["logf"], a.head + 1)
                        pe.wait_ge(staged[a.hs], a.pair * 32 + 32)
                    if a.t > 2 and a.c == 2:
                        pe.wait_ge(e["state"], a.done - 3)
                    pe.transpose(ps[:, 6, 0:P], lf[:, a.hs, a.t0:a.t0 + P], k.ident[:])
                    pe.transpose(ps[:, 6, P:2 * P], v[:, a.hs, a.t0:a.t0 + P], k.ident[:]).then_inc(e["turned"], 1)

                def sums(a):
                    decay = k.sdecay if a.sample else k.decay
                    n, w = a.n, a.levels * a.n
                    pe.wait_ge(e["low"], a.done)
                    pe.wait_ge(e["valued"], a.done)
                    if a.t > 0:
                        pe.wait_ge(e["decayed"], a.done - 1)
                    cuts = [(1, 0, w)] if a.sample else [(1, 0, 4 * P), (2, 4 * P, w)]
                    for bank, c0, c1 in cuts + [(0, w, w + 2 * n)]:
                        for n_, part in enumerate((lth, ltl)):
                            mm = pe.matmul(ps[:, bank, 0:c1 - c0], part[0:n, :], decay[0:n, c0:c1],
                                           start=n_ == 0, stop=n_ == 1)
                    mm.then_inc(e["summed"], 1)

                def score(a):
                    x, n = a.ex(), a.n
                    pe.wait_ge(e["keys"], a.done)
                    pe.wait_ge(e["queries"], a.done)
                    if a.t > 0:
                        pe.wait_ge(e["state"], a.done - 1)
                        pe.wait_ge(e["copied"], a.done - 1)
                        pe.wait_ge(e["picked"], a.done - 1)
                    pe.transpose(ps[:, 7, 2 * P:3 * P], kd[:, a.s, :], k.ident[:])
                    for l in range(a.levels):
                        pe.matmul(ps[0:n, 3 + l * n // 512, l * n % 512:l * n % 512 + n], x[:, l, :], x[:, l, :],
                                  start=True, stop=True)
                    at = a.levels * n
                    pe.matmul(ps[0:n, 3 + at // 512, at % 512:at % 512 + n], kk[:, a.hs, a.cols], a.z(0),
                              start=True, stop=True).then_inc(e["scored"], 1)

                def advance(a):
                    n, vv, qq = a.n, vt[:, a.c, :], qd[:, a.s, :]
                    pe.wait_ge(e["attended"], a.done)
                    pe.wait_ge(e["keyrows"], a.done)
                    if not a.sample:
                        pe.matmul(ps[:, 7, 0:P], vv, att[:], start=True, stop=a.c == 0)
                        if a.c > 0:
                            pe.matmul(ps[:, 7, 0:P], S[:, a.hs], qq, start=False, stop=True)
                        pe.matmul(ps[:, 7, P:2 * P], kt[:], vv, start=True, stop=True).then_inc(e["read"], 1)
                        return
                    pe.matmul(ps[:, 7, 0:NS], vv[0:NS], att[0:NS, 0:NS], start=True, stop=True)
                    for b in range(NB):
                        for r in (slice(0, 64), slice(64, P)):
                            pe.matmul(ps[r, 7, b * NQ:(b + 1) * NQ], s0[:, a.hs, b, r], qq[:, b * NQ:(b + 1) * NQ],
                                      start=False, stop=True, skip_group_check=True)
                    pe.wait_ge(e["vmasked"], a.head + 1)
                    for g in range(2):
                        mm = pe.matmul(ps[:, 5 + g, :], kt[0:NS, :], vm[:, 4 * g:4 * g + 4, :].rearrange("p b v -> p (b v)"),
                                       start=True, stop=True)
                    mm.then_inc(e["read"], 1)

                def work(i, t, rest):
                    for s, at in ((0, C + 1), (1, W)):
                        if t == at:
                            pe.wait_ge(e["squared"], i * 2 + (s + 1))
                            pe.wait_ge(e["state"], i * W + C * (s + 1))
                            pe.wait_ge(e["low"], i * W + (C + 4 if s == 0 else rest))
                            for a in range(2):
                                mm = pe.matmul(ps[:, 5 + a, 0:HALF], k.mean[:], y[:, a * HALF:(a + 1) * HALF], start=True, stop=True)
                            mm.then_inc(e["meant"], 1)
                            pe.wait_ge(e["rlog"], i * 2 + (s + 1))

                steps(pe, {"turn": turn, "sum": sums, "score": score, "advance": advance}, work,
                      ("sum", "advance", "turn", "score"))

            @block.scalar
            def _(act):
                def prepare(head, s):
                    z = zf[:, bass.ds((H + head) * T, T)]
                    act.activation(f[:], z, ACT.Sigmoid)
                    act.activation(kk[:, s, :], z, ACT.Sigmoid, scale=-1.0).then_inc(e["sigmoids"], 1)

                def logs(head, s):
                    act.wait_ge(e["lifted"], head + 1)
                    act.activation(lf[:, s, 0:T], f[:], ACT.Ln).then_inc(e["logged"], 1)

                def turn(a):
                    act.wait_ge(e["turned"], a.done)
                    act.activation(lth[0:a.n, :], ps[0:a.n, 6, 0:P], ACT.Copy).then_inc(e["high"], 1)
                    act.activation(vt[0:a.n, a.c, :], ps[0:a.n, 6, P:2 * P], ACT.Copy).then_inc(e["valued"], 1)

                def sums(a):
                    n = a.n
                    act.wait_ge(e["summed"], a.done)
                    act.activation(a.ex(), ps[:, 1:3, :].rearrange("p a n -> p (a n)")[:, 0:a.levels * n]
                                   .rearrange("p (l n) -> p l n", n=n), ACT.Exp)
                    act.activation(qd[:, a.s, 0:n], ps[:, 0, 0:n], ACT.Exp)
                    act.activation(kd[:, a.s, 0:n], ps[:, 0, n:2 * n], ACT.Exp).then_inc(e["decayed"], 1)

                def score(a):
                    act.wait_ge(e["scored"], a.done)
                    act.activation(kt[0:a.n, :], ps[0:a.n, 7, 2 * P:3 * P], ACT.Copy).then_inc(e["keyrows"], 1)

                def advance(a):
                    act.wait_ge(e["read"], a.done)
                    act.activation(o[:, a.hs, a.cols], ps[:, 7, 0:a.n], ACT.Copy).then_inc(e["copied"], 1)

                def finish(i, s, part):
                    head = i * 2 + s
                    if part == 0:
                        act.wait_ge(e["copied"], i * W + C * (s + 1))
                        act.wait_ge(e["olow"], head + 1)
                        act.activation(y[:], o[:, s, :], ACT.Square).then_inc(e["squared"], 1)
                    elif part == 1:
                        act.wait_ge(e["meant"], head + 1)
                        act.activation(halves(orstd[:]), ps[:, 5:7, 0:HALF], ACT.Ln, bias=k.eps[:, 0:1]).then_inc(e["rlog"], 1)
                        act.wait_ge(e["rlog"], head + 1)
                        act.activation(orstd[:], orstd[:], ACT.Exp, scale=-0.5).then_inc(e["rstd"], 1)
                        act.activation(gate[:], zf[:, bass.ds((3 * H + head) * T, T)], ACT.Silu).then_inc(e["gate"], 1)
                    else:
                        act.wait_ge(e["gated"], head + 1)
                        act.activation(xh[:, bass.ds(head * T, T)], y[:], ACT.Copy).then_inc(e["ohigh"], 1)

                def work(i, t, rest):
                    if t in (0, C) and (t == 0 or rest > W):
                        head = i * 2 + t // C + 1
                        prepare(head, (t // C + 1) % 2)
                    if t in (1, C + 1) and (t == 1 or rest > W):
                        logs(i * 2 + t // C + 1, (t // C + 1) % 2)
                    for s, part, at in ((0, 0, C), (0, 1, C + 1), (0, 2, C + 3), (1, 0, W), (1, 1, W), (1, 2, W)):
                        if t == at:
                            finish(i, s, part)

                prepare(0, 0)
                logs(0, 0)
                steps(act, {"turn": turn, "sum": sums, "score": score, "advance": advance}, work,
                      ("advance", "sum", "turn", "score"))

            @block.gpsimd
            def _(pool):
                def sums(a):
                    x, keys = a.ex(), kk[:, a.hs, a.cols]
                    if a.c == 0:
                        pool.wait_ge(e["scaled"], a.head + 1)
                    pool.wait_ge(e["decayed"], a.done)
                    for l in range(a.levels):
                        b = 1 << l
                        xv, kv = (r.rearrange("p (a r b) -> p a r b", r=2, b=b)[:, :, 0, :] for r in (x[:, l, :], keys))
                        pool.tensor_tensor(xv, xv, kv, ALU.mult)
                    dk = kd[:, a.s, 0:a.n]
                    pool.tensor_tensor(dk, dk, keys, ALU.mult).then_inc(e["keys"], 1)
                    if a.sample:
                        pool.wait_ge(e["valued"], a.done)
                        pool.wait_ge(e["free"], a.head + 2)
                        pool.tensor_tensor(vm[:], vt[0:NS, a.c, :].unsqueeze(1).broadcast_to([NS, NB, P]),
                                           k.batch[:].rearrange("p (b v) -> p b v", b=NB), ALU.mult).then_inc(e["vmasked"], 1)

                steps(pool, {"turn": none, "sum": sums, "score": none, "advance": none}, none, ("sum", "advance"))

            @block.vector
            def _(dve):
                def prepare(head, s):
                    lb, one_lb = (k.lb[:, bass.ds(head, 1), j] for j in range(2))
                    dve.wait_ge(e["sigmoids"], head + 1)
                    dve.tensor_scalar(kk[:, s, :], kk[:, s, :], one_lb, None, ALU.mult).then_inc(e["scaled"], 1)
                    dve.tensor_scalar(f[:], f[:], one_lb, lb, ALU.mult, ALU.add).then_inc(e["floored"], 1)
                    dve.wait_ge(e["floored"], head * 2 + 1)
                    dve.tensor_scalar(f[:], f[:], MIN_F, None, ALU.max).then_inc(e["floored"], 1)
                    dve.wait_ge(e["floored"], head * 2 + 2)
                    dve.tensor_scalar(tiny[:], f[:], 2.0 ** -30, 2.0 ** LN_LIFT - 1.0, ALU.is_lt, ALU.mult).then_inc(e["tiny"], 1)
                    dve.wait_ge(e["tiny"], head + 1)
                    dve.scalar_tensor_tensor(f[:], tiny[:], 1.0, f[:], ALU.add, ALU.mult).then_inc(e["lifted"], 1)

                def logs(head, s):
                    dve.wait_ge(e["logged"], head + 1)
                    dve.scalar_tensor_tensor(lf[:, s, 0:T], tiny[:], -LN_LIFT * float(np.log(2.0)) / (2.0 ** LN_LIFT - 1.0),
                                             lf[:, s, 0:T], ALU.mult, ALU.add).then_inc(e["logf"], 1)

                def turn(a):
                    dve.wait_ge(e["high"], a.done)
                    dve.wait_ge(e["valued"], a.done)
                    dve.tensor_tensor(ltl[0:a.n, :], ps[0:a.n, 6, 0:P], lth[0:a.n, :].bitcast(F32), ALU.subtract
                                      ).then_inc(e["low"], 1)

                def sums(a):
                    x, n, z = a.ex(), a.n, a.z(0)
                    dve.wait_ge(e["decayed"], a.done)
                    for l in range(a.levels):
                        b = 1 << l
                        xv, qv = (r.rearrange("p (a r b) -> p a r b", r=2, b=b)[:, :, 1, :] for r in (x[:, l, :], z))
                        dve.tensor_tensor(xv, xv, qv, ALU.mult)
                    lst = (last[:, a.s, 0:NB], qd[:, a.s, NQ - 1:n:NQ]) if a.sample else (last[:, a.s, 0:1], qd[:, a.s, n - 1:n])
                    dve.tensor_copy(*lst).then_inc(e["last"], 1)
                    dve.wait_ge(e["last"], a.done)
                    dve.tensor_tensor(qd[:, a.s, 0:n], qd[:, a.s, 0:n], z, ALU.mult).then_inc(e["queries"], 1)

                def score(a):
                    masks = (k.ssplit if a.sample else k.split)[:].rearrange("p (l n) -> p l n", n=a.n)
                    w = a.levels + 1
                    dve.wait_ge(e["scored"], a.done)
                    pairs = picked[0:a.n, 0:w * a.n].rearrange("p (l n) -> p l n", l=w)
                    dve.tensor_tensor(pairs, a.scores(), masks, ALU.mult).then_inc(e["picked"], 1)
                    dve.wait_ge(e["picked"], a.done)
                    dve.tensor_reduce(att[0:a.n, 0:a.n], pairs.rearrange("p l n -> p n l"), AX.X, ALU.add
                                      ).then_inc(e["attended"], 1)

                def advance(a):
                    dve.wait_ge(e["copied"], a.done)
                    if a.c == 0:
                        dve.wait_ge(e["free"], a.head + 1)
                        dve.tensor_copy(S[:, a.hs], ps[:, 7, P:2 * P]).then_inc(e["state"], 1)
                    elif not a.sample:
                        dve.scalar_tensor_tensor(S[:, a.hs], S[:, a.hs], last[:, a.s, 0:1], ps[:, 7, P:2 * P], ALU.mult,
                                                 ALU.add).then_inc(e["state"], 1)
                    else:
                        dve.wait_ge(e["free"], a.head + 2)
                        for b in range(NB):
                            ins = dve.scalar_tensor_tensor(
                                snew[:, b, :], s0[:, a.hs, b, :], last[:, a.s, b:b + 1],
                                ps[:, 5 + b // 4, (b % 4) * P:(b % 4 + 1) * P], ALU.mult, ALU.add)
                        ins.then_inc(e["state"], 1)
                    dve.wait_ge(e["state"], a.done)

                def finish(i, s, part):
                    head = i * 2 + s
                    if part == 0:
                        dve.wait_ge(e["rstd"], head + 1)
                        dve.scalar_tensor_tensor(y[:], o[:, s, :], k.onorm[:, 0:1], orstd[:], ALU.mult, ALU.mult
                                                 ).then_inc(e["normed"], 1)
                        dve.wait_ge(e["normed"], head + 1)
                        dve.wait_ge(e["gate"], head + 1)
                        dve.tensor_tensor(y[:], y[:], gate[:], ALU.mult).then_inc(e["gated"], 1)
                    else:
                        dve.wait_ge(e["ohigh"], head + 1)
                        dve.tensor_tensor(xl[:, bass.ds(head * T, T)], y[:], xh[:, bass.ds(head * T, T)].bitcast(F32),
                                          ALU.subtract).then_inc(e["olow"], 1)

                def work(i, t, rest):
                    if t in (0, C) and (t == 0 or rest > W):
                        prepare(i * 2 + t // C + 1, (t // C + 1) % 2)
                    if t in (1, C + 1) and (t == 1 or rest > W):
                        logs(i * 2 + t // C + 1, (t // C + 1) % 2)
                    if t == C + 2:
                        finish(i, 0, 0)
                    if t == C + 3:
                        finish(i, 0, 1)
                    if t == W:
                        finish(i, 1, 0)
                        finish(i, 1, 1)

                dve.sem_inc(e["olow"], 1)
                dve.memset(lf[:, 0, T:T + NS], 0.0).then_inc(e["zero"], 1)
                dve.memset(lf[:, 1, T:T + NS], 0.0).then_inc(e["zero"], 1)
                dve.memset(v[:, :, T:T + NS], 0.0).then_inc(e["zero"], 1)
                dve.memset(kd[:], 0.0).then_inc(e["zero"], 1)
                dve.wait_ge(e["zero"], 4)
                prepare(0, 0)
                logs(0, 0)
                steps(dve, {"turn": turn, "sum": sums, "score": score, "advance": advance}, work,
                      ("advance", "sum", "turn", "score"))




def lower_bound(k):
    nc = k.nc
    top, ex, tot, done, scaled = (k.sem("lb_" + n) for n in ("top", "exp", "total", "done", "scaled"))
    with ExitStack() as st:
        d, p, r, q = (k.sb(st, "lb_" + n, [P, KD]) for n in ("d", "p", "r", "q"))
        with nc.Block() as block:
            @block.vector
            def _(dve):
                dve.tensor_scalar(k.qn8[:], k.qn[:], DH ** -0.5, None, ALU.mult).then_inc(scaled, 1)
                dve.tensor_tensor(d[:], k.a_lb[:], k.a_lb[:], ALU.subtract).then_inc(top, 1)
                dve.wait_ge(ex, 1)
                dve.reciprocal(r[:], p[:]).then_inc(tot, 1)
                dve.wait_ge(tot, 1)
                dve.tensor_tensor(q[:], p[:], r[:], ALU.mult).then_inc(tot, 1)
                dve.wait_ge(tot, 2)
                dve.tensor_tensor(k.lb[:, :, 0], q[:], q[:], ALU.subtract).then_inc(tot, 1)
                dve.wait_ge(tot, 3)
                dve.tensor_scalar(k.lb[:, :, 1], k.lb[:, :, 0], -1.0, 1.0, ALU.mult, ALU.add).then_inc(done, 1)

            @block.scalar
            def _(act):
                act.wait_ge(top, 1)
                act.activation(p[:], d[:], ACT.Exp).then_inc(ex, 1)


def forget_values(k, xh, xl):
    nc, ps = k.nc, k.ps
    e = {n: k.sem("fv_" + n) for n in ("loaded", "high", "low", "summed", "z", "abs", "exp", "ln", "logf", "turned", "rows",
                                       "stored", "cum", "c", "cstored")}
    with ExitStack() as tmp:
        lfrows = k.sb(tmp, "lf_rows", [P, 5, BH])
        w = k.sb(tmp, "fv_w", [P, KD, BH])
        wh, wl = (k.sb(tmp, n, [P, KD, BH], F32R) for n in ("fv_wh", "fv_wl"))
        bf = k.sb(tmp, "fv_bf", [BH, 1])
        tri, ones = k.sb(tmp, "fv_tri", [P, P]), k.sb(tmp, "fv_ones", [P, P])
        z, ab, lf = (k.sb(tmp, n, [BH, T]) for n in ("fv_z", "fv_ab", "fv_lf"))
        c2 = k.sb(tmp, "fv_c", [BH, 2, SEQ])
        with nc.Block() as block:
            @block.sync
            def _(sp):
                sp.dma_start(w[:], k.w["w_kvf"].rearrange("(k p) n -> p k n", p=P)[:, :, 2 * D:2 * D + BH]).then_inc(e["loaded"], 16)
                sp.dma_start(bf[:], k.w["b_f"].rearrange("(p o) -> p o", o=1), allow_slow_non_contiguous=True).then_inc(e["loaded"], 16)
                sp.dma_start(tri[:], k.w["c_tri"]).then_inc(e["loaded"], 16)
                sp.wait_ge(e["rows"], 1)
                sp.dma_start(k.out["logf_prompt"].rearrange("b (c p) h -> p (b c) h", p=P), lfrows[:, 0:4, :]).then_inc(e["stored"], 16)
                sp.dma_start(k.out["logf_sample"].rearrange("b q h -> (b q) h"), lfrows[0:NS, 4, :]).then_inc(e["stored"], 16)
                sp.wait_ge(e["c"], 2)
                sp.dma_start(k.cum_prompt.rearrange("s h n -> h s n"), c2[:]).then_inc(e["cstored"], 16)
                sp.wait_ge(e["stored"], 32)
                sp.wait_ge(e["cstored"], 16)

            @block.scalar
            def _(act):
                act.wait_ge(e["loaded"], 48)
                act.activation(wh[:], w[:], ACT.Copy).then_inc(e["high"], 1)
                act.wait_ge(e["summed"], 1)
                act.activation(halves(z[:]), ps[0:BH, 0:2, 0:HALF], ACT.Identity, bias=bf[:, 0:1]).then_inc(e["z"], 1)
                act.wait_ge(e["z"], 1)
                act.activation(ab[:], z[:], ACT.Abs).then_inc(e["abs"], 1)
                act.wait_ge(e["abs"], 1)
                act.activation(ab[:], ab[:], ACT.Exp, scale=-1.0).then_inc(e["exp"], 1)
                act.wait_ge(e["exp"], 1)
                act.activation(ab[:], ab[:], ACT.Ln, bias=1.0).then_inc(e["ln"], 1)
                act.wait_ge(e["cum"], 1)
                act.activation(c2[:, 0, :], ps[0:BH, 3, :], ACT.Copy).then_inc(e["c"], 1)
                act.activation(c2[:, 1, :], ps[0:BH, 3, :], ACT.Copy, scale=-1.0).then_inc(e["c"], 1)

            @block.vector
            def _(dve):
                dve.memset(ones[:], 1.0)
                dve.wait_ge(e["high"], 1)
                dve.tensor_tensor(wl[:], w[:], wh[:].bitcast(F32), ALU.subtract).then_inc(e["low"], 1)
                dve.wait_ge(e["ln"], 1)
                dve.scalar_tensor_tensor(lf[:], z[:], 0.0, ab[:], ALU.min, ALU.subtract).then_inc(e["logf"], 1)
                dve.wait_ge(e["turned"], 1)
                dve.tensor_copy(lfrows[:, 0:4, :], ps[:, 2, 0:4 * BH].rearrange("p (c h) -> p c h", c=4))
                dve.tensor_copy(lfrows[0:NS, 4, :], ps[0:NS, 2, 4 * BH:5 * BH]).then_inc(e["rows"], 1)

            @block.tensor
            def _(pe):
                pe.wait_ge(e["low"], 1)
                for t in range(KD):
                    for n, (wt, at) in enumerate(((wh, xh), (wh, xl), (wl, xh))):
                        for a in range(2):
                            mm = pe.matmul(ps[0:BH, a, 0:HALF], wt[:, t, :], at[:, t, a * HALF:(a + 1) * HALF],
                                           start=t == 0 and n == 0, stop=t == KD - 1 and n == 2)
                mm.then_inc(e["summed"], 1)
                pe.wait_ge(e["logf"], 1)
                for c in range(5):
                    n = P if c < 4 else NS
                    mm = pe.transpose(ps[0:n, 2, c * BH:(c + 1) * BH], lf[:, c * P:c * P + n], k.ident[0:BH, 0:BH])
                mm.then_inc(e["turned"], 1)
                pe.wait_ge(e["rows"], 1)
                for c in range(4):
                    for i in range(c + 1):
                        mm = pe.matmul(ps[0:BH, 3, c * P:(c + 1) * P], lfrows[:, i, :], (tri if i == c else ones)[:],
                                       start=i == 0, stop=i == c)
                mm.then_inc(e["cum"], 1)


def head_rows(k, name, flat, first, gain=None, rows=None):
    nc, ps = k.nc, k.ps
    e = {n: k.sem(name + "_" + n) for n in ("squared", "summed", "logged", "rstd", "y", "kept", "turned", "rows")}
    with ExitStack() as tmp:
        sq, rstd, y = (k.sb(tmp, name + n, [P, T]) for n in ("_sq", "_rstd", "_y"))
        tile = lambda j: flat[:, bass.ds((j + first) * T, T)]
        with nc.Block() as block:
            @block.scalar
            def _(act):
                with act.Fori(0, KD) as j:
                    if gain is not None:
                        act.activation(sq[:], tile(j), ACT.Square).then_inc(e["squared"], 1)
                        act.wait_ge(e["summed"], j + 1)
                        act.activation(halves(rstd[:]), ps[:, 0:2, 0:HALF], ACT.Ln, bias=k.eps[:, 0:1]).then_inc(e["logged"], 1)
                        act.wait_ge(e["logged"], j + 1)
                        act.activation(rstd[:], rstd[:], ACT.Exp, scale=-0.5).then_inc(e["rstd"], 1)
                        act.wait_ge(e["y"], j + 1)
                    if rows is not None:
                        act.wait_ge(e["turned"], j + 1)
                        act.activation(rows[:, 0:4, bass.ds(j * P, P)], ps[:, 4, :].rearrange("p (c n) -> p c n", c=4), ACT.Copy)
                        act.activation(rows[0:NS, 4, bass.ds(j * P, P)], ps[0:NS, 5, 0:P], ACT.Copy).then_inc(e["rows"], 1)

            @block.vector
            def _(dve):
                if rows is not None:
                    dve.sem_inc(e["rows"], 1)
                if gain is not None:
                    dve.sem_inc(e["kept"], 1)
                with dve.Fori(0, KD) as j:
                    if rows is not None:
                        dve.wait_ge(e["rows"], j + 1)
                    if gain is not None:
                        dve.wait_ge(e["kept"], j + 1)
                        dve.wait_ge(e["rstd"], j + 1)
                        dve.scalar_tensor_tensor(y[:], tile(j), gain, rstd[:], ALU.mult, ALU.mult).then_inc(e["y"], 1)
                    else:
                        dve.tensor_copy(y[:], tile(j)).then_inc(e["y"], 1)

            @block.gpsimd
            def _(pool):
                if gain is not None:
                    with pool.Fori(0, KD) as j:
                        pool.wait_ge(e["y"], j + 1)
                        pool.tensor_copy(tile(j), y[:]).then_inc(e["kept"], 1)

            @block.tensor
            def _(pe):
                with pe.Fori(0, KD) as j:
                    if gain is not None:
                        pe.wait_ge(e["squared"], j + 1)
                        for a in range(2):
                            mm = pe.matmul(ps[:, a, 0:HALF], k.headmean[:], sq[:, a * HALF:(a + 1) * HALF], start=True, stop=True)
                        mm.then_inc(e["summed"], 1)
                    if rows is not None:
                        pe.wait_ge(e["y"], j + 1)
                        pe.wait_ge(e["rows"], j + 1)
                        for c in range(4):
                            pe.transpose(ps[:, 4, c * P:(c + 1) * P], y[:, c * P:(c + 1) * P], k.ident[:])
                        pe.transpose(ps[0:NS, 5, 0:P], y[:, SEQ:T], k.ident[:]).then_inc(e["turned"], 1)


def prompt_attention(k, kf, qf, vrows, oT, pages, past_logf, past_sems):
    nc, ps = k.nc, k.ps
    e = {n: k.sem("pa_" + n) for n in ("const", "staged", "scored", "max", "exp", "inv", "scaled", "turned", "rows", "mixed", "done")}
    U = 8
    with ExitStack() as st:
        kj, qj, vj = k.sb(st, "pa_k", [P, SEQ]), k.sb(st, "pa_q", [P, SEQ]), k.sb(st, "pa_v", [P, 4, P])
        bl, br = k.sb(st, "pa_bl", [2, 2, SEQ]), k.sb(st, "pa_br", [2, 2, SEQ])
        causal = k.sb(st, "pa_causal", [P, P])
        nm, tot, inv = (k.sb(st, n, [P, 2]) for n in ("pa_nm", "pa_tot", "pa_inv"))
        pr, pt = k.sb(st, "pa_pr", [P, 2, SEQ]), k.sb(st, "pa_pt", [P, 2, SEQ])

        with nc.Block() as block:
            @block.gpsimd
            def _(pool):
                pool.dma_start(pages[:], k.w["page_table"].rearrange("b p -> (b p)").unsqueeze(0)).then_inc(past_sems["pages"], 16)
                pool.wait_ge(past_sems["pages"], 16)
                with pool.Fori(0, NB) as b:
                    for p in range(PAGES):
                        page = pool.value_load(pages[0:1, bass.ds(b * PAGES + p, 1)], min_val=0, max_val=k.n_pool - 1)
                        pool.dma_start(past_logf[:, p, bass.ds(b * BH, BH)], k.w["cache_logf"][bass.ds(page, 1)]
                                       .rearrange("o t h -> t (o h)")).then_inc(past_sems["gathered"], 16)

            @block.sync
            def _(sp):
                sp.dma_start(causal[:], k.w["c_causal"]).then_inc(e["const"], 16)
                for a in range(2):
                    sp.dma_start(bl[0:1, a, :], k.w["c_ones"][0:1, 0:SEQ]).then_inc(e["const"], 16)
                    sp.dma_start(br[1:2, a, :], k.w["c_ones"][0:1, 0:SEQ]).then_inc(e["const"], 16)
                sp.sem_inc(e["done"], 1)
                with sp.Fori(0, KD) as j:
                    sp.wait_ge(e["done"], j + 1)
                    sp.dma_start(kj[:], kf[:, bass.ds(j * T, SEQ)]).then_inc(e["staged"], 16)
                    sp.dma_start(qj[:], qf[:, bass.ds(j * T, SEQ)]).then_inc(e["staged"], 16)
                    sp.dma_start(vj[:], vrows[:, 0:4, bass.ds(j * P, P)]).then_inc(e["staged"], 16)
                    sp.dma_start(bl[1:2, :, :], k.cum_prompt[0][bass.ds(2 * j, 2)].unsqueeze(0)).then_inc(e["staged"], 16)
                    sp.dma_start(br[0:1, :, :], k.cum_prompt[1][bass.ds(2 * j, 2)].unsqueeze(0)).then_inc(e["staged"], 16)

            @block.tensor
            def _(pe):
                def score(j, u):
                    a, i = divmod(u, 4)
                    n = (i + 1) * P
                    if u >= 2:
                        pe.wait_ge(e["exp"], U * j + u - 1)
                    r = slice(DH * a, DH * (a + 1))
                    out = ps[:, u % 2, 0:n]
                    pe.matmul(out, qj[r, i * P:(i + 1) * P], kj[r, 0:n], start=True, stop=False)
                    pe.matmul(ps[:, u % 2, i * P:n], k.ident[:], causal[:], start=False, stop=False)
                    pe.matmul(out, bl[:, a, i * P:(i + 1) * P], br[:, a, 0:n], start=False, stop=True
                              ).then_inc(e["scored"], 1)

                def turn(j, u):
                    pe.wait_ge(e["scaled"], U * j + u + 1)
                    if u >= 2:
                        pe.wait_ge(e["rows"], U * j + u - 1)
                    for c in range(u % 4 + 1):
                        mm = pe.transpose(ps[:, 2 + u % 2, c * P:(c + 1) * P], pr[:, u % 2, c * P:(c + 1) * P], k.ident[:])
                    mm.then_inc(e["turned"], 1)

                def mix(j, u):
                    a, i = divmod(u, 4)
                    pe.wait_ge(e["rows"], U * j + u + 1)
                    for c in range(i + 1):
                        mm = pe.matmul(ps[DH * a:DH * (a + 1), 4, i * P:(i + 1) * P], vj[:, c, DH * a:DH * (a + 1)],
                                       pt[:, u % 2, c * P:(c + 1) * P], start=c == 0, stop=c == i)
                    mm.then_inc(e["mixed"], 1)

                pe.wait_ge(e["const"], 80)
                with pe.Fori(0, KD) as j:
                    pe.wait_ge(e["staged"], 80 * j + 80)
                    pe.wait_ge(e["done"], j + 1)
                    for u in range(U + 2):
                        if u < U:
                            score(j, u)
                        if 1 <= u <= U:
                            turn(j, u - 1)
                        if u >= 2:
                            mix(j, u - 2)

            @block.scalar
            def _(act):
                with act.Fori(0, KD) as j:
                    for u in range(U):
                        n = (u % 4 + 1) * P
                        act.wait_ge(e["max"], U * j + u + 1)
                        if u >= 2:
                            act.wait_ge(e["turned"], U * j + u - 1)
                        act.activation(pr[:, u % 2, 0:n], ps[:, u % 2, 0:n], ACT.Exp, bias=nm[:, u % 2:u % 2 + 1],
                                       accum_out=tot[:, u % 2:u % 2 + 1]).then_inc(e["exp"], 1)

            @block.vector
            def _(dve):
                def rows(j, u):
                    n = (u % 4 + 1) * P
                    dve.wait_ge(e["turned"], U * j + u + 1)
                    if u >= 2:
                        dve.wait_ge(e["mixed"], U * j + u - 1)
                    dve.tensor_copy(pt[:, u % 2, 0:n], ps[:, 2 + u % 2, 0:n]).then_inc(e["rows"], 1)

                with dve.Fori(0, KD) as j:
                    for u in range(U):
                        n = (u % 4 + 1) * P
                        s = slice(u % 2, u % 2 + 1)
                        dve.wait_ge(e["scored"], U * j + u + 1)
                        if u >= 2:
                            dve.wait_ge(e["exp"], U * j + u - 1)
                        dve.tensor_reduce(nm[:, s], ps[:, u % 2, 0:n], AX.X, ALU.max, negate=True).then_inc(e["max"], 1)
                        if u >= 1:
                            rows(j, u - 1)
                        dve.wait_ge(e["exp"], U * j + u + 1)
                        dve.reciprocal(inv[:, s], tot[:, s]).then_inc(e["inv"], 1)
                        dve.wait_ge(e["inv"], U * j + u + 1)
                        dve.tensor_scalar(pr[:, u % 2, 0:n], pr[:, u % 2, 0:n], inv[:, s], None, ALU.mult).then_inc(e["scaled"], 1)
                    rows(j, U - 1)
                    dve.wait_ge(e["mixed"], U * j + U)
                    dve.tensor_copy(oT[:, bass.ds(j * T, SEQ)], ps[:, 4, :]).then_inc(e["done"], 1)


def past_decay(k, lf, past_sems):
    nc, ps = k.nc, k.ps
    e = {n: k.sem("pd_" + n) for n in ("loaded", "summed", "off", "neg", "new", "stored")}
    with ExitStack() as st:
        lnew = k.sb(st, "pd_new", [P, NQ])
        tri = k.sb(st, "pd_tri", [P, P])
        off = k.sb(st, "pd_off", [P, PAGES + 1])
        cnew = k.sb(st, "pd_cnew", [P, NQ])
        neg = k.sb(st, "pd_neg", [P, PAST + NQ])
        with nc.Block() as block:
            @block.sync
            def _(sp):
                sp.dma_start(tri[:], k.w["c_tri"]).then_inc(e["loaded"], 16)
                for b in range(NB):
                    sp.dma_start(lnew[b * BH:(b + 1) * BH, :], k.out["logf_sample"][b].rearrange("q h -> h q"),
                                 allow_slow_non_contiguous=True).then_inc(e["loaded"], 16)
                sp.wait_ge(e["neg"], PAGES + 1)
                sp.wait_ge(e["new"], NQ)
                sp.dma_start(k.neg_decay, neg[:]).then_inc(e["stored"], 16)
                sp.dma_start(k.new_decay.rearrange("b (h q) -> (b h) q", h=BH), cnew[:]).then_inc(e["stored"], 16)
                sp.wait_ge(e["stored"], 32)

            @block.tensor
            def _(pe):
                pe.wait_ge(e["loaded"], 16 * (1 + NB))
                pe.wait_ge(past_sems["gathered"], 16 * NB * PAGES)
                for p in range(PAGES):
                    mm = pe.matmul(ps[:, p // 4, (p % 4) * P:(p % 4 + 1) * P], lf[:, p, :], tri[:], start=True, stop=True)
                mm.then_inc(e["summed"], 1)

            @block.vector
            def _(dve):
                dve.memset(off[:, 0:1], 0.0).then_inc(e["off"], 1)
                dve.wait_ge(e["summed"], 1)
                for p in range(PAGES):
                    local = ps[:, p // 4, (p % 4) * P:(p % 4 + 1) * P]
                    dve.wait_ge(e["off"], p + 1)
                    dve.tensor_tensor(off[:, p + 1:p + 2], off[:, p:p + 1], local[:, P - 1:P], ALU.add).then_inc(e["off"], 1)
                    dve.tensor_scalar(neg[:, p * P:(p + 1) * P], local, off[:, p:p + 1], -1.0, ALU.add, ALU.mult).then_inc(e["neg"], 1)
                for q in range(NQ):
                    before = off[:, PAGES:PAGES + 1] if q == 0 else cnew[:, q - 1:q]
                    dve.wait_ge(e["off"], PAGES + 1)
                    if q > 0:
                        dve.wait_ge(e["new"], q)
                    dve.tensor_tensor(cnew[:, q:q + 1], before, lnew[:, q:q + 1], ALU.add).then_inc(e["new"], 1)
                dve.wait_ge(e["new"], NQ)
                dve.tensor_scalar(neg[:, PAST:PAST + NQ], cnew[:], -1.0, None, ALU.mult).then_inc(e["neg"], 1)


def sample_attention(k, ks, qs, oT):
    nc, ps = k.nc, k.ps
    e = {n: k.sem("sa_" + n) for n in (
        "const", "zero", "rows", "vnew", "pages", "q", "qh", "ql", "turned", "kh", "kl", "used", "scored", "mx", "max", "exp",
        "sum", "inv", "pturned", "ph", "pl", "tailt", "tail", "vh", "vl", "pv", "om", "picked", "done")}
    kload = [k.sem(f"sa_kload{s}") for s in range(2)]
    vload = [k.sem(f"sa_vload{s}") for s in range(2)]
    G, J = 4, KD
    STEPS, HV = G * J, 2 * PAGES
    INSIDE = HV - 6
    KSLOTS, VSLOTS = 3, 4
    with ExitStack() as st:
        sb = lambda n, shape, dt=F32: k.sb(st, "sa_" + n, shape, dt)
        pages = sb("pages", [1, NB * PAGES], I32)
        kp, vp = sb("kp", [P, 2, 4, D]), sb("vp", [P, 2, 4, D])
        kh, kl = sb("kh", [P, KSLOTS, SEQ], F32R), sb("kl", [P, KSLOTS, SEQ], F32R)
        vh, vl = sb("vh", [P, VSLOTS, SEQ], F32R), sb("vl", [P, VSLOTS, SEQ], F32R)
        qz = sb("qz", [P, J * P])
        qh, ql = sb("qh", [P, J, P], F32R), sb("ql", [P, J, P], F32R)
        vn = sb("vn", [NQ, D])
        rowl, rowr = sb("rowl", [BH + 1, P]), sb("rowr", [BH + 1, PAST + NQ])
        scausal, pickq, rowhead = sb("scausal", [P, NQ]), sb("pickq", [P, NQ]), sb("rowhead", [P, D])
        mx, tot, nm, inv = sb("mx", [P, G + 1]), sb("tot", [P, G + 1]), sb("nm", [P, 1]), sb("inv", [P, 2])
        pr, ptail, ptt = sb("pr", [P, PAST]), sb("ptail", [P, NQ]), sb("ptt", [NQ, P])
        ph, pl = sb("ph", [P, PAGES, P], F32R), sb("pl", [P, PAGES, P], F32R)
        om = sb("om", [P, D])
        cache = {"k": k.w["cache_k"].rearrange("n t h d -> n t (h d)"), "v": k.w["cache_v"].rearrange("n t h d -> n t (h d)")}

        def at(h):
            return 3 + h * (STEPS - 2) // INSIDE

        def step_units(i, lead):
            return [h for h in range(HV) if (i == 0 if h < lead else h - lead < INSIDE and at(h - lead) == i)]

        def last_units(lead):
            return range(INSIDE + lead, HV)

        LEAD = 3

        with nc.Block() as block:
            @block.sync
            def _(sp):
                sp.dma_start(pages[:], k.w["page_table"].rearrange("b p -> (b p)").unsqueeze(0)).then_inc(e["pages"], 16)
                for dst, src in ((rowl[0:BH, :], "c_headrow"), (scausal[:], "c_scausal"), (pickq[:], "c_pickq"),
                                 (rowhead[:], "c_rowhead")):
                    sp.dma_start(dst, k.w[src]).then_inc(e["const"], 16)
                sp.dma_start(rowr[BH:BH + 1, :], k.w["c_ones"]).then_inc(e["const"], 16)
                sp.wait_ge(e["pages"], 16)
                sp.sem_inc(e["turned"], 2 * J)
                sp.sem_inc(e["vl"], 16)
                sp.sem_inc(e["pv"], VSLOTS)
                sp.sem_inc(e["done"], 1)

                def load(b, g, which, ring, sems, free, value):
                    numbers = [sp.value_load(pages[0:1, bass.ds(b * PAGES + g * 4 + p, 1)], min_val=0, max_val=k.n_pool - 1)
                               for p in range(4)]
                    sp.wait_ge(free, value)
                    for p, page in enumerate(numbers):
                        sp.dma_start(ring[:, g % 2, p, :], cache[which][bass.ds(page, 1)].rearrange("o t n -> t (o n)")
                                     ).then_inc(sems[g % 2], 16)

                def rows(b):
                    sp.dma_start(rowr[0:BH, :], k.neg_decay[bass.ds(b * BH, BH), :]).then_inc(e["rows"], 16)
                    sp.dma_start(rowl[BH:BH + 1, :], k.new_decay[bass.ds(b, 1), :]).then_inc(e["rows"], 16)

                def keys(b, g):
                    load(b, g, "k", kp, kload, e["turned"], b * STEPS + (g + 1) * J)

                def values(b, g):
                    load(b, g, "v", vp, vload, e["vl"], b * HV + (g + 1) * 8)

                def new_values(b):
                    sp.dma_start(vn[:], k.out["v_sample"].rearrange("b q h d -> b q (h d)")[bass.ds(b, 1)]
                                 .rearrange("b q n -> (b q) n")).then_inc(e["vnew"], 16)

                keys(0, 0)
                rows(0)
                for g in range(1, G):
                    keys(0, g)
                with sp.Fori(0, NB - 1) as c:
                    for g in range(G):
                        keys(c + 1, g)
                        if g == 1:
                            sp.wait_ge(e["scored"], c + 1)
                            rows(c + 1)
                        values(c, g)
                        if g == 1:
                            sp.wait_ge(e["pv"], c * HV + VSLOTS)
                            new_values(c)
                for g in range(G):
                    values(NB - 1, g)
                    if g == 1:
                        sp.wait_ge(e["pv"], (NB - 1) * HV + VSLOTS)
                        new_values(NB - 1)

            @block.tensor
            def _(pe):
                def turn(b, i):
                    g, j = divmod(i, J)
                    if j == 0:
                        pe.wait_ge(kload[g % 2], (b * 2 + g // 2 + 1) * 64)
                    if i >= 2:
                        pe.wait_ge(e["kl"], b * STEPS + i - 1)
                    for p in range(4):
                        mm = pe.transpose(ps[:, 4 + i % 2, p * P:(p + 1) * P], kp[:, g % 2, p, j * P:(j + 1) * P], k.ident[:])
                    mm.then_inc(e["turned"], 1)

                def score(b, c, i):
                    g, j = divmod(i, J)
                    pe.wait_ge(e["kl"], b * STEPS + i + 1)
                    if i == 0:
                        pe.wait_ge(e["ql"], b + 1)
                    if j == 0 and c is not None:
                        pe.wait_ge(e["pl"], c * G + g + 1)
                    for n, (qt, kt) in enumerate(((qh, kh), (ql, kh), (qh, kl))):
                        mm = pe.matmul(ps[:, g, :], qt[:, j, :], kt[:, i % KSLOTS, :], start=j == 0 and n == 0, stop=False)
                    if j == J - 1:
                        if g == 0:
                            pe.wait_ge(e["rows"], b * 32 + 32)
                        mm = pe.matmul(ps[:, g, :], rowl[:], rowr[:, g * SEQ:(g + 1) * SEQ], start=False, stop=True)
                    mm.then_inc(e["used"], 1)

                def new_scores(b):
                    pe.matmul(ps[:, 4, 0:NQ], rowl[:], rowr[:, PAST:PAST + NQ], start=True, stop=False)
                    pe.matmul(ps[:, 4, 0:NQ], k.ident[:], scausal[:], start=False, stop=False)
                    for j in range(J):
                        mm = pe.matmul(ps[:, 4, 0:NQ], qz[:, j * P:(j + 1) * P], ks[:, j, bass.ds(b * NQ, NQ)],
                                       start=False, stop=j == J - 1)
                    mm.then_inc(e["scored"], 1)

                def mix(c, h):
                    p, a = divmod(h, 2)
                    pe.wait_ge(e["vl"], c * HV + h + 17)
                    if h == 0:
                        pe.wait_ge(e["done"], c + 1)
                    if h % 8 == 0:
                        pe.wait_ge(e["pl"], c * G + h // 8 + 1)
                    for n, (pp, vv) in enumerate(((ph, vh), (pl, vh), (ph, vl))):
                        mm = pe.matmul(ps[:, 6 + a, :], pp[:, p, :], vv[:, h % VSLOTS, :], start=h < 2 and n == 0, stop=False)
                    if p == PAGES - 1:
                        pe.wait_ge(e["tail"], c + 1)
                        pe.wait_ge(e["vnew"], c * 16 + 16)
                        mm = pe.matmul(ps[:, 6 + a, :], ptt[:], vn[:, a * SEQ:(a + 1) * SEQ], start=False, stop=True)
                    mm.then_inc(e["pv"], 1)

                def turn_probabilities(b):
                    for g in range(G):
                        pe.wait_ge(e["exp"], b * (G + 1) + g + 2)
                        for p in range(4):
                            mm = pe.transpose(ps[:, g, p * P:(p + 1) * P], pr[:, (4 * g + p) * P:(4 * g + p + 1) * P], k.ident[:])
                        mm.then_inc(e["pturned"], 1)
                    pe.transpose(ps[0:NQ, 5, 0:P], ptail[:], k.ident[:]).then_inc(e["tailt"], 1)

                def pick(c):
                    pe.wait_ge(e["om"], c + 1)
                    for j in range(J):
                        mm = pe.matmul(ps[:, 6, j * NQ:(j + 1) * NQ], om[:, j * P:(j + 1) * P], pickq[:], start=True, stop=True)
                    mm.then_inc(e["picked"], 1)

                def body(b, c):
                    for i in range(STEPS + 2):
                        if i < STEPS:
                            if i == 1 and c is not None:
                                pe.wait_ge(e["tail"], c + 1)
                            turn(b, i)
                        if i >= 2:
                            score(b, c, i - 2)
                        if c is not None:
                            for h in step_units(i, 0):
                                mix(c, h)
                    new_scores(b)
                    if c is not None:
                        for h in last_units(0):
                            mix(c, h)
                    turn_probabilities(b)
                    if c is not None:
                        pick(c)

                pe.wait_ge(e["const"], 80)
                body(0, None)
                with pe.Fori(0, NB - 1) as c:
                    body(c + 1, c)
                for h in range(HV):
                    mix(NB - 1, h)
                pick(NB - 1)

            @block.scalar
            def _(act):
                def key_high(b, c, i):
                    act.wait_ge(e["turned"], b * STEPS + 2 * J + i + 1)
                    if i >= KSLOTS:
                        act.wait_ge(e["used"], b * STEPS + i - KSLOTS + 1)
                    act.activation(kh[:, i % KSLOTS, :], ps[:, 4 + i % 2, :], ACT.Copy).then_inc(e["kh"], 1)

                def value_high(c, h):
                    if h % 8 == 0:
                        act.wait_ge(vload[(h // 8) % 2], (c * 2 + h // 16 + 1) * 64)
                    act.wait_ge(e["pv"], c * HV + h + 1)
                    act.activation(vh[:, h % VSLOTS, :], vp[:, (h // 8) % 2, h // 2 % 4, (h % 2) * SEQ:(h % 2 + 1) * SEQ],
                                   ACT.Copy).then_inc(e["vh"], 1)

                def query_high(b):
                    act.wait_ge(e["q"], b * 2 + 2)
                    act.activation(qh[:].rearrange("p j n -> p (j n)"), qz[:], ACT.Copy).then_inc(e["qh"], 1)

                def body(b, c):
                    for i in range(STEPS + 2):
                        if i < STEPS:
                            key_high(b, c, i)
                        if c is not None:
                            for h in step_units(i, LEAD):
                                value_high(c, h)
                    late = list(last_units(LEAD)) if c is not None else []
                    for h in late[:2]:
                        value_high(c, h)
                    act.wait_ge(e["max"], b + 1)
                    act.activation(ptail[:], ps[:, 4, 0:NQ], ACT.Exp, bias=nm[:, 0:1], accum_out=tot[:, G:G + 1]).then_inc(e["exp"], 1)
                    for g in range(G):
                        act.activation(pr[:, g * SEQ:(g + 1) * SEQ], ps[:, g, :], ACT.Exp, bias=nm[:, 0:1],
                                       accum_out=tot[:, g:g + 1]).then_inc(e["exp"], 1)
                        if g == 0:
                            for h in late[2:]:
                                value_high(c, h)
                    query_high(b + 1)
                    if c is not None:
                        act.wait_ge(e["pv"], c * HV + HV + VSLOTS)
                    for g in range(G):
                        act.wait_ge(e["pturned"], b * G + g + 1)
                        act.activation(ph[:, 4 * g:4 * g + 4, :].rearrange("p a n -> p (a n)"), ps[:, g, :], ACT.Copy
                                       ).then_inc(e["ph"], 1)

                query_high(0)
                body(0, None)
                with act.Fori(0, NB - 1) as c:
                    body(c + 1, c)
                for h in range(HV):
                    value_high(NB - 1, h)

            @block.vector
            def _(dve):
                def key_low(b, i):
                    dve.wait_ge(e["kh"], b * STEPS + i + 1)
                    dve.tensor_tensor(kl[:, i % KSLOTS, :], ps[:, 4 + i % 2, :], kh[:, i % KSLOTS, :].bitcast(F32),
                                      ALU.subtract).then_inc(e["kl"], 1)

                def value_low(c, h):
                    dve.wait_ge(e["vh"], c * HV + h + 1)
                    dve.tensor_tensor(vl[:, h % VSLOTS, :], vp[:, (h // 8) % 2, h // 2 % 4, (h % 2) * SEQ:(h % 2 + 1) * SEQ],
                                      vh[:, h % VSLOTS, :].bitcast(F32), ALU.subtract).then_inc(e["vl"], 1)

                def group_max(b, g):
                    dve.wait_ge(e["used"], b * STEPS + (g + 1) * J)
                    dve.tensor_reduce(mx[:, g:g + 1], ps[:, g, :], AX.X, ALU.max).then_inc(e["mx"], 1)

                def queries(b):
                    for a in range(2):
                        r = slice(DH * a, DH * (a + 1))
                        dst = blocks(qz[r, :], J, 2 * NQ, a * NQ, NQ)
                        dve.tensor_copy(dst, qs[r, :, bass.ds(b * NQ, NQ)]).then_inc(e["q"], 1)

                def query_low(b):
                    dve.wait_ge(e["qh"], b + 1)
                    dve.tensor_tensor(ql[:].rearrange("p j n -> p (j n)"), qz[:],
                                      qh[:].rearrange("p j n -> p (j n)").bitcast(F32), ALU.subtract).then_inc(e["ql"], 1)

                def outputs(c):
                    dve.wait_ge(e["inv"], c + 1)
                    dve.wait_ge(e["pv"], c * HV + HV + VSLOTS)
                    dve.scalar_tensor_tensor(om[:], ps[:, 6:8, :].rearrange("p a n -> p (a n)"), inv[:, 1:2], rowhead[:],
                                             ALU.mult, ALU.mult).then_inc(e["om"], 1)

                def finish(c):
                    dve.wait_ge(e["picked"], c + 1)
                    dve.tensor_copy(oT[:].rearrange("p (j n) -> p j n", j=J)[:, :, bass.ds(c * NQ + SEQ, NQ)],
                                    ps[:, 6, 0:J * NQ].rearrange("p (j n) -> p j n", j=J)).then_inc(e["done"], 1)

                def body(b, c):
                    for i in range(STEPS + 2):
                        if i < STEPS:
                            key_low(b, i)
                        if i > J + 2 and (i - 3) % J == 0:
                            group_max(b, (i - 3) // J - 1)
                        if c is not None:
                            for h in step_units(i, LEAD):
                                value_low(c, h)
                    group_max(b, G - 1)
                    late = list(last_units(LEAD)) if c is not None else []
                    for h in late[:1]:
                        value_low(c, h)
                    dve.wait_ge(e["scored"], b + 1)
                    dve.tensor_reduce(mx[:, G:G + 1], ps[:, 4, 0:NQ], AX.X, ALU.max).then_inc(e["mx"], 1)
                    dve.wait_ge(e["mx"], (G + 1) * b + G + 1)
                    dve.tensor_reduce(nm[:], mx[:], AX.X, ALU.max, negate=True).then_inc(e["max"], 1)
                    for h in late[1:]:
                        value_low(c, h)
                    queries(b + 1)
                    if c is not None:
                        outputs(c)
                    query_low(b + 1)
                    for g in range(G):
                        dve.wait_ge(e["ph"], b * G + g + 1)
                        dve.tensor_tensor(pl[:, 4 * g:4 * g + 4, :].rearrange("p a n -> p (a n)"), ps[:, g, :],
                                          ph[:, 4 * g:4 * g + 4, :].rearrange("p a n -> p (a n)").bitcast(F32),
                                          ALU.subtract).then_inc(e["pl"], 1)
                    dve.wait_ge(e["tailt"], b + 1)
                    dve.tensor_copy(ptt[:], ps[0:NQ, 5, 0:P]).then_inc(e["tail"], 1)
                    dve.wait_ge(e["exp"], (G + 1) * b + G + 1)
                    dve.tensor_reduce(inv[:, 0:1], tot[:], AX.X, ALU.add).then_inc(e["sum"], 1)
                    dve.wait_ge(e["sum"], b + 1)
                    dve.reciprocal(inv[:, 1:2], inv[:, 0:1]).then_inc(e["inv"], 1)
                    if c is not None:
                        finish(c)

                dve.memset(qz[:], 0.0).then_inc(e["zero"], 1)
                dve.wait_ge(e["zero"], 1)
                queries(0)
                query_low(0)
                body(0, None)
                with dve.Fori(0, NB - 1) as c:
                    body(c + 1, c)
                for h in range(HV):
                    value_low(NB - 1, h)
                outputs(NB - 1)
                finish(NB - 1)


def blocks(ap, count, step, first, n):
    pattern = [list(ap.ap[0]), [P + step, count], [1, n]]
    return bass.AP(ap.tensor, ap.offset + first, pattern)


def split_rows(k, oT):
    high, low = k.sem("sr_high"), k.sem("sr_low")
    flat = [t[:].rearrange("p k n -> p (k n)") for t in (k.xh, k.xl)]
    with k.nc.Block() as block:
        @block.scalar
        def _(act):
            act.activation(flat[0], oT[:], ACT.Copy).then_inc(high, 1)

        @block.vector
        def _(dve):
            dve.wait_ge(high, 1)
            dve.tensor_tensor(flat[1], oT[:], flat[0].bitcast(F32), ALU.subtract).then_inc(low, 1)


def with_split(k, name):
    st = ExitStack()
    k.xh, k.xl = k.sb(st, name + "_xh", [P, KD, T], F32R), k.sb(st, name + "_xl", [P, KD, T], F32R)
    return st


def fox(k, gains):
    nc = k.nc
    with ExitStack() as so, ExitStack() as so_past:
        oT = k.sb(so, "oT", [P, KD * T])
        ks = k.sb(so, "k_new", [P, KD, NS])
        qs = k.sb(so, "q_new", [P, KD, NS + NQ])
        pages = k.sb(so_past, "past_pages", [1, NB * PAGES], I32)
        past_logf = k.sb(so_past, "past_logf", [P, PAGES, NB * BH])
        with ExitStack() as st:
            kv, q = k.sb(st, "kv", [P, 2 * KD * T]), k.sb(st, "qf", [P, KD * T])
            with with_split(k, "kvx"):
                norm(k, "kvn", gains["kv_norm"])
                dense(k, "kvf", k.w["w_kvf"], KD, 1, k.xh, k.xl, KD, lambda i, u: (i * 2 + u) * P, store_to(kv[:]))
                forget_values(k, k.xh, k.xl)
                norm(k, "bn", gains["b_norm"])
                dense(k, "wq", k.w["b_wq"][0], KD, 1, k.xh, k.xl, KD // 2, lambda i, u: (i * 2 + u) * P, store_to(q[:]))
            vrows = k.sb(st, "v_rows", [P, 5, D])
            head_rows(k, "vr", kv, KD, rows=vrows)
            store_rows(k, "v", vrows)
            with ExitStack() as kr:
                krows = k.sb(kr, "k_rows", [P, 5, D])
                head_rows(k, "kr", kv, 0, gain=k.kn[:, 0:1], rows=krows)
                store_rows(k, "k", krows)
            k.retire()
            head_rows(k, "qr", q, 0, gain=k.qn8[:, 0:1])
            past_sems = {n: k.sem("past_" + n) for n in ("pages", "gathered")}
            prompt_attention(k, kv, q, vrows, oT, pages, past_logf, past_sems)
            copied = k.sem("new_copied")
            with nc.Block() as block:
                @block.vector
                def _(dve):
                    dve.tensor_copy(ks[:], kv[:, 0:KD * T].rearrange("p (j n) -> p j n", j=KD)[:, :, SEQ:T]).then_inc(copied, 1)
                    dve.memset(qs[:, :, NS:NS + NQ], 0.0).then_inc(copied, 1)
                    dve.tensor_copy(qs[:, :, 0:NS], q[:].rearrange("p (j n) -> p j n", j=KD)[:, :, SEQ:T]).then_inc(copied, 1)
        past_decay(k, past_logf, past_sems)
        so_past.close()
        sample_attention(k, ks, qs, oT)
        k.retire()
        with with_split(k, "ox"):
            split_rows(k, oT)
            dense(k, "wo", k.w["b_wo"][0], KD, 1, k.xh, k.xl, KD // 2, lambda i, u: (i * 2 + u) * P, add_to_stream(k))


def store_rows(k, which, rows):
    done = k.sem(which + "_stored")
    with k.nc.Block() as block:
        @block.sync
        def _(sp):
            sp.dma_start(k.out[which + "_prompt"].rearrange("b (c p) h d -> p (b c) (h d)", p=P), rows[:, 0:4, :]).then_inc(done, 16)
            sp.dma_start(k.out[which + "_sample"].rearrange("b q h d -> (b q) (h d)"), rows[0:NS, 4, :]).then_inc(done, 16)
            sp.wait_ge(done, 32)


def store_y(k):
    nc = k.nc
    turned, copied, stored = (k.sem("y_" + n) for n in ("turned", "copied", "stored"))
    with ExitStack() as st:
        rows = k.sb(st, "y_rows", [P, 5, D])
        with nc.Block() as block:
            @block.tensor
            def _(pe):
                for f in range(KD):
                    b = 2 * (f % 2)
                    if f >= 2:
                        pe.wait_ge(copied, f - 1)
                    for c in range(4):
                        pe.transpose(k.ps[:, b, c * P:(c + 1) * P], k.xT[:, f, c * P:(c + 1) * P], k.ident[:])
                    pe.transpose(k.ps[0:NS, b + 1, 0:P], k.xT[:, f, SEQ:T], k.ident[:]).then_inc(turned, 1)

            @block.vector
            def _(dve):
                for f in range(KD):
                    b = 2 * (f % 2)
                    dve.wait_ge(turned, f + 1)
                    dve.tensor_copy(rows[:, 0:4, f * P:(f + 1) * P], k.ps[:, b, :].rearrange("p (c n) -> p c n", c=4))
                    dve.tensor_copy(rows[0:NS, 4, f * P:(f + 1) * P], k.ps[0:NS, b + 1, 0:P]).then_inc(copied, 1)

            @block.sync
            def _(sp):
                sp.wait_ge(copied, KD)
                sp.dma_start(k.out["y_prompt"].rearrange("b (c p) d -> p (b c) d", p=P), rows[:, 0:4, :]).then_inc(stored, 16)
                sp.dma_start(k.out["y_sample"].rearrange("b q d -> (b q) d"), rows[0:NS, 4, :]).then_inc(stored, 16)
                sp.wait_ge(stored, 32)


OUTS = [("y_prompt", (1, SEQ, D)), ("y_sample", (NB, NQ, D)), ("hgrn_prompt", (1, 1, H, P, P)),
        ("k_prompt", (1, SEQ, BH, DH)), ("v_prompt", (1, SEQ, BH, DH)), ("logf_prompt", (1, SEQ, BH)),
        ("hgrn_sample", (1, NB, H, P, P)), ("k_sample", (NB, NQ, BH, DH)), ("v_sample", (NB, NQ, BH, DH)),
        ("logf_sample", (NB, NQ, BH))]


def ffn(k, name, layer, gain):
    with ExitStack() as st:
        st.enter_context(with_split(k, name))
        norm(k, name + "n", gain)
        fh, fl = (k.sb(st, name + n, [P, KF, T], F32R) for n in ("_fh", "_fl"))
        dense(k, name + "gu", k.w["w_gate_up"][layer], KD, 1, k.xh, k.xl, KF, lambda i, u: i * P + u * FF, None,
              swiglu=(fh[:].rearrange("p k n -> p (k n)"), fl[:].rearrange("p k n -> p (k n)")))
        dense(k, name + "dn", k.w["w_down"][layer], KF // 2, 2, fh, fl, KD // 2, lambda i, u: (i * 2 + u) * P,
              add_to_stream(k))


def add_to_stream(k):
    flat = k.xT[:].rearrange("p k n -> p (k n)")

    def evacuate(dve, i, u, ps):
        x = halves(flat[:, bass.ds((i * 2 + u) * T, T)])
        return dve.tensor_tensor(x, x, ps, ALU.add)
    return evacuate


def store_to(flat, first=0):
    def evacuate(dve, i, u, ps):
        return dve.tensor_copy(halves(flat[:, bass.ds((i * 2 + u + first) * T, T)]), ps)
    return evacuate


def program(nc, a, outs, stop_after=99):
    with ExitStack() as stack:
        k = Core(nc, stack)
        k.w, k.out = a, outs
        k.x_prompt, k.x_sample, k.state_hgrn = a["x_prompt"], a["x_sample"], a["state_hgrn"]
        sb = lambda name, shape, dt=F32: k.sb(stack, name, shape, dt)
        k.ps = stack.enter_context(nc.psum_tensor("ps", [P, 8, 512], F32))
        k.xT = sb("xT", [P, KD, T])
        k.ident, k.mean, k.headmean = sb("ident", [P, P]), sb("mean", [P, P]), sb("headmean", [P, P])
        k.eps = sb("eps", [P, 1])
        k.lb, k.a_lb = sb("lb", [P, KD, 2]), sb("a_lbT", [P, KD])
        k.dlast = sb("dlast", [P, NB])
        k.n_pool = a["cache_k"].shape[0]
        k.cum_prompt = nc.dram_tensor("cum_prompt", [2, BH, SEQ], F32).ap()
        k.neg_decay = nc.dram_tensor("neg_decay", [NB * BH, PAST + NQ], F32).ap()
        k.new_decay = nc.dram_tensor("new_decay", [NB, BH * NQ], F32).ap()
        k.qn8 = sb("qn8", [P, 1])
        gains = {n: sb("g_" + n, [P, KD]) for n in ("a_norm", "kv_norm", "b_norm", "ffn0", "ffn1")}
        k.onorm, k.qn, k.kn = sb("onorm", [P, 1]), sb("qn", [P, 1]), sb("kn", [P, 1])
        k.const_loads = [(k.ident[:], a["c_ident"]), (k.mean[:], a["c_mean"]), (k.headmean[:], a["c_headmean"]),
                         (k.eps[:], a["c_eps"]),
                         (k.a_lb[:], a["a_lb"][0].rearrange("(k p) -> p k", p=P)),
                         (gains["a_norm"][:], a["a_norm"][0].rearrange("(k p) -> p k", p=P)),
                         (gains["kv_norm"][:], a["kv_norm"].rearrange("(k p) -> p k", p=P)),
                         (gains["b_norm"][:], a["b_norm"][0].rearrange("(k p) -> p k", p=P)),
                         (gains["ffn0"][:], a["ffn_norm"][0].rearrange("(k p) -> p k", p=P)),
                         (gains["ffn1"][:], a["ffn_norm"][1].rearrange("(k p) -> p k", p=P)),
                         (k.onorm[:], a["a_onorm"][0].rearrange("(p o) -> p o", o=1))]
        for half in range(2):
            k.const_loads += [(k.qn[half * DH:(half + 1) * DH, :], a["q_norm"][0].rearrange("(p o) -> p o", o=1)),
                              (k.kn[half * DH:(half + 1) * DH, :], a["k_norm"].rearrange("(p o) -> p o", o=1))]
        load_inputs(k)
        if stop_after < 1:
            return
        lower_bound(k)
        with with_split(k, "hx"), ExitStack() as hg:
            norm(k, "an", gains["a_norm"])
            k.z = k.sb(hg, "z", [P, 4 * H, T])
            if stop_after != 1.5:
                dense(k, "win", a["a_w_in"][0], KD, 1, k.xh, k.xl, 2 * H, lambda i, u: (i * 2 + u) * P,
                      store_to(k.z[:].rearrange("p k n -> p (k n)")))
            if stop_after < 2:
                return
            hgrn_constants(k, hg)
            hgrn(k)
            if stop_after < 3:
                return
            hg.close()
            dense(k, "wout", a["a_w_out"][0], KD, 1, k.xh, k.xl, KD // 2, lambda i, u: (i * 2 + u) * P, add_to_stream(k))
        k.retire()
        ffn(k, "f0", 0, gains["ffn0"])
        if stop_after < 4:
            return
        k.retire()
        fox(k, gains)
        ffn(k, "f1", 1, gains["ffn1"])
        store_y(k)


def hgrn_constants(k, st):
    nc = k.nc
    k.decay = k.sb(st, "decay", [P, (LEVELS + 2) * P], F32R)
    k.sdecay = k.sb(st, "sdecay", [NS, (SLEVELS + 2) * NS], F32R)
    k.split = k.sb(st, "split", [P, (LEVELS + 1) * P])
    k.ssplit = k.sb(st, "ssplit", [NS, (SLEVELS + 1) * NS])
    k.batch = k.sb(st, "batch", [NS, NB * P])
    got, done = k.sem("hc_loaded"), k.sem("hc_done")
    with ExitStack() as tmp:
        raw = k.sb(tmp, "decay_raw", [P, (LEVELS + 2) * P])
        sraw = k.sb(tmp, "sdecay_raw", [NS, (SLEVELS + 2) * NS])
        with nc.Block() as block:
            @block.sync
            def _(sp):
                for dst, src in ((raw, "c_decay"), (sraw, "c_sdecay"), (k.split, "c_split"), (k.ssplit, "c_ssplit"),
                                 (k.batch, "c_batch")):
                    sp.dma_start(dst[:], k.w[src]).then_inc(got, 16)
                sp.wait_ge(got, 80)

            @block.vector
            def _(dve):
                dve.wait_ge(got, 80)
                dve.tensor_copy(k.decay[:], raw[:]).then_inc(done, 1)
                dve.tensor_copy(k.sdecay[:], sraw[:]).then_inc(done, 1)


_INS = ["x_prompt", "x_sample", "state_hgrn", "cache_k", "cache_v", "cache_logf", "page_table", "a_norm", "a_w_in", "a_lb",
        "a_onorm", "a_w_out", "kv_norm", "w_kvf", "b_f", "k_norm", "b_norm", "b_wq", "q_norm", "b_wo", "ffn_norm",
        "w_gate_up", "w_down"]


def kernel(**inputs):
    from concourse import bacc
    from concourse.bass_utils import run_bass_kernel_spmd

    nc = bacc.Bacc("TRN2", target_bir_lowering=False, num_devices=1)
    arrays = {n: np.ascontiguousarray(inputs[n]) for n in _INS}
    arrays.update(shape_constants())
    arrays["c_eps"] = np.full((P, 1), EPS, np.float32)
    aps = {n: nc.dram_tensor("in_" + n, v.shape, mybir.dt.from_np(v.dtype), kind="ExternalInput").ap()
           for n, v in arrays.items()}
    outs = {n: nc.dram_tensor("out_" + n, s, F32, kind="ExternalOutput").ap() for n, s in OUTS}
    program(nc, aps, outs)
    r = run_bass_kernel_spmd(nc, [{"in_" + n: v for n, v in arrays.items()}], core_ids=[0])
    return tuple(r.results[0]["out_" + n] for n, _ in OUTS)
```

```python
from contextlib import ExitStack

import numpy as np

import concourse.bass as bass
from concourse import mybir

F32 = mybir.dt.float32
F32R = mybir.dt.float32r
I32 = mybir.dt.int32
ACT = mybir.ActivationFunctionType
ALU = mybir.AluOpType
AX = mybir.AxisListType

P = 128
D = 1024
KD = D // P
SEQ = 512
NB, NQ = 8, 8
NS = NB * NQ
T = SEQ + NS
HALF = T // 2
H = 8
BH, DH = 16, 64
FF = 2816
KF = FF // P
PAGES, PAGE = 16, 128
PAST = PAGES * PAGE
EPS = 1e-6
MIN_F = 1e-30
MASK = -1e30
LEVELS = 7
SLEVELS = 3
LN_LIFT = 50


def decay_sums(n, levels, chunk):
    i, t = np.arange(n)[:, None], np.arange(n)[None, :]
    out = []
    for l in range(levels):
        mid = ((t >> (l + 1)) << (l + 1)) + (1 << l)
        late = (t >> l) & 1
        out.append(np.where(late == 1, (i >= mid) & (i <= t), (i > t) & (i < mid)))
    same = i // chunk == t // chunk
    out.append(same & (i <= t))
    out.append(same & (i > t))
    return np.stack(out, axis=1).astype(np.float32)


def split_masks(n, levels):
    s, t = np.arange(n)[:, None], np.arange(n)[None, :]
    out = [(s >> (l + 1) == t >> (l + 1)) & ((s >> l) & 1 == 0) & ((t >> l) & 1 == 1) for l in range(levels)]
    out.append(s == t)
    return np.stack(out, axis=1).astype(np.float32)


def shape_constants():
    i = np.arange(P)
    hq = i[:, None]
    c = {
        "c_ident": np.eye(P),
        "c_ones": np.ones((2, PAST + NQ)),
        "c_mean": np.full((P, P), 1.0 / P),
        "c_headmean": (i[:, None] // DH == i[None, :] // DH) / DH,
        "c_decay": decay_sums(P, LEVELS, P).reshape(P, -1),
        "c_sdecay": decay_sums(NS, SLEVELS, NQ).reshape(NS, -1),
        "c_tri": (i[:, None] <= i[None, :]),
        "c_causal": np.where(i[None, :] <= i[:, None], 0.0, MASK),
        "c_scausal": np.where(np.arange(NQ)[None, :] <= hq % NQ, 0.0, MASK),
        "c_headrow": (np.arange(BH)[:, None] == i[None, :] // NQ),
        "c_pickq": (hq % NQ == np.arange(NQ)[None, :]),
        "c_rowhead": np.repeat(hq // NQ == np.arange(BH)[None, :], DH, axis=1),
        "c_batch": np.repeat(np.arange(NS)[:, None] // NQ == np.arange(NB)[None, :], P, axis=1),
        "c_newtri": ((i[:NS, None] // NQ == i[None, :NS] // NQ) & (i[:NS, None] <= i[None, :NS])),
    }
    c = {k: np.ascontiguousarray(v, dtype=np.float32) for k, v in c.items()}
    c["c_split"] = split_masks(P, LEVELS).reshape(P, -1)
    c["c_ssplit"] = split_masks(NS, SLEVELS).reshape(NS, -1)
    return c


class Core:

    def __init__(self, nc, stack):
        self.nc, self.stack, self.open = nc, stack, []

    def sb(self, stack, name, shape, dt=F32):
        return stack.enter_context(self.nc.sbuf_tensor(name, shape, dt))

    def sem(self, name):
        self.open.append(self.nc.alloc_semaphore(name=name))
        return self.open[-1]

    def retire(self):
        self.nc.clear_and_free_semaphores(self.open)
        self.nc.all_engine_barrier()
        self.open = []


def halves(ap):
    return ap.rearrange("p (a n) -> p a n", a=2)


def load_inputs(k):
    nc, x = k.nc, k.xT
    with ExitStack() as st:
        rows = k.sb(st, "x_rows", [P, 5, D])
        loaded, xrows, turned, stored = (k.sem(n) for n in ("consts_loaded", "x_loaded", "x_turned", "x_stored"))
        n_const = len(k.const_loads)
        with nc.Block() as block:
            @block.sync
            def _(sp):
                sp.dma_start(rows[:, 0:4, :], k.x_prompt.rearrange("b (c p) d -> p (b c) d", p=P)).then_inc(xrows, 16)
                sp.dma_start(rows[0:NS, 4, :], k.x_sample.rearrange("b q d -> (b q) d")).then_inc(xrows, 16)
                for dst, src in k.const_loads:
                    sp.dma_start(dst, src, allow_slow_non_contiguous=True).then_inc(loaded, 16)
                sp.wait_ge(loaded, 16 * n_const)

            @block.tensor
            def _(pe):
                pe.wait_ge(loaded, 16 * n_const)
                pe.wait_ge(xrows, 32)
                for f in range(KD):
                    if f >= 2:
                        pe.wait_ge(stored, f - 1)
                    for c in range(4):
                        nc.tensor.transpose(k.ps[:, 2 * (f % 2), c * P:(c + 1) * P], rows[:, c, f * P:(f + 1) * P], k.ident[:])
                    nc.tensor.transpose(k.ps[:, 2 * (f % 2) + 1, 0:NS], rows[0:NS, 4, f * P:(f + 1) * P],
                                        k.ident[0:NS, 0:NS]).then_inc(turned, 1)

            @block.vector
            def _(dve):
                for f in range(KD):
                    dve.wait_ge(turned, f + 1)
                    nc.vector.tensor_copy(x[:, f, 0:SEQ], k.ps[:, 2 * (f % 2), :])
                    nc.vector.tensor_copy(x[:, f, SEQ:T], k.ps[:, 2 * (f % 2) + 1, 0:NS]).then_inc(stored, 1)


class Norm:

    def __init__(self, k, name, gain, st, rstd=None):
        self.k, self.gain, self.known = k, gain, rstd is not None and rstd[1]
        self.sq, self.y = (k.sb(st, name + n, [P, 2, T]) for n in ("_sq", "_y"))
        self.rstd = rstd[0] if rstd is not None else k.sb(st, name + "_rstd", [P, T])
        self.squared, self.summed, self.logged, self.scaled, self.normed, self.high, self.low = (
            k.sem(name + s) for s in ("_squared", "_summed", "_logged", "_scaled", "_normed", "_high", "_low"))

    def scalar_first(self, act):
        k, sq = self.k, self.sq
        for f in range(0 if self.known else KD):
            if f >= 2:
                act.wait_ge(self.summed, f - 1)
            act.activation(sq[:, f % 2, :], k.xT[:, f, :], ACT.Square).then_inc(self.squared, 1)

    def scalar_second(self, act):
        k, rstd, y = self.k, self.rstd, self.y
        if not self.known:
            act.wait_ge(self.summed, KD)
            act.activation(halves(rstd[:]), k.ps[:, 0:2, 0:HALF], ACT.Ln, scale=1.0 / KD, bias=k.eps[:, 0:1]
                           ).then_inc(self.logged, 1)
            act.wait_ge(self.logged, 1)
            act.activation(rstd[:], rstd[:], ACT.Exp, scale=-0.5).then_inc(self.scaled, 1)
        for f in range(KD):
            act.wait_ge(self.normed, f + 1)
            act.activation(k.xh[:, f, :], y[:, f % 2, :], ACT.Copy).then_inc(self.high, 1)

    def gpsimd(self, pool):
        pass

    def tensor(self, pe):
        k, sq = self.k, self.sq
        for f in range(0 if self.known else KD):
            pe.wait_ge(self.squared, f + 1)
            for a in range(2):
                mm = pe.matmul(k.ps[:, a, 0:HALF], k.mean[:], sq[:, f % 2, a * HALF:(a + 1) * HALF],
                               start=f == 0, stop=f == KD - 1)
            mm.then_inc(self.summed, 1)

    def vector(self, dve):
        k, rstd, y = self.k, self.rstd, self.y

        def low(f):
            dve.wait_ge(self.high, f + 1)
            dve.tensor_tensor(k.xl[:, f, :], y[:, f % 2, :], k.xh[:, f, :].bitcast(F32), ALU.subtract).then_inc(self.low, 1)

        if not self.known:
            dve.wait_ge(self.scaled, 1)
        for f in range(KD):
            if f >= 2:
                dve.wait_ge(self.low, f - 1)
            dve.scalar_tensor_tensor(y[:, f % 2, :], k.xT[:, f, :], self.gain[:, f:f + 1], rstd[:],
                                     ALU.mult, ALU.mult).then_inc(self.normed, 1)
            if f >= 1:
                low(f - 1)
        low(KD - 1)


def dense(k, name, weight, kt, chunks, ah, al, pairs, col_of, evacuate, swiglu=None, gain=None, rstd=None, before=None):
    nc = k.nc
    w = weight.rearrange("(k p) n -> p k n", p=P)
    loaded = [k.sem(f"{name}_loaded{s}") for s in range(2)]
    free = [k.sem(f"{name}_free{u}") for u in range(2)]
    high, low, used, gated, mixed, parted = (
        k.sem(f"{name}_{s}") for s in ("high", "low", "used", "gated", "mixed", "parted"))
    units = 2 * chunks
    with ExitStack() as st:
        wraw = k.sb(st, name + "_wraw", [P, 2, kt, P])
        wh, wl = (k.sb(st, name + n, [P, 2, kt, P], F32R) for n in ("_wh", "_wl"))
        gate = k.sb(st, name + "_gate", [P, T]) if swiglu else None
        prod = k.sb(st, name + "_prod", [P, T]) if swiglu else None
        norm = Norm(k, name + "_n", gain, st, rstd) if gain is not None else before
        with nc.Block() as block:
            @block.sync
            def _(sp):
                sp.sem_inc(low, 2)
                with sp.Fori(0, pairs) as i:
                    for v in range(units):
                        u, c = divmod(v, chunks)
                        sp.wait_ge(low, i * units + v + 1)
                        sp.dma_start(wraw[:, v % 2, :, :], w[:, c * kt:(c + 1) * kt, bass.ds(col_of(i, u), P)]
                                     ).then_inc(loaded[v % 2], 16)

            @block.scalar
            def _(act):
                act.sem_inc(used, 2)
                if swiglu:
                    act.sem_inc(gated, 1)

                def split(i, v):
                    act.wait_ge(loaded[v % 2], (i * (units // 2) + v // 2) * 16 + 16)
                    act.wait_ge(used, i * units + v + 1)
                    act.activation(wh[:, v % 2, :, :], wraw[:, v % 2, :, :], ACT.Copy).then_inc(high, 1)

                def silu(i):
                    act.wait_ge(used, i * units + chunks + 2)
                    act.wait_ge(mixed, i + 1)
                    act.activation(halves(gate[:]), k.ps[:, 0:2, 0:HALF], ACT.Silu).then_inc(gated, 1)

                if norm:
                    norm.scalar_first(act)
                if not swiglu:
                    for v in range(units):
                        split(0, v)
                    if norm:
                        norm.scalar_second(act)
                    with act.Fori(0, pairs - 1) as i:
                        for v in range(units):
                            split(i + 1, v)
                else:
                    split(0, 0)
                    if norm:
                        norm.scalar_second(act)
                    with act.Fori(0, pairs - 1) as i:
                        split(i, 1)
                        split(i + 1, 0)
                        silu(i)
                    split(pairs - 1, 1)
                    silu(pairs - 1)

            @block.gpsimd
            def _(pool):
                if norm:
                    norm.gpsimd(pool)
                with pool.Fori(0, pairs) as i:
                    for v in range(units):
                        pool.wait_ge(high, i * units + v + 1)
                        pool.tensor_tensor(wl[:, v % 2, :, :], wraw[:, v % 2, :, :],
                                           wh[:, v % 2, :, :].bitcast(F32), ALU.subtract).then_inc(low, 1)

            @block.tensor
            def _(pe):
                if norm:
                    norm.tensor(pe)
                with pe.Fori(0, pairs) as i:
                    for v in range(units):
                        u, c = divmod(v, chunks)
                        if c == 0 and swiglu:
                            pe.wait_ge(gated if u == 0 else mixed, i + 1)
                        elif c == 0:
                            pe.wait_ge(free[u], i + 1)
                        pe.wait_ge(low, i * units + v + 3)
                        for t in range(kt):
                            if norm and u == 0:
                                pe.wait_ge(norm.low, t + 1)
                            for n, (wt, at) in enumerate(((wh, ah), (wh, al), (wl, ah))):
                                for a in range(2):
                                    mm = pe.matmul(k.ps[:, 2 * u + a, 0:HALF], wt[:, v % 2, t, :],
                                                   at[:, c * kt + t, a * HALF:(a + 1) * HALF],
                                                   start=c == 0 and t == 0 and n == 0,
                                                   stop=c == chunks - 1 and t == kt - 1 and n == 2)
                        mm.then_inc(used, 1)

            @block.vector
            def _(dve):
                if norm:
                    norm.vector(dve)
                if swiglu:
                    dve.sem_inc(mixed, 1)
                else:
                    dve.sem_inc(free[0], 1)
                    dve.sem_inc(free[1], 1)
                with dve.Fori(0, pairs) as i:
                    if not swiglu:
                        for u in range(2):
                            dve.wait_ge(used, i * units + (u + 1) * chunks + 2)
                            evacuate(dve, i, u, k.ps[:, 2 * u:2 * u + 2, 0:HALF]).then_inc(free[u], 1)
                    else:
                        dh, dl = swiglu
                        dve.wait_ge(gated, i + 2)
                        dve.wait_ge(used, i * units + units + 2)
                        dve.tensor_tensor(halves(prod[:]), halves(gate[:]), k.ps[:, 2:4, 0:HALF],
                                          ALU.mult).then_inc(mixed, 1)
                        dve.wait_ge(mixed, i + 2)
                        dve.tensor_copy(dh[:, bass.ds(i * T, T)], prod[:]).then_inc(parted, 1)
                        dve.wait_ge(parted, i * 2 + 1)
                        dve.tensor_tensor(dl[:, bass.ds(i * T, T)], prod[:], dh[:, bass.ds(i * T, T)].bitcast(F32),
                                          ALU.subtract).then_inc(parted, 1)
                        dve.wait_ge(parted, i * 2 + 2)


def hgrn_inputs(k, st):
    e = {n: k.sem("hi_" + n) for n in ("keys", "sigmoids", "scaled", "floored", "tiny", "lifted", "logged", "logf", "gates",
                                       "loaded", "decays")}
    k.decay = k.sb(st, "decay", [P, (LEVELS + 2) * P], F32R)
    k.sdecay = k.sb(st, "sdecay", [NS, (SLEVELS + 2) * NS], F32R)
    k.split = k.sb(st, "split", [P, (LEVELS + 1) * P])
    k.ssplit = k.sb(st, "ssplit", [NS, (SLEVELS + 1) * NS])
    k.batch = k.sb(st, "batch", [NS, NB * P])
    tmp = st.enter_context(ExitStack())
    raw = k.sb(tmp, "decay_raw", [P, (LEVELS + 2) * P])
    sraw = k.sb(tmp, "sdecay_raw", [NS, (SLEVELS + 2) * NS])
    zf = k.z[:].rearrange("p k n -> p (k n)")
    keys, tiny = k.keys[:], k.tiny[:]

    def cols(flat, head, part=0):
        return flat[:, (part * H + head) * T:(part * H + head + 1) * T]

    with k.nc.Block() as block:
        @block.sync
        def _(sp):
            for dst, src in ((raw, "c_decay"), (sraw, "c_sdecay"), (k.split, "c_split"), (k.ssplit, "c_ssplit"),
                             (k.batch, "c_batch")):
                sp.dma_start(dst[:], k.w[src]).then_inc(e["loaded"], 16)
            sp.wait_ge(e["loaded"], 80)

        @block.scalar
        def _(act):
            for h in range(H):
                act.activation(cols(keys, h), cols(zf, h, 1), ACT.Sigmoid, scale=-1.0).then_inc(e["keys"], 1)
                act.activation(cols(zf, h, 1), cols(zf, h, 1), ACT.Sigmoid).then_inc(e["sigmoids"], 1)
            act.activation(zf[:, 3 * H * T:4 * H * T], zf[:, 3 * H * T:4 * H * T], ACT.Silu).then_inc(e["gates"], 1)
            for h in range(H):
                act.wait_ge(e["lifted"], h + 1)
                act.activation(cols(zf, h, 1), cols(zf, h, 1), ACT.Ln).then_inc(e["logged"], 1)

        @block.gpsimd
        def _(pool):
            for h in range(H):
                pool.wait_ge(e["keys"], h + 1)
                pool.tensor_scalar(cols(keys, h), cols(keys, h), k.lb[:, h:h + 1, 1], None, ALU.mult).then_inc(e["scaled"], 1)

        @block.vector
        def _(dve):
            for h in range(H):
                f, t = cols(zf, h, 1), cols(tiny, h)
                lb, one_lb = (k.lb[:, h:h + 1, j] for j in range(2))
                dve.wait_ge(e["sigmoids"], h + 1)
                dve.tensor_scalar(f, f, one_lb, lb, ALU.mult, ALU.add).then_inc(e["floored"], 1)
                dve.wait_ge(e["floored"], h * 2 + 1)
                dve.tensor_scalar(f, f, MIN_F, None, ALU.max).then_inc(e["floored"], 1)
                dve.wait_ge(e["floored"], h * 2 + 2)
                dve.tensor_scalar(t, f, 2.0 ** -30, 2.0 ** LN_LIFT - 1.0, ALU.is_lt, ALU.mult).then_inc(e["tiny"], 1)
                dve.wait_ge(e["tiny"], h + 1)
                dve.scalar_tensor_tensor(f, t, 1.0, f, ALU.add, ALU.mult).then_inc(e["lifted"], 1)
            dve.wait_ge(e["loaded"], 80)
            dve.tensor_copy(k.decay[:], raw[:]).then_inc(e["decays"], 1)
            dve.tensor_copy(k.sdecay[:], sraw[:]).then_inc(e["decays"], 1)
            for h in range(H):
                f, t = cols(zf, h, 1), cols(tiny, h)
                dve.wait_ge(e["logged"], h + 1)
                dve.scalar_tensor_tensor(f, t, -LN_LIFT * float(np.log(2.0)) / (2.0 ** LN_LIFT - 1.0), f,
                                         ALU.mult, ALU.add).then_inc(e["logf"], 1)
    tmp.close()


def hgrn(k):
    nc, ps = k.nc, k.ps
    names = ("turned", "high", "low", "valued", "summed", "decayed", "queries", "keys", "last", "scored", "picked", "attended",
             "keyrows", "vmasked", "read", "copied", "state", "free", "stored", "zero", "staged0", "staged1", "pstored")
    e = {n: k.sem("hgrn_" + n) for n in names}
    staged = [e["staged0"], e["staged1"]]
    C = 5
    W = 2 * C
    N = H * C
    with ExitStack() as st:
        sb = lambda n, shape, dt=F32: k.sb(st, "hg_" + n, shape, dt)
        v = sb("v", [P, 2, T + NS])
        s0 = sb("s0", [P, 2, NB, P])
        kk, lf = sb("k", [P, 2, T]), sb("lf", [P, 2, T + NS])
        lth, ltl = sb("lth", [P, P], F32R), sb("ltl", [P, P], F32R)
        vt = sb("vt", [P, C, P])
        ex = sb("ex", [P, C, LEVELS, P])
        qd, kd = sb("qd", [P, C, P]), sb("kd", [P, C, P])
        last = sb("last", [P, C, NB])
        picked = sb("picked", [P, (LEVELS + 1) * P])
        att, kt = sb("att", [P, P]), sb("kt", [P, P])
        vm, snew = sb("vm", [NS, NB, P]), sb("snew", [P, NB, P])
        S = sb("S", [P, 2, P])
        zf = k.z[:].rearrange("p k n -> p (k n)")
        keys = k.keys[:]

        class Tile:

            def __init__(self, i, t):
                self.t = t
                self.done = i * W + (t + 1)
                self.pair = i + t // W
                self.c = t % C
                self.head = i * 2 + t // C
                self.hs = (t // C) % 2
                self.s = t % C
                self.sample = self.c == C - 1
                self.t0 = self.c * P
                self.n, self.levels = (NS, SLEVELS) if self.sample else (P, LEVELS)
                self.cols = slice(self.t0, self.t0 + self.n)

            def z(self, j):
                return zf[:, bass.ds((j * H + self.head) * T + self.t0, self.n)]

            def key_rows(self):
                return ps[:, 7, 2 * P:3 * P] if self.c == 0 else ps[:, 5, 0:P]

            def ex(self):
                return ex[:, self.s].rearrange("p l n -> p (l n)")[:, 0:self.levels * self.n].rearrange("p (l n) -> p l n", n=self.n)

            def scores(self):
                w = self.levels + 1
                if self.sample:
                    return ps[0:self.n, 3, 0:w * self.n].rearrange("p (l n) -> p l n", l=w)
                return ps[:, 3:5, :].rearrange("p a n -> p (a n)").rearrange("p (l n) -> p l n", l=w)

        def steps(eng, stage):
            ahead = {"advance": 0, "score": 1, "sum": 3, "turn": 4}

            for name, t in (("turn", 0), ("sum", 0), ("turn", 1), ("sum", 1), ("turn", 2), ("sum", 2), ("turn", 3), ("score", 0)):
                stage[name](Tile(0, t))

            def body(i, rest):
                for t in range(W):
                    for name in ahead:
                        if t + ahead[name] < rest:
                            stage[name](Tile(i, t + ahead[name]))

            with eng.Fori(0, H // 2 - 1) as i:
                body(i, W + 4)
            body(H // 2 - 1, W)

        none = lambda *a: None

        with nc.Block() as block:
            @block.sync
            def _(sp):
                def stage_head(i, s):
                    head = i * 2 + s
                    sp.dma_start(lf[:, s, 0:T], zf[:, bass.ds((H + head) * T, T)]).then_inc(staged[s], 16)
                    sp.dma_start(kk[:, s], keys[:, bass.ds(head * T, T)]).then_inc(staged[s], 16)
                    sp.dma_start(v[:, s, 0:T], zf[:, bass.ds((2 * H + head) * T, T)]).then_inc(staged[s], 16)
                    sp.dma_start(s0[:, s], k.state_hgrn[0].rearrange("b h d v -> h d b v")[bass.ds(head, 1)]
                                 .rearrange("h d b v -> (h d) b v")).then_inc(staged[s], 16)

                def put(i, s):
                    head = i * 2 + s
                    sp.wait_ge(e["state"], i * W + (C * s + 4))
                    sp.dma_start(k.out["hgrn_prompt"][0, 0][bass.ds(head, 1)].rearrange("h d v -> (h d) v"), S[:, s]
                                 ).then_inc(e["pstored"], 16)
                    sp.wait_ge(e["state"], i * W + (C * s + 5))
                    sp.dma_start(k.out["hgrn_sample"][0].rearrange("b h d v -> h d b v")[bass.ds(head, 1)]
                                 .rearrange("h d b v -> (h d) b v"), snew[:]).then_inc(e["stored"], 16)
                    sp.wait_ge(e["pstored"], head * 16 + 16)
                    sp.wait_ge(e["stored"], head * 16 + 16)
                    sp.sem_inc(e["free"], 1)

                sp.sem_inc(e["free"], 2)
                stage_head(0, 0)
                stage_head(0, 1)
                with sp.Fori(0, H // 2 - 1) as i:
                    for s in range(2):
                        put(i, s)
                        stage_head(i + 1, s)
                put(H // 2 - 1, 0)
                put(H // 2 - 1, 1)

            @block.tensor
            def _(pe):
                def turn(a):
                    if a.c == 0:
                        pe.wait_ge(staged[a.hs], a.pair * 64 + 64)
                    if a.t > 3 and a.c == 3:
                        pe.wait_ge(e["state"], a.done - 4)
                    pe.transpose(ps[:, 6, 0:P], lf[:, a.hs, a.t0:a.t0 + P], k.ident[:])
                    pe.transpose(ps[:, 6, P:2 * P], v[:, a.hs, a.t0:a.t0 + P], k.ident[:]).then_inc(e["turned"], 1)

                def sums(a):
                    decay = k.sdecay if a.sample else k.decay
                    n, w = a.n, a.levels * a.n
                    pe.wait_ge(e["low"], a.done)
                    pe.wait_ge(e["valued"], a.done)
                    if a.t > 0:
                        pe.wait_ge(e["decayed"], a.done - 1)
                    cuts = [(1, 0, w)] if a.sample else [(1, 0, 4 * P), (2, 4 * P, w)]
                    for bank, c0, c1 in cuts + [(0, w, w + 2 * n)]:
                        for n_, part in enumerate((lth, ltl)):
                            mm = pe.matmul(ps[:, bank, 0:c1 - c0], part[0:n, :], decay[0:n, c0:c1],
                                           start=n_ == 0, stop=n_ == 1)
                    mm.then_inc(e["summed"], 1)

                def score(a):
                    x, n = a.ex(), a.n
                    pe.wait_ge(e["keys"], a.done)
                    pe.wait_ge(e["queries"], a.done)
                    if a.t > 0:
                        pe.wait_ge(e["picked"], a.done - 1)
                        pe.wait_ge(e["keyrows"], a.done - 1)
                    if a.t > 0 and a.c == 0:
                        pe.wait_ge(e["copied"], a.done - 1)
                    if a.t > 0 and a.c == 1:
                        pe.wait_ge(e["state"], a.done - 2)
                    pe.transpose(a.key_rows(), kd[:, a.s, :], k.ident[:])
                    for l in range(a.levels):
                        pe.matmul(ps[0:n, 3 + l * n // 512, l * n % 512:l * n % 512 + n], x[:, l, :], x[:, l, :],
                                  start=True, stop=True)
                    at = a.levels * n
                    pe.matmul(ps[0:n, 3 + at // 512, at % 512:at % 512 + n], kk[:, a.hs, a.cols], a.z(0),
                              start=True, stop=True).then_inc(e["scored"], 1)

                def advance(a):
                    n, vv, qq = a.n, vt[:, a.c, :], qd[:, a.s, :]
                    pe.wait_ge(e["attended"], a.done)
                    pe.wait_ge(e["keyrows"], a.done)
                    if a.t > 0:
                        pe.wait_ge(e["state"], a.done - 1)
                        pe.wait_ge(e["copied"], a.done - 1)
                    if not a.sample:
                        pe.matmul(ps[:, 7, 0:P], vv, att[:], start=True, stop=a.c == 0)
                        if a.c > 0:
                            pe.matmul(ps[:, 7, 0:P], S[:, a.hs], qq, start=False, stop=True)
                        pe.matmul(ps[:, 7, P:2 * P], kt[:], vv, start=True, stop=True).then_inc(e["read"], 1)
                        return
                    pe.matmul(ps[:, 7, 0:NS], vv[0:NS], att[0:NS, 0:NS], start=True, stop=True)
                    for b in range(NB):
                        for r in (slice(0, 64), slice(64, P)):
                            pe.matmul(ps[r, 7, b * NQ:(b + 1) * NQ], s0[:, a.hs, b, r], qq[:, b * NQ:(b + 1) * NQ],
                                      start=False, stop=True, skip_group_check=True)
                    pe.wait_ge(e["vmasked"], a.head + 1)
                    rows = min(a.done + 3, N) if isinstance(a.done, int) else a.done + 3
                    pe.wait_ge(e["low"], rows)
                    for g in range(2):
                        mm = pe.matmul(ps[:, 5 + g, :], kt[0:NS, :], vm[:, 4 * g:4 * g + 4, :].rearrange("p b v -> p (b v)"),
                                       start=True, stop=True)
                    mm.then_inc(e["read"], 1)

                steps(pe, {"turn": turn, "sum": sums, "score": score, "advance": advance})

            @block.scalar
            def _(act):
                def turn(a):
                    act.wait_ge(e["turned"], a.done)
                    act.activation(lth[0:a.n, :], ps[0:a.n, 6, 0:P], ACT.Copy).then_inc(e["high"], 1)
                    act.activation(vt[0:a.n, a.c, :], ps[0:a.n, 6, P:2 * P], ACT.Copy).then_inc(e["valued"], 1)

                def sums(a):
                    n = a.n
                    act.wait_ge(e["summed"], a.done)
                    act.activation(a.ex(), ps[:, 1:3, :].rearrange("p a n -> p (a n)")[:, 0:a.levels * n]
                                   .rearrange("p (l n) -> p l n", n=n), ACT.Exp)
                    act.activation(qd[:, a.s, 0:n], ps[:, 0, 0:n], ACT.Exp)
                    act.activation(kd[:, a.s, 0:n], ps[:, 0, n:2 * n], ACT.Exp).then_inc(e["decayed"], 1)

                def score(a):
                    act.wait_ge(e["scored"], a.done)
                    act.activation(kt[0:a.n, :], a.key_rows()[0:a.n], ACT.Copy).then_inc(e["keyrows"], 1)

                def advance(a):
                    act.wait_ge(e["read"], a.done)
                    act.activation(a.z(0), ps[:, 7, 0:a.n], ACT.Copy).then_inc(e["copied"], 1)

                steps(act, {"turn": turn, "sum": sums, "score": score, "advance": advance})

            @block.gpsimd
            def _(pool):
                def sums(a):
                    x, keys = a.ex(), kk[:, a.hs, a.cols]
                    pool.wait_ge(e["decayed"], a.done)
                    for l in range(a.levels):
                        b = 1 << l
                        xv, kv = (r.rearrange("p (a r b) -> p a r b", r=2, b=b)[:, :, 0, :] for r in (x[:, l, :], keys))
                        pool.tensor_tensor(xv, xv, kv, ALU.mult)
                    dk = kd[:, a.s, 0:a.n]
                    pool.tensor_tensor(dk, dk, keys, ALU.mult).then_inc(e["keys"], 1)
                    if a.sample:
                        pool.wait_ge(e["valued"], a.done)
                        pool.wait_ge(e["free"], a.head + 2)
                        pool.tensor_tensor(vm[:], vt[0:NS, a.c, :].unsqueeze(1).broadcast_to([NS, NB, P]),
                                           k.batch[:].rearrange("p (b v) -> p b v", b=NB), ALU.mult).then_inc(e["vmasked"], 1)

                steps(pool, {"turn": none, "sum": sums, "score": none, "advance": none})

            @block.vector
            def _(dve):
                def turn(a):
                    dve.wait_ge(e["high"], a.done)
                    dve.wait_ge(e["valued"], a.done)
                    dve.tensor_tensor(ltl[0:a.n, :], ps[0:a.n, 6, 0:P], lth[0:a.n, :].bitcast(F32), ALU.subtract
                                      ).then_inc(e["low"], 1)

                def sums(a):
                    x, n, z = a.ex(), a.n, a.z(0)
                    dve.wait_ge(e["decayed"], a.done)
                    for l in range(a.levels):
                        b = 1 << l
                        xv, qv = (r.rearrange("p (a r b) -> p a r b", r=2, b=b)[:, :, 1, :] for r in (x[:, l, :], z))
                        dve.tensor_tensor(xv, xv, qv, ALU.mult)
                    lst = (last[:, a.s, 0:NB], qd[:, a.s, NQ - 1:n:NQ]) if a.sample else (last[:, a.s, 0:1], qd[:, a.s, n - 1:n])
                    dve.tensor_copy(*lst).then_inc(e["last"], 1)
                    dve.wait_ge(e["last"], a.done)
                    dve.tensor_tensor(qd[:, a.s, 0:n], qd[:, a.s, 0:n], z, ALU.mult).then_inc(e["queries"], 1)

                def score(a):
                    masks = (k.ssplit if a.sample else k.split)[:].rearrange("p (l n) -> p l n", n=a.n)
                    w = a.levels + 1
                    dve.wait_ge(e["scored"], a.done)
                    pairs = picked[0:a.n, 0:w * a.n].rearrange("p (l n) -> p l n", l=w)
                    dve.tensor_tensor(pairs, a.scores(), masks, ALU.mult).then_inc(e["picked"], 1)
                    dve.wait_ge(e["picked"], a.done)
                    dve.tensor_reduce(att[0:a.n, 0:a.n], pairs.rearrange("p l n -> p n l"), AX.X, ALU.add
                                      ).then_inc(e["attended"], 1)

                def advance(a):
                    dve.wait_ge(e["copied"], a.done)
                    if a.c == 0:
                        dve.wait_ge(e["free"], a.head + 1)
                        dve.tensor_copy(S[:, a.hs], ps[:, 7, P:2 * P]).then_inc(e["state"], 1)
                    elif not a.sample:
                        dve.scalar_tensor_tensor(S[:, a.hs], S[:, a.hs], last[:, a.s, 0:1], ps[:, 7, P:2 * P], ALU.mult,
                                                 ALU.add).then_inc(e["state"], 1)
                    else:
                        dve.wait_ge(e["free"], a.head + 2)
                        for b in range(NB):
                            ins = dve.scalar_tensor_tensor(
                                snew[:, b, :], s0[:, a.hs, b, :], last[:, a.s, b:b + 1],
                                ps[:, 5 + b // 4, (b % 4) * P:(b % 4 + 1) * P], ALU.mult, ALU.add)
                        ins.then_inc(e["state"], 1)
                    dve.wait_ge(e["state"], a.done)

                dve.memset(lf[:, 0, T:T + NS], 0.0).then_inc(e["zero"], 1)
                dve.memset(lf[:, 1, T:T + NS], 0.0).then_inc(e["zero"], 1)
                dve.memset(v[:, :, T:T + NS], 0.0).then_inc(e["zero"], 1)
                dve.memset(kd[:], 0.0).then_inc(e["zero"], 1)
                dve.wait_ge(e["zero"], 4)
                steps(dve, {"turn": turn, "sum": sums, "score": score, "advance": advance})


class HeadOutputs:

    def __init__(self, k):
        self.k = k
        self.squared, self.meant, self.logged, self.rstd, self.gain, self.normed, self.gated, self.high, self.low = (
            k.sem("ho_" + n) for n in ("squared", "meant", "logged", "rstd", "gain", "normed", "gated", "high", "low"))
        self.z, self.xh, self.xl = (t[:].rearrange("p k n -> p (k n)") for t in (k.z, k.xh, k.xl))

    def cols(self, flat, h, part=0):
        return flat[:, (part * H + h) * T:(part * H + h + 1) * T]

    def tensor(self, pe):
        k, sq = self.k, self.z
        for h in range(H):
            b, c = 2 * (h % 4), (H + h) * T
            pe.wait_ge(self.squared, h + 1)
            if h >= 4:
                pe.wait_ge(self.logged, h - 3)
            for a in range(2):
                mm = pe.matmul(k.ps[:, b + a, 0:HALF], k.mean[:], sq[:, c + a * HALF:c + (a + 1) * HALF], start=True, stop=True)
            mm.then_inc(self.meant, 1)

    def scalar_first(self, act):
        for h in range(H):
            act.activation(self.cols(self.z, h, 1), self.cols(self.z, h), ACT.Square).then_inc(self.squared, 1)

    def scalar_second(self, act):
        k, z = self.k, self.z
        for h in range(H):
            b = 2 * (h % 4)
            act.wait_ge(self.meant, h + 1)
            act.activation(halves(self.cols(z, h, 2)), k.ps[:, b:b + 2, 0:HALF], ACT.Ln, bias=k.eps[:, 0:1]).then_inc(self.logged, 1)
        for h in range(H):
            act.wait_ge(self.logged, h + 1)
            act.activation(self.cols(z, h, 2), self.cols(z, h, 2), ACT.Exp, scale=-0.5).then_inc(self.rstd, 1)
        for h in range(H):
            act.wait_ge(self.gated, h + 1)
            act.activation(self.cols(self.xh, h), self.cols(z, h), ACT.Copy).then_inc(self.high, 1)

    def gpsimd(self, pool):
        for h in range(H):
            pool.tensor_scalar(self.cols(self.z, h, 3), self.cols(self.z, h, 3), self.k.onorm[:, 0:1], None, ALU.mult
                               ).then_inc(self.gain, 1)

    def vector(self, dve):
        z = self.z

        def low(h):
            dve.wait_ge(self.high, h + 1)
            dve.tensor_tensor(self.cols(self.xl, h), self.cols(z, h), self.cols(self.xh, h).bitcast(F32), ALU.subtract
                              ).then_inc(self.low, 1)

        for h in range(H):
            dve.wait_ge(self.rstd, h + 1)
            dve.wait_ge(self.gain, h + 1)
            dve.tensor_tensor(self.cols(z, h, 2), self.cols(z, h, 2), self.cols(z, h, 3), ALU.mult).then_inc(self.normed, 1)
            dve.wait_ge(self.normed, h + 1)
            dve.tensor_tensor(self.cols(z, h), self.cols(z, h), self.cols(z, h, 2), ALU.mult).then_inc(self.gated, 1)
            if h > 0:
                low(h - 1)
        low(H - 1)


def lower_bound(k):
    nc = k.nc
    top, ex, tot, done, scaled = (k.sem("lb_" + n) for n in ("top", "exp", "total", "done", "scaled"))
    with ExitStack() as st:
        d, p, r, q = (k.sb(st, "lb_" + n, [P, KD]) for n in ("d", "p", "r", "q"))
        with nc.Block() as block:
            @block.vector
            def _(dve):
                dve.tensor_scalar(k.qn8[:], k.qn[:], DH ** -0.5, None, ALU.mult).then_inc(scaled, 1)
                dve.tensor_tensor(d[:], k.a_lb[:], k.a_lb[:], ALU.subtract).then_inc(top, 1)
                dve.wait_ge(ex, 1)
                dve.reciprocal(r[:], p[:]).then_inc(tot, 1)
                dve.wait_ge(tot, 1)
                dve.tensor_tensor(q[:], p[:], r[:], ALU.mult).then_inc(tot, 1)
                dve.wait_ge(tot, 2)
                dve.tensor_tensor(k.lb[:, :, 0], q[:], q[:], ALU.subtract).then_inc(tot, 1)
                dve.wait_ge(tot, 3)
                dve.tensor_scalar(k.lb[:, :, 1], k.lb[:, :, 0], -1.0, 1.0, ALU.mult, ALU.add).then_inc(done, 1)

            @block.scalar
            def _(act):
                act.wait_ge(top, 1)
                act.activation(p[:], d[:], ACT.Exp).then_inc(ex, 1)


def forget_values(k, xh, xl):
    nc, ps = k.nc, k.ps
    e = {n: k.sem("fv_" + n) for n in ("loaded", "high", "low", "summed", "z", "abs", "exp", "ln", "logf", "turned", "rows",
                                       "stored", "cum", "c", "cstored")}
    with ExitStack() as tmp:
        lfrows = k.sb(tmp, "lf_rows", [P, 5, BH])
        w = k.sb(tmp, "fv_w", [P, KD, BH])
        wh, wl = (k.sb(tmp, n, [P, KD, BH], F32R) for n in ("fv_wh", "fv_wl"))
        bf = k.sb(tmp, "fv_bf", [BH, 1])
        tri, ones = k.sb(tmp, "fv_tri", [P, P]), k.sb(tmp, "fv_ones", [P, P])
        z, ab, lf = (k.sb(tmp, n, [BH, T]) for n in ("fv_z", "fv_ab", "fv_lf"))
        c4 = k.sb(tmp, "fv_c", [BH, 4, SEQ], F32R)
        with nc.Block() as block:
            @block.sync
            def _(sp):
                sp.dma_start(w[:], k.w["w_kvf"].rearrange("(k p) n -> p k n", p=P)[:, :, 2 * D:2 * D + BH]).then_inc(e["loaded"], 16)
                sp.dma_start(bf[:], k.w["b_f"].rearrange("(p o) -> p o", o=1), allow_slow_non_contiguous=True).then_inc(e["loaded"], 16)
                sp.dma_start(tri[:], k.w["c_tri"]).then_inc(e["loaded"], 16)
                sp.wait_ge(e["rows"], 1)
                sp.dma_start(k.out["logf_prompt"].rearrange("b (c p) h -> p (b c) h", p=P), lfrows[:, 0:4, :]).then_inc(e["stored"], 16)
                sp.dma_start(k.out["logf_sample"].rearrange("b q h -> (b q) h"), lfrows[0:NS, 4, :]).then_inc(e["stored"], 16)
                sp.wait_ge(e["c"], 3)
                sp.dma_start(k.cum_prompt.rearrange("s h n -> h s n"), c4[:].bitcast(F32)).then_inc(e["cstored"], 16)
                sp.wait_ge(e["stored"], 32)
                sp.wait_ge(e["cstored"], 16)

            @block.scalar
            def _(act):
                act.wait_ge(e["loaded"], 48)
                act.activation(wh[:], w[:], ACT.Copy).then_inc(e["high"], 1)
                act.wait_ge(e["summed"], 1)
                act.activation(halves(z[:]), ps[0:BH, 0:2, 0:HALF], ACT.Identity, bias=bf[:, 0:1]).then_inc(e["z"], 1)
                act.wait_ge(e["z"], 1)
                act.activation(ab[:], z[:], ACT.Abs).then_inc(e["abs"], 1)
                act.wait_ge(e["abs"], 1)
                act.activation(ab[:], ab[:], ACT.Exp, scale=-1.0).then_inc(e["exp"], 1)
                act.wait_ge(e["exp"], 1)
                act.activation(ab[:], ab[:], ACT.Ln, bias=1.0).then_inc(e["ln"], 1)
                act.wait_ge(e["cum"], 1)
                act.activation(c4[:, 0, :], ps[0:BH, 3, :], ACT.Copy).then_inc(e["c"], 1)
                act.wait_ge(e["c"], 2)
                act.activation(c4[:, 2:4, :], c4[:, 0:2, :].bitcast(F32), ACT.Copy, scale=-1.0).then_inc(e["c"], 1)

            @block.vector
            def _(dve):
                dve.memset(ones[:], 1.0)
                dve.wait_ge(e["high"], 1)
                dve.tensor_tensor(wl[:], w[:], wh[:].bitcast(F32), ALU.subtract).then_inc(e["low"], 1)
                dve.wait_ge(e["ln"], 1)
                dve.scalar_tensor_tensor(lf[:], z[:], 0.0, ab[:], ALU.min, ALU.subtract).then_inc(e["logf"], 1)
                dve.wait_ge(e["turned"], 1)
                dve.tensor_copy(lfrows[:, 0:4, :], ps[:, 2, 0:4 * BH].rearrange("p (c h) -> p c h", c=4))
                dve.tensor_copy(lfrows[0:NS, 4, :], ps[0:NS, 2, 4 * BH:5 * BH]).then_inc(e["rows"], 1)
                dve.wait_ge(e["c"], 1)
                dve.tensor_tensor(c4[:, 1, :], ps[0:BH, 3, :], c4[:, 0, :].bitcast(F32), ALU.subtract).then_inc(e["c"], 1)

            @block.tensor
            def _(pe):
                pe.wait_ge(e["low"], 1)
                for t in range(KD):
                    for n, (wt, at) in enumerate(((wh, xh), (wh, xl), (wl, xh))):
                        for a in range(2):
                            mm = pe.matmul(ps[0:BH, a, 0:HALF], wt[:, t, :], at[:, t, a * HALF:(a + 1) * HALF],
                                           start=t == 0 and n == 0, stop=t == KD - 1 and n == 2)
                mm.then_inc(e["summed"], 1)
                pe.wait_ge(e["logf"], 1)
                for c in range(5):
                    n = P if c < 4 else NS
                    mm = pe.transpose(ps[0:n, 2, c * BH:(c + 1) * BH], lf[:, c * P:c * P + n], k.ident[0:BH, 0:BH])
                mm.then_inc(e["turned"], 1)
                pe.wait_ge(e["rows"], 1)
                for c in range(4):
                    for i in range(c + 1):
                        mm = pe.matmul(ps[0:BH, 3, c * P:(c + 1) * P], lfrows[:, i, :], (tri if i == c else ones)[:],
                                       start=i == 0, stop=i == c)
                mm.then_inc(e["cum"], 1)


def head_rows(k, name, flat, first, gain=None, rows=None):
    nc, ps = k.nc, k.ps
    e = {n: k.sem(name + "_" + n) for n in ("squared", "summed", "logged", "rstd", "y", "turned")}
    with ExitStack() as tmp:
        sq = k.sb(tmp, name + "_sq", [P, KD, T]) if gain is not None else None
        tile = lambda j: flat[:, (j + first) * T:(j + first + 1) * T]
        evacuated = [k.sem(f"{name}_evacuated{s}") for s in range(2)]

        def evacuate(eng, copy, j):
            b = 4 + 2 * (j % 2)
            eng.wait_ge(e["turned"], j + 1)
            copy(rows[:, 0:4, j * P:(j + 1) * P], ps[:, b, :].rearrange("p (c n) -> p c n", c=4))
            copy(rows[0:NS, 4, j * P:(j + 1) * P], ps[0:NS, b + 1, 0:P]).then_inc(evacuated[j % 2], 1)

        with nc.Block() as block:
            @block.scalar
            def _(act):
                if gain is not None:
                    for j in range(KD):
                        act.activation(sq[:, j, :], tile(j), ACT.Square).then_inc(e["squared"], 1)
                    for j in range(KD):
                        b = 2 * (j % 2)
                        act.wait_ge(e["summed"], j + 1)
                        act.activation(halves(sq[:, j, :]), ps[:, b:b + 2, 0:HALF], ACT.Ln, bias=k.eps[:, 0:1]).then_inc(e["logged"], 1)
                    for j in range(KD):
                        act.wait_ge(e["logged"], j + 1)
                        act.activation(sq[:, j, :], sq[:, j, :], ACT.Exp, scale=-0.5).then_inc(e["rstd"], 1)
                if rows is not None:
                    for j in range(0, KD, 2):
                        evacuate(act, lambda o, i: act.activation(o, i, ACT.Copy), j)

            @block.vector
            def _(dve):
                for j in range(KD):
                    if gain is not None:
                        dve.wait_ge(e["rstd"], j + 1)
                        dve.scalar_tensor_tensor(tile(j), tile(j), gain, sq[:, j, :], ALU.mult, ALU.mult).then_inc(e["y"], 1)
                    if rows is not None and j % 2 == 0 and j > 0:
                        evacuate(dve, dve.tensor_copy, j - 1)
                if rows is not None:
                    evacuate(dve, dve.tensor_copy, KD - 1)

            @block.tensor
            def _(pe):
                if gain is not None:
                    for j in range(KD):
                        b = 2 * (j % 2)
                        pe.wait_ge(e["squared"], j + 1)
                        if j >= 2:
                            pe.wait_ge(e["logged"], j - 1)
                        for a in range(2):
                            mm = pe.matmul(ps[:, b + a, 0:HALF], k.headmean[:], sq[:, j, a * HALF:(a + 1) * HALF], start=True, stop=True)
                        mm.then_inc(e["summed"], 1)
                if rows is not None:
                    for j in range(KD):
                        b, y = 4 + 2 * (j % 2), tile(j)
                        if gain is not None:
                            pe.wait_ge(e["y"], j + 1)
                        if j >= 2:
                            pe.wait_ge(evacuated[j % 2], j // 2)
                        for c in range(4):
                            pe.transpose(ps[:, b, c * P:(c + 1) * P], y[:, c * P:(c + 1) * P], k.ident[:])
                        pe.transpose(ps[0:NS, b + 1, 0:P], y[:, SEQ:T], k.ident[:]).then_inc(e["turned"], 1)


def prompt_attention(k, kf, qf, vrows, oT, pages, past_logf, past_sems, row_stored):
    nc, ps = k.nc, k.ps
    e = {n: k.sem("pa_" + n) for n in ("const", "decays", "rounded", "scored", "max", "exp", "inv", "scaled", "turned", "rows", "mixed", "done")}
    staged = [k.sem(f"pa_staged{s}") for s in range(2)]
    U = 16
    with ExitStack() as st:
        kj, qj, vj = k.sb(st, "pa_k", [P, 2, SEQ]), k.sb(st, "pa_q", [P, 2, SEQ]), k.sb(st, "pa_v", [P, 2, 4, P])
        bl, br = k.sb(st, "pa_bl", [4, 4, SEQ], F32R), k.sb(st, "pa_br", [4, 4, SEQ], F32R)
        blraw, brraw = k.sb(st, "pa_blraw", [4, 2, SEQ]), k.sb(st, "pa_brraw", [4, 2, SEQ])
        causal = k.sb(st, "pa_causal", [P, P])
        nm, tot, inv = (k.sb(st, n, [P, 2]) for n in ("pa_nm", "pa_tot", "pa_inv"))
        pr, pt = k.sb(st, "pa_pr", [P, 2, SEQ]), k.sb(st, "pa_pt", [P, 2, SEQ])

        def slot(u):
            return u // 8, u // 4 % 2, u % 4

        with nc.Block() as block:
            @block.gpsimd
            def _(pool):
                pool.dma_start(pages[:], k.w["page_table"].rearrange("b p -> (b p)").unsqueeze(0)).then_inc(past_sems["pages"], 16)
                pool.wait_ge(past_sems["pages"], 16)
                with pool.Fori(0, NB) as b:
                    for p in range(PAGES):
                        page = pool.value_load(pages[0:1, bass.ds(b * PAGES + p, 1)], min_val=0, max_val=k.n_pool - 1)
                        pool.dma_start(past_logf[:, p, bass.ds(b * BH, BH)], k.w["cache_logf"][bass.ds(page, 1)]
                                       .rearrange("o t h -> t (o h)")).then_inc(past_sems["gathered"], 16)

            @block.sync
            def _(sp):
                sp.dma_start(causal[:], k.w["c_causal"]).then_inc(e["const"], 16)
                for a in range(2):
                    sp.dma_start(blraw[0:2, a, :], k.w["c_ones"][:, 0:SEQ]).then_inc(e["const"], 16)
                    sp.dma_start(brraw[2:4, a, :], k.w["c_ones"][:, 0:SEQ]).then_inc(e["const"], 16)
                sp.wait_ge(row_stored, 64)
                sp.sem_inc(e["done"], 2)
                sp.sem_inc(e["rounded"], 1)
                with sp.Fori(0, KD // 2) as j:
                    for s in range(2):
                        pair = 2 * j + s
                        sp.wait_ge(e["done"], 2 * j + (s + 1))
                        sp.dma_start(kj[:, s], kf[:, bass.ds(pair * T, SEQ)]).then_inc(staged[s], 16)
                        sp.dma_start(qj[:, s], qf[:, bass.ds(pair * T, SEQ)]).then_inc(staged[s], 16)
                        sp.dma_start(vj[:, s], vrows[:, 0:4, bass.ds(pair * P, P)]).then_inc(staged[s], 16)
                        sp.wait_ge(e["rounded"], 2 * j + (s + 1))
                        sp.dma_start(blraw[2:4], k.cum_prompt[0:2, bass.ds(2 * pair, 2)]).then_inc(e["decays"], 16)
                        sp.dma_start(brraw[0:2], k.cum_prompt[2:4, bass.ds(2 * pair, 2)]).then_inc(e["decays"], 16)

            @block.tensor
            def _(pe):
                def score(j, u):
                    s, a, i = slot(u)
                    n = (i + 1) * P
                    if u % 8 == 0:
                        pe.wait_ge(staged[s], 48 * j + 48)
                        pe.wait_ge(e["rounded"], 2 * j + (s + 2))
                    if u >= 2:
                        pe.wait_ge(e["exp"], U * j + u - 1)
                    r = slice(DH * a, DH * (a + 1))
                    out = ps[:, u % 2, 0:n]
                    pe.matmul(out, qj[r, s, i * P:(i + 1) * P], kj[r, s, 0:n], start=True, stop=False)
                    pe.matmul(ps[:, u % 2, i * P:n], k.ident[:], causal[:], start=False, stop=False)
                    pe.matmul(out, bl[:, 2 * s + a, i * P:(i + 1) * P], br[:, 2 * s + a, 0:n], start=False, stop=True
                              ).then_inc(e["scored"], 1)

                def turn(j, u):
                    pe.wait_ge(e["scaled"], U * j + u + 1)
                    if u >= 2:
                        pe.wait_ge(e["rows"], U * j + u - 1)
                    for c in range(u % 4 + 1):
                        mm = pe.transpose(ps[:, 2 + u % 2, c * P:(c + 1) * P], pr[:, u % 2, c * P:(c + 1) * P], k.ident[:])
                    mm.then_inc(e["turned"], 1)

                def mix(j, u):
                    s, a, i = slot(u)
                    if u % 8 == 0:
                        pe.wait_ge(e["done"], 2 * j + (s + 1))
                    pe.wait_ge(e["rows"], U * j + u + 1)
                    for c in range(i + 1):
                        mm = pe.matmul(ps[DH * a:DH * (a + 1), 4 + s, i * P:(i + 1) * P], vj[:, s, c, DH * a:DH * (a + 1)],
                                       pt[:, u % 2, c * P:(c + 1) * P], start=c == 0, stop=c == i)
                    mm.then_inc(e["mixed"], 1)

                pe.wait_ge(e["const"], 80)
                with pe.Fori(0, KD // 2) as j:
                    for u in range(U + 3):
                        if u < U:
                            score(j, u)
                        if 2 <= u < U + 2:
                            turn(j, u - 2)
                        if u >= 3:
                            mix(j, u - 3)

            @block.scalar
            def _(act):
                def decays(j, s):
                    act.wait_ge(e["decays"], 64 * j + (32 * s + 32))
                    act.activation(bl[:, 2 * s:2 * s + 2, :], blraw[:], ACT.Copy)
                    act.activation(br[:, 2 * s:2 * s + 2, :], brraw[:], ACT.Copy).then_inc(e["rounded"], 1)

                act.wait_ge(e["const"], 80)
                with act.Fori(0, KD // 2) as j:
                    for u in range(U):
                        if u in (0, 4):
                            decays(j, u // 4)
                        n = (u % 4 + 1) * P
                        act.wait_ge(e["max"], U * j + u + 1)
                        if u >= 2:
                            act.wait_ge(e["turned"], U * j + u - 1)
                        act.activation(pr[:, u % 2, 0:n], ps[:, u % 2, 0:n], ACT.Exp, bias=nm[:, u % 2:u % 2 + 1],
                                       accum_out=tot[:, u % 2:u % 2 + 1]).then_inc(e["exp"], 1)

            @block.vector
            def _(dve):
                def rows(j, u):
                    n = (u % 4 + 1) * P
                    dve.wait_ge(e["turned"], U * j + u + 1)
                    if u >= 2:
                        dve.wait_ge(e["mixed"], U * j + u - 1)
                    dve.tensor_copy(pt[:, u % 2, 0:n], ps[:, 2 + u % 2, 0:n]).then_inc(e["rows"], 1)

                def output(j, s):
                    dve.wait_ge(e["mixed"], U * j + 8 * s + 8)
                    dve.tensor_copy(oT[:, bass.ds((2 * j + s) * T, SEQ)], ps[:, 4 + s, :]).then_inc(e["done"], 1)

                def maximum(j, u):
                    n, s = (u % 4 + 1) * P, slice(u % 2, u % 2 + 1)
                    dve.wait_ge(e["scored"], U * j + u + 1)
                    if u >= 2:
                        dve.wait_ge(e["exp"], U * j + u - 1)
                    dve.tensor_reduce(nm[:, s], ps[:, u % 2, 0:n], AX.X, ALU.max, negate=True).then_inc(e["max"], 1)

                def scale(j, u):
                    n, s = (u % 4 + 1) * P, slice(u % 2, u % 2 + 1)
                    dve.wait_ge(e["exp"], U * j + u + 1)
                    dve.reciprocal(inv[:, s], tot[:, s]).then_inc(e["inv"], 1)
                    dve.wait_ge(e["inv"], U * j + u + 1)
                    dve.tensor_scalar(pr[:, u % 2, 0:n], pr[:, u % 2, 0:n], inv[:, s], None, ALU.mult).then_inc(e["scaled"], 1)

                with dve.Fori(0, KD // 2) as j:
                    for u in range(U + 2):
                        if u < U:
                            maximum(j, u)
                        if 1 <= u <= U:
                            scale(j, u - 1)
                        if u >= 2:
                            rows(j, u - 2)
                        if u == 8 + 3:
                            output(j, 0)
                    output(j, 1)


class PastDecay:

    def __init__(self, k, st, lf, past_sems, whole, high, low):
        self.k, self.lf, self.past_sems = k, lf, past_sems
        self.neg, self.parts = whole, (high, low)
        self.loaded, self.summed, self.off, self.negated, self.new, self.parted, self.stored = (
            k.sem("pd_" + n) for n in ("loaded", "summed", "off", "neg", "new", "parts", "stored"))
        self.lnew, self.cnew, self.negnew = (k.sb(st, "pd_" + n, [P, NQ]) for n in ("new", "cnew", "negnew"))
        self.tri, self.total = k.sb(st, "pd_tri", [P, P]), k.sb(st, "pd_off", [P, PAGES + 1])
        self.newparts, self.negnewparts = (k.sb(st, "pd_" + n, [P, 2, NQ], F32R) for n in ("newparts", "negnewparts"))

    def load(self, sp):
        k = self.k
        sp.dma_start(self.tri[:], k.w["c_tri"]).then_inc(self.loaded, 16)
        for b in range(NB):
            sp.dma_start(self.lnew[b * BH:(b + 1) * BH, :], k.out["logf_sample"][b].rearrange("q h -> h q"),
                         allow_slow_non_contiguous=True).then_inc(self.loaded, 16)

    def store(self, sp):
        k = self.k
        sp.wait_ge(self.parted, 6)
        for part in range(2):
            sp.dma_start(k.neg_decay[part, :, 0:PAST], self.parts[part].bitcast(F32)).then_inc(self.stored, 16)
        sp.dma_start(k.neg_decay[:, :, PAST:PAST + NQ].rearrange("s r n -> r s n"), self.negnewparts[:].bitcast(F32)
                     ).then_inc(self.stored, 16)
        sp.dma_start(k.new_decay.rearrange("s b (h q) -> (b h) s q", h=BH), self.newparts[:].bitcast(F32)).then_inc(self.stored, 16)
        sp.wait_ge(self.stored, 64)

    def tensor(self, pe):
        pe.wait_ge(self.loaded, 16 * (1 + NB))
        pe.wait_ge(self.past_sems["gathered"], 16 * NB * PAGES)
        for p in range(PAGES):
            mm = pe.matmul(self.k.ps[:, p // 4, (p % 4) * P:(p % 4 + 1) * P], self.lf[:, p, :], self.tri[:], start=True, stop=True)
        mm.then_inc(self.summed, 1)

    def vector(self, dve):
        ps, total, cnew = self.k.ps, self.total, self.cnew
        dve.memset(total[:, 0:1], 0.0).then_inc(self.off, 1)
        dve.wait_ge(self.summed, 1)
        for p in range(PAGES):
            local = ps[:, p // 4, (p % 4) * P:(p % 4 + 1) * P]
            dve.wait_ge(self.off, p + 1)
            dve.tensor_tensor(total[:, p + 1:p + 2], total[:, p:p + 1], local[:, P - 1:P], ALU.add).then_inc(self.off, 1)
            dve.tensor_scalar(self.neg[:, p * P:(p + 1) * P], local, total[:, p:p + 1], -1.0, ALU.add, ALU.mult
                              ).then_inc(self.negated, 1)
        for q in range(NQ):
            before = total[:, PAGES:PAGES + 1] if q == 0 else cnew[:, q - 1:q]
            dve.wait_ge(self.off, PAGES + 1)
            if q > 0:
                dve.wait_ge(self.new, q)
            dve.tensor_tensor(cnew[:, q:q + 1], before, self.lnew[:, q:q + 1], ALU.add).then_inc(self.new, 1)
        dve.wait_ge(self.new, NQ)
        dve.tensor_scalar(self.negnew[:], cnew[:], -1.0, None, ALU.mult).then_inc(self.negated, 1)
        dve.wait_ge(self.negated, PAGES + 1)
        for n, (high, low, whole) in enumerate(((self.parts[0], self.parts[1], self.neg),
                                                (self.negnewparts[:, 0, :], self.negnewparts[:, 1, :], self.negnew[:]),
                                                (self.newparts[:, 0, :], self.newparts[:, 1, :], cnew[:]))):
            dve.tensor_copy(high, whole).then_inc(self.parted, 1)
            dve.wait_ge(self.parted, 2 * n + 1)
            dve.tensor_tensor(low, whole, high.bitcast(F32), ALU.subtract).then_inc(self.parted, 1)


def sample_attention(k, ks, qs, oT, past_logf, past_sems):
    nc, ps = k.nc, k.ps
    e = {n: k.sem("sa_" + n) for n in (
        "const", "zero", "rows", "rounded", "vnew", "pages", "q", "qh", "ql", "turned", "kh", "kl", "used", "scored", "mx", "max", "exp",
        "sum", "inv", "pturned", "ph", "pl", "tailt", "tail", "vh", "vl", "pv", "om", "picked", "done")}
    kload = [k.sem(f"sa_kload{s}") for s in range(2)]
    vload = [k.sem(f"sa_vload{s}") for s in range(2)]
    G, J = 4, KD
    STEPS, HV = G * J, 2 * PAGES
    INSIDE = HV - 6
    KSLOTS, VSLOTS = 3, 4
    with ExitStack() as st:
        sb = lambda n, shape, dt=F32: k.sb(st, "sa_" + n, shape, dt)
        pages = sb("pages", [1, NB * PAGES], I32)
        kp, vp = sb("kp", [P, 2, 4, D]), sb("vp", [P, 2, 4, D])
        kh, kl = sb("kh", [P, KSLOTS, SEQ], F32R), sb("kl", [P, KSLOTS, SEQ], F32R)
        vh, vl = sb("vh", [P, VSLOTS, SEQ], F32R), sb("vl", [P, VSLOTS, SEQ], F32R)
        qz = sb("qz", [P, J * P])
        qh, ql = sb("qh", [P, J, P], F32R), sb("ql", [P, J, P], F32R)
        vn = sb("vn", [NQ, D])
        rowl, rowr = sb("rowl", [2 * BH + 2, P], F32R), sb("rowr", [2 * BH + 2, PAST + NQ], F32R)
        rawl, rawr = sb("rawl", [2 * BH + 2, P]), sb("rawr", [2 * BH + 2, PAST + NQ])
        scausal, pickq, rowhead = sb("scausal", [P, NQ]), sb("pickq", [P, NQ]), sb("rowhead", [P, D])
        mx, tot, nm, inv = sb("mx", [P, G + 1]), sb("tot", [P, G + 1]), sb("nm", [P, 1]), sb("inv", [P, 2])
        pr, ptail, ptt = sb("pr", [P, PAST]), sb("ptail", [P, NQ]), sb("ptt", [NQ, P])
        ph, pl = sb("ph", [P, PAGES, P], F32R), sb("pl", [P, PAGES, P], F32R)
        om = past_logf[:].rearrange("p a n -> p (a n)")[:, 0:D]
        past = PastDecay(k, st, past_logf, past_sems, pr[:], *(t[:].rearrange("p a n -> p (a n)") for t in (ph, pl)))
        cache = {"k": k.w["cache_k"].rearrange("n t h d -> n t (h d)"), "v": k.w["cache_v"].rearrange("n t h d -> n t (h d)")}

        def at(h):
            return 3 + h * (STEPS - 2) // INSIDE

        def step_units(i, lead):
            return [h for h in range(HV) if (i == 0 if h < lead else h - lead < INSIDE and at(h - lead) == i)]

        def last_units(lead):
            return range(INSIDE + lead, HV)

        LEAD = 3

        with nc.Block() as block:
            @block.sync
            def _(sp):
                sp.dma_start(pages[:], k.w["page_table"].rearrange("b p -> (b p)").unsqueeze(0)).then_inc(e["pages"], 16)
                past.load(sp)
                for dst, src in ((rawl[0:BH, :], "c_headrow"), (rawl[BH:2 * BH, :], "c_headrow"), (scausal[:], "c_scausal"), (pickq[:], "c_pickq"),
                                 (rowhead[:], "c_rowhead")):
                    sp.dma_start(dst, k.w[src]).then_inc(e["const"], 16)
                sp.dma_start(rawr[2 * BH:2 * BH + 2, :], k.w["c_ones"]).then_inc(e["const"], 16)
                sp.wait_ge(e["pages"], 16)
                sp.sem_inc(e["turned"], 2 * J)
                sp.sem_inc(e["vl"], 16)
                sp.sem_inc(e["pv"], VSLOTS)
                sp.sem_inc(e["done"], 1)

                def load(b, g, which, ring, sems, free, value):
                    numbers = [sp.value_load(pages[0:1, bass.ds(b * PAGES + g * 4 + p, 1)], min_val=0, max_val=k.n_pool - 1)
                               for p in range(4)]
                    sp.wait_ge(free, value)
                    for p, page in enumerate(numbers):
                        sp.dma_start(ring[:, g % 2, p, :], cache[which][bass.ds(page, 1)].rearrange("o t n -> t (o n)")
                                     ).then_inc(sems[g % 2], 16)

                def rows(b):
                    for part in range(2):
                        sp.dma_start(rawr[part * BH:(part + 1) * BH, :], k.neg_decay[part, bass.ds(b * BH, BH), :]).then_inc(e["rows"], 16)
                    sp.dma_start(rawl[2 * BH:2 * BH + 2, :], k.new_decay[:, bass.ds(b, 1), :].rearrange("s b n -> (s b) n")
                                 ).then_inc(e["rows"], 16)

                def keys(b, g):
                    load(b, g, "k", kp, kload, e["turned"], b * STEPS + (g + 1) * J)

                def values(b, g):
                    load(b, g, "v", vp, vload, e["vl"], b * HV + (g + 1) * 8)

                def new_values(b):
                    sp.dma_start(vn[:], k.out["v_sample"].rearrange("b q h d -> b q (h d)")[bass.ds(b, 1)]
                                 .rearrange("b q n -> (b q) n")).then_inc(e["vnew"], 16)

                keys(0, 0)
                keys(0, 1)
                past.store(sp)
                rows(0)
                for g in range(2, G):
                    keys(0, g)
                with sp.Fori(0, NB - 1) as c:
                    for g in range(G):
                        keys(c + 1, g)
                        if g == 1:
                            sp.wait_ge(e["rounded"], c + 1)
                            rows(c + 1)
                        values(c, g)
                        if g == 1:
                            sp.wait_ge(e["pv"], c * HV + VSLOTS)
                            new_values(c)
                for g in range(G):
                    values(NB - 1, g)
                    if g == 1:
                        sp.wait_ge(e["pv"], (NB - 1) * HV + VSLOTS)
                        new_values(NB - 1)

            @block.tensor
            def _(pe):
                def turn(b, i):
                    g, j = divmod(i, J)
                    if j == 0:
                        pe.wait_ge(kload[g % 2], (b * 2 + g // 2 + 1) * 64)
                    if i >= 2:
                        pe.wait_ge(e["kl"], b * STEPS + i - 1)
                    for p in range(4):
                        mm = pe.transpose(ps[:, 4 + i % 2, p * P:(p + 1) * P], kp[:, g % 2, p, j * P:(j + 1) * P], k.ident[:])
                    mm.then_inc(e["turned"], 1)

                def score(b, c, i):
                    g, j = divmod(i, J)
                    pe.wait_ge(e["kl"], b * STEPS + i + 1)
                    if i == 0:
                        pe.wait_ge(e["ql"], b + 1)
                    if j == 0 and c is not None:
                        pe.wait_ge(e["pl"], c * G + g + 1)
                    for n, (qt, kt) in enumerate(((qh, kh), (ql, kh), (qh, kl))):
                        mm = pe.matmul(ps[:, g, :], qt[:, j, :], kt[:, i % KSLOTS, :], start=j == 0 and n == 0, stop=False)
                    if j == J - 1:
                        if g == 0:
                            pe.wait_ge(e["rounded"], b + 1)
                        mm = pe.matmul(ps[:, g, :], rowl[:], rowr[:, g * SEQ:(g + 1) * SEQ], start=False, stop=True)
                    mm.then_inc(e["used"], 1)

                def new_scores(b):
                    pe.matmul(ps[:, 4, 0:NQ], rowl[:], rowr[:, PAST:PAST + NQ], start=True, stop=False)
                    pe.matmul(ps[:, 4, 0:NQ], k.ident[:], scausal[:], start=False, stop=False)
                    for j in range(J):
                        mm = pe.matmul(ps[:, 4, 0:NQ], qz[:, j * P:(j + 1) * P], ks[:, j, bass.ds(b * NQ, NQ)],
                                       start=False, stop=j == J - 1)
                    mm.then_inc(e["scored"], 1)

                def mix(c, h):
                    p, a = divmod(h, 2)
                    pe.wait_ge(e["vl"], c * HV + h + 17)
                    if h == 0:
                        pe.wait_ge(e["done"], c + 1)
                    if h % 8 == 0:
                        pe.wait_ge(e["pl"], c * G + h // 8 + 1)
                    for n, (pp, vv) in enumerate(((ph, vh), (pl, vh), (ph, vl))):
                        mm = pe.matmul(ps[:, 6 + a, :], pp[:, p, :], vv[:, h % VSLOTS, :], start=h < 2 and n == 0, stop=False)
                    if p == PAGES - 1:
                        pe.wait_ge(e["tail"], c + 1)
                        pe.wait_ge(e["vnew"], c * 16 + 16)
                        mm = pe.matmul(ps[:, 6 + a, :], ptt[:], vn[:, a * SEQ:(a + 1) * SEQ], start=False, stop=True)
                    mm.then_inc(e["pv"], 1)

                def turn_probabilities(b):
                    for g in range(G):
                        pe.wait_ge(e["exp"], b * (G + 1) + g + 2)
                        for p in range(4):
                            mm = pe.transpose(ps[:, g, p * P:(p + 1) * P], pr[:, (4 * g + p) * P:(4 * g + p + 1) * P], k.ident[:])
                        mm.then_inc(e["pturned"], 1)
                    pe.transpose(ps[0:NQ, 5, 0:P], ptail[:], k.ident[:]).then_inc(e["tailt"], 1)

                def pick(c):
                    pe.wait_ge(e["om"], c + 1)
                    for j in range(J):
                        mm = pe.matmul(ps[:, 6, j * NQ:(j + 1) * NQ], om[:, j * P:(j + 1) * P], pickq[:], start=True, stop=True)
                    mm.then_inc(e["picked"], 1)

                def body(b, c):
                    for i in range(STEPS + 2):
                        if i < STEPS:
                            if i == 1 and c is not None:
                                pe.wait_ge(e["tail"], c + 1)
                            turn(b, i)
                        if i >= 2:
                            score(b, c, i - 2)
                        if c is not None:
                            for h in step_units(i, 0):
                                mix(c, h)
                    new_scores(b)
                    if c is not None:
                        for h in last_units(0):
                            mix(c, h)
                    turn_probabilities(b)
                    if c is not None:
                        pick(c)

                past.tensor(pe)
                pe.wait_ge(e["const"], 96)
                body(0, None)
                with pe.Fori(0, NB - 1) as c:
                    body(c + 1, c)
                for h in range(HV):
                    mix(NB - 1, h)
                pick(NB - 1)

            @block.scalar
            def _(act):
                def key_high(b, c, i):
                    act.wait_ge(e["turned"], b * STEPS + 2 * J + i + 1)
                    if i >= KSLOTS:
                        act.wait_ge(e["used"], b * STEPS + i - KSLOTS + 1)
                    act.activation(kh[:, i % KSLOTS, :], ps[:, 4 + i % 2, :], ACT.Copy).then_inc(e["kh"], 1)

                def value_high(c, h):
                    if h % 8 == 0:
                        act.wait_ge(vload[(h // 8) % 2], (c * 2 + h // 16 + 1) * 64)
                    act.wait_ge(e["pv"], c * HV + h + 1)
                    act.activation(vh[:, h % VSLOTS, :], vp[:, (h // 8) % 2, h // 2 % 4, (h % 2) * SEQ:(h % 2 + 1) * SEQ],
                                   ACT.Copy).then_inc(e["vh"], 1)

                def decays(b):
                    act.wait_ge(e["rows"], b * 48 + 48)
                    act.activation(rowl[:], rawl[:], ACT.Copy)
                    act.activation(rowr[:], rawr[:], ACT.Copy).then_inc(e["rounded"], 1)

                def query_high(b):
                    act.wait_ge(e["q"], b * 2 + 2)
                    act.activation(qh[:].rearrange("p j n -> p (j n)"), qz[:], ACT.Copy).then_inc(e["qh"], 1)

                def body(b, c):
                    for i in range(STEPS + 2):
                        if i < STEPS:
                            key_high(b, c, i)
                        if i == J // 2:
                            decays(b)
                        if c is not None:
                            for h in step_units(i, LEAD):
                                value_high(c, h)
                    late = list(last_units(LEAD)) if c is not None else []
                    for h in late[:2]:
                        value_high(c, h)
                    act.wait_ge(e["max"], b + 1)
                    act.activation(ptail[:], ps[:, 4, 0:NQ], ACT.Exp, bias=nm[:, 0:1], accum_out=tot[:, G:G + 1]).then_inc(e["exp"], 1)
                    for g in range(G):
                        act.activation(pr[:, g * SEQ:(g + 1) * SEQ], ps[:, g, :], ACT.Exp, bias=nm[:, 0:1],
                                       accum_out=tot[:, g:g + 1]).then_inc(e["exp"], 1)
                        if g == 0:
                            for h in late[2:]:
                                value_high(c, h)
                    query_high(b + 1)
                    if c is not None:
                        act.wait_ge(e["pv"], c * HV + HV + VSLOTS)
                    for g in range(G):
                        act.wait_ge(e["pturned"], b * G + g + 1)
                        act.activation(ph[:, 4 * g:4 * g + 4, :].rearrange("p a n -> p (a n)"), ps[:, g, :], ACT.Copy
                                       ).then_inc(e["ph"], 1)

                act.wait_ge(e["const"], 96)
                query_high(0)
                body(0, None)
                with act.Fori(0, NB - 1) as c:
                    body(c + 1, c)
                for h in range(HV):
                    value_high(NB - 1, h)

            @block.vector
            def _(dve):
                def key_low(b, i):
                    dve.wait_ge(e["kh"], b * STEPS + i + 1)
                    dve.tensor_tensor(kl[:, i % KSLOTS, :], ps[:, 4 + i % 2, :], kh[:, i % KSLOTS, :].bitcast(F32),
                                      ALU.subtract).then_inc(e["kl"], 1)

                def value_low(c, h):
                    dve.wait_ge(e["vh"], c * HV + h + 1)
                    dve.tensor_tensor(vl[:, h % VSLOTS, :], vp[:, (h // 8) % 2, h // 2 % 4, (h % 2) * SEQ:(h % 2 + 1) * SEQ],
                                      vh[:, h % VSLOTS, :].bitcast(F32), ALU.subtract).then_inc(e["vl"], 1)

                def group_max(b, g):
                    dve.wait_ge(e["used"], b * STEPS + (g + 1) * J)
                    dve.tensor_reduce(mx[:, g:g + 1], ps[:, g, :], AX.X, ALU.max).then_inc(e["mx"], 1)

                def queries(b):
                    for a in range(2):
                        r = slice(DH * a, DH * (a + 1))
                        dst = blocks(qz[r, :], J, 2 * NQ, a * NQ, NQ)
                        dve.tensor_copy(dst, qs[r, :, bass.ds(b * NQ, NQ)]).then_inc(e["q"], 1)

                def query_low(b):
                    dve.wait_ge(e["qh"], b + 1)
                    dve.tensor_tensor(ql[:].rearrange("p j n -> p (j n)"), qz[:],
                                      qh[:].rearrange("p j n -> p (j n)").bitcast(F32), ALU.subtract).then_inc(e["ql"], 1)

                def outputs(c):
                    dve.wait_ge(e["inv"], c + 1)
                    dve.wait_ge(e["pv"], c * HV + HV + VSLOTS)
                    dve.scalar_tensor_tensor(om, ps[:, 6:8, :].rearrange("p a n -> p (a n)"), inv[:, 1:2], rowhead[:],
                                             ALU.mult, ALU.mult).then_inc(e["om"], 1)

                def finish(c):
                    dve.wait_ge(e["picked"], c + 1)
                    dve.tensor_copy(oT[:].rearrange("p (j n) -> p j n", j=J)[:, :, bass.ds(c * NQ + SEQ, NQ)],
                                    ps[:, 6, 0:J * NQ].rearrange("p (j n) -> p j n", j=J)).then_inc(e["done"], 1)

                def body(b, c):
                    for i in range(STEPS + 2):
                        if i < STEPS:
                            key_low(b, i)
                        if i > J + 2 and (i - 3) % J == 0:
                            group_max(b, (i - 3) // J - 1)
                        if c is not None:
                            for h in step_units(i, LEAD):
                                value_low(c, h)
                    group_max(b, G - 1)
                    late = list(last_units(LEAD)) if c is not None else []
                    for h in late[:1]:
                        value_low(c, h)
                    dve.wait_ge(e["scored"], b + 1)
                    dve.tensor_reduce(mx[:, G:G + 1], ps[:, 4, 0:NQ], AX.X, ALU.max).then_inc(e["mx"], 1)
                    dve.wait_ge(e["mx"], (G + 1) * b + G + 1)
                    dve.tensor_reduce(nm[:], mx[:], AX.X, ALU.max, negate=True).then_inc(e["max"], 1)
                    for h in late[1:]:
                        value_low(c, h)
                    queries(b + 1)
                    if c is not None:
                        outputs(c)
                    query_low(b + 1)
                    for g in range(G):
                        dve.wait_ge(e["ph"], b * G + g + 1)
                        dve.tensor_tensor(pl[:, 4 * g:4 * g + 4, :].rearrange("p a n -> p (a n)"), ps[:, g, :],
                                          ph[:, 4 * g:4 * g + 4, :].rearrange("p a n -> p (a n)").bitcast(F32),
                                          ALU.subtract).then_inc(e["pl"], 1)
                    dve.wait_ge(e["tailt"], b + 1)
                    dve.tensor_copy(ptt[:], ps[0:NQ, 5, 0:P]).then_inc(e["tail"], 1)
                    dve.wait_ge(e["exp"], (G + 1) * b + G + 1)
                    dve.tensor_reduce(inv[:, 0:1], tot[:], AX.X, ALU.add).then_inc(e["sum"], 1)
                    dve.wait_ge(e["sum"], b + 1)
                    dve.reciprocal(inv[:, 1:2], inv[:, 0:1]).then_inc(e["inv"], 1)
                    if c is not None:
                        finish(c)

                past.vector(dve)
                dve.memset(qz[:], 0.0).then_inc(e["zero"], 1)
                dve.wait_ge(e["zero"], 1)
                queries(0)
                query_low(0)
                body(0, None)
                with dve.Fori(0, NB - 1) as c:
                    body(c + 1, c)
                for h in range(HV):
                    value_low(NB - 1, h)
                outputs(NB - 1)
                finish(NB - 1)


def blocks(ap, count, step, first, n):
    pattern = [list(ap.ap[0]), [P + step, count], [1, n]]
    return bass.AP(ap.tensor, ap.offset + first, pattern)


class Split:

    def __init__(self, k, oT):
        self.k, self.o = k, oT[:].rearrange("p (k n) -> p k n", n=T)
        self.high, self.low = k.sem("sr_high"), k.sem("sr_low")

    def scalar_first(self, act):
        for f in range(KD):
            act.activation(self.k.xh[:, f, :], self.o[:, f, :], ACT.Copy).then_inc(self.high, 1)

    def scalar_second(self, act):
        pass

    def tensor(self, pe):
        pass

    def gpsimd(self, pool):
        pass

    def vector(self, dve):
        for f in range(KD):
            dve.wait_ge(self.high, f + 1)
            dve.tensor_tensor(self.k.xl[:, f, :], self.o[:, f, :], self.k.xh[:, f, :].bitcast(F32), ALU.subtract
                              ).then_inc(self.low, 1)


def with_split(k, name):
    st = ExitStack()
    k.xh, k.xl = k.sb(st, name + "_xh", [P, KD, T], F32R), k.sb(st, name + "_xl", [P, KD, T], F32R)
    return st


def fox(k, gains):
    nc = k.nc
    with ExitStack() as so, ExitStack() as so_past:
        oT = k.sb(so, "oT", [P, KD * T])
        ks = k.sb(so, "k_new", [P, KD, NS])
        qs = k.sb(so, "q_new", [P, KD, NS + NQ])
        pages = k.sb(so_past, "past_pages", [1, NB * PAGES], I32)
        past_logf = k.sb(so_past, "past_logf", [P, PAGES, NB * BH])
        with ExitStack() as st:
            kv, q = k.sb(st, "kv", [P, 2 * KD * T]), k.sb(st, "qf", [P, KD * T])
            with with_split(k, "kvx"), ExitStack() as shared:
                rstd = k.sb(shared, "kvb_rstd", [P, T])
                dense(k, "kvf", k.w["w_kvf"], KD, 1, k.xh, k.xl, KD, lambda i, u: (i * 2 + u) * P, store_to(kv[:]),
                      gain=gains["kv_norm"], rstd=(rstd, False))
                forget_values(k, k.xh, k.xl)
                dense(k, "wq", k.w["b_wq"][0], KD, 1, k.xh, k.xl, KD // 2, lambda i, u: (i * 2 + u) * P, store_to(q[:]),
                      gain=gains["b_norm"], rstd=(rstd, True))
            k.retire()
            vrows, krows = k.sb(st, "v_rows", [P, 5, D]), k.sb(st, "k_rows", [P, 5, D])
            row_stored = k.sem("rows_stored")
            head_rows(k, "vr", kv, KD, rows=vrows)
            store_rows(k, "v", vrows, row_stored)
            head_rows(k, "kr", kv, 0, gain=k.kn[:, 0:1], rows=krows)
            store_rows(k, "k", krows, row_stored)
            head_rows(k, "qr", q, 0, gain=k.qn8[:, 0:1])
            past_sems = {n: k.sem("past_" + n) for n in ("pages", "gathered")}
            prompt_attention(k, kv, q, vrows, oT, pages, past_logf, past_sems, row_stored)
            copied = k.sem("new_copied")
            with nc.Block() as block:
                @block.vector
                def _(dve):
                    dve.tensor_copy(ks[:], kv[:, 0:KD * T].rearrange("p (j n) -> p j n", j=KD)[:, :, SEQ:T]).then_inc(copied, 1)
                    dve.memset(qs[:, :, NS:NS + NQ], 0.0).then_inc(copied, 1)
                    dve.tensor_copy(qs[:, :, 0:NS], q[:].rearrange("p (j n) -> p j n", j=KD)[:, :, SEQ:T]).then_inc(copied, 1)
        sample_attention(k, ks, qs, oT, past_logf, past_sems)
        so_past.close()
        k.retire()
        with with_split(k, "ox"):
            dense(k, "wo", k.w["b_wo"][0], KD, 1, k.xh, k.xl, KD // 2, lambda i, u: (i * 2 + u) * P, add_to_stream(k),
                  before=Split(k, oT))


def store_rows(k, which, rows, done):
    with k.nc.Block() as block:
        @block.sync
        def _(sp):
            sp.dma_start(k.out[which + "_prompt"].rearrange("b (c p) h d -> p (b c) (h d)", p=P), rows[:, 0:4, :]).then_inc(done, 16)
            sp.dma_start(k.out[which + "_sample"].rearrange("b q h d -> (b q) (h d)"), rows[0:NS, 4, :]).then_inc(done, 16)


def store_y(k):
    nc = k.nc
    turned, copied, stored = (k.sem("y_" + n) for n in ("turned", "copied", "stored"))
    with ExitStack() as st:
        rows = k.sb(st, "y_rows", [P, 5, D])
        with nc.Block() as block:
            @block.tensor
            def _(pe):
                for f in range(KD):
                    b = 2 * (f % 2)
                    if f >= 2:
                        pe.wait_ge(copied, f - 1)
                    for c in range(4):
                        pe.transpose(k.ps[:, b, c * P:(c + 1) * P], k.xT[:, f, c * P:(c + 1) * P], k.ident[:])
                    pe.transpose(k.ps[0:NS, b + 1, 0:P], k.xT[:, f, SEQ:T], k.ident[:]).then_inc(turned, 1)

            @block.vector
            def _(dve):
                for f in range(KD):
                    b = 2 * (f % 2)
                    dve.wait_ge(turned, f + 1)
                    dve.tensor_copy(rows[:, 0:4, f * P:(f + 1) * P], k.ps[:, b, :].rearrange("p (c n) -> p c n", c=4))
                    dve.tensor_copy(rows[0:NS, 4, f * P:(f + 1) * P], k.ps[0:NS, b + 1, 0:P]).then_inc(copied, 1)

            @block.sync
            def _(sp):
                sp.wait_ge(copied, KD)
                sp.dma_start(k.out["y_prompt"].rearrange("b (c p) d -> p (b c) d", p=P), rows[:, 0:4, :]).then_inc(stored, 16)
                sp.dma_start(k.out["y_sample"].rearrange("b q d -> (b q) d"), rows[0:NS, 4, :]).then_inc(stored, 16)
                sp.wait_ge(stored, 32)


OUTS = [("y_prompt", (1, SEQ, D)), ("y_sample", (NB, NQ, D)), ("hgrn_prompt", (1, 1, H, P, P)),
        ("k_prompt", (1, SEQ, BH, DH)), ("v_prompt", (1, SEQ, BH, DH)), ("logf_prompt", (1, SEQ, BH)),
        ("hgrn_sample", (1, NB, H, P, P)), ("k_sample", (NB, NQ, BH, DH)), ("v_sample", (NB, NQ, BH, DH)),
        ("logf_sample", (NB, NQ, BH))]


def ffn(k, name, layer, gain):
    with ExitStack() as st:
        st.enter_context(with_split(k, name))
        fh, fl = (k.sb(st, name + n, [P, KF, T], F32R) for n in ("_fh", "_fl"))
        dense(k, name + "gu", k.w["w_gate_up"][layer], KD, 1, k.xh, k.xl, KF, lambda i, u: i * P + u * FF, None,
              swiglu=(fh[:].rearrange("p k n -> p (k n)"), fl[:].rearrange("p k n -> p (k n)")), gain=gain)
        dense(k, name + "dn", k.w["w_down"][layer], KF // 2, 2, fh, fl, KD // 2, lambda i, u: (i * 2 + u) * P,
              add_to_stream(k))


def add_to_stream(k):
    flat = k.xT[:].rearrange("p k n -> p (k n)")

    def evacuate(dve, i, u, ps):
        x = halves(flat[:, bass.ds((i * 2 + u) * T, T)])
        return dve.tensor_tensor(x, x, ps, ALU.add)
    return evacuate


def store_to(flat, first=0):
    def evacuate(dve, i, u, ps):
        return dve.tensor_copy(halves(flat[:, bass.ds((i * 2 + u + first) * T, T)]), ps)
    return evacuate


def program(nc, a, outs):
    with ExitStack() as stack:
        k = Core(nc, stack)
        k.w, k.out = a, outs
        k.x_prompt, k.x_sample, k.state_hgrn = a["x_prompt"], a["x_sample"], a["state_hgrn"]
        sb = lambda name, shape, dt=F32: k.sb(stack, name, shape, dt)
        k.ps = stack.enter_context(nc.psum_tensor("ps", [P, 8, 512], F32))
        k.xT = sb("xT", [P, KD, T])
        k.ident, k.mean, k.headmean = sb("ident", [P, P]), sb("mean", [P, P]), sb("headmean", [P, P])
        k.eps = sb("eps", [P, 1])
        k.lb, k.a_lb = sb("lb", [P, KD, 2]), sb("a_lbT", [P, KD])
        k.n_pool = a["cache_k"].shape[0]
        k.cum_prompt = nc.dram_tensor("cum_prompt", [4, BH, SEQ], F32).ap()
        k.neg_decay = nc.dram_tensor("neg_decay", [2, NB * BH, PAST + NQ], F32).ap()
        k.new_decay = nc.dram_tensor("new_decay", [2, NB, BH * NQ], F32).ap()
        k.qn8 = sb("qn8", [P, 1])
        gains = {n: sb("g_" + n, [P, KD]) for n in ("a_norm", "kv_norm", "b_norm", "ffn0", "ffn1")}
        k.onorm, k.qn, k.kn = sb("onorm", [P, 1]), sb("qn", [P, 1]), sb("kn", [P, 1])
        k.const_loads = [(k.ident[:], a["c_ident"]), (k.mean[:], a["c_mean"]), (k.headmean[:], a["c_headmean"]),
                         (k.eps[:], a["c_eps"]),
                         (k.a_lb[:], a["a_lb"][0].rearrange("(k p) -> p k", p=P)),
                         (gains["a_norm"][:], a["a_norm"][0].rearrange("(k p) -> p k", p=P)),
                         (gains["kv_norm"][:], a["kv_norm"].rearrange("(k p) -> p k", p=P)),
                         (gains["b_norm"][:], a["b_norm"][0].rearrange("(k p) -> p k", p=P)),
                         (gains["ffn0"][:], a["ffn_norm"][0].rearrange("(k p) -> p k", p=P)),
                         (gains["ffn1"][:], a["ffn_norm"][1].rearrange("(k p) -> p k", p=P)),
                         (k.onorm[:], a["a_onorm"][0].rearrange("(p o) -> p o", o=1))]
        for half in range(2):
            k.const_loads += [(k.qn[half * DH:(half + 1) * DH, :], a["q_norm"][0].rearrange("(p o) -> p o", o=1)),
                              (k.kn[half * DH:(half + 1) * DH, :], a["k_norm"].rearrange("(p o) -> p o", o=1))]
        load_inputs(k)
        lower_bound(k)
        with ExitStack() as hg:
            k.z = k.sb(hg, "z", [P, 4 * H, T])
            with with_split(k, "ax"):
                dense(k, "win", a["a_w_in"][0], KD, 1, k.xh, k.xl, 2 * H, lambda i, u: (i * 2 + u) * P,
                      store_to(k.z[:].rearrange("p k n -> p (k n)")), gain=gains["a_norm"])
            with ExitStack() as heads:
                k.keys, k.tiny = k.sb(heads, "hg_keys", [P, H * T]), k.sb(heads, "hg_tiny", [P, H * T])
                hgrn_inputs(k, heads)
                hgrn(k)
            with with_split(k, "hx"):
                dense(k, "wout", a["a_w_out"][0], KD, 1, k.xh, k.xl, KD // 2, lambda i, u: (i * 2 + u) * P, add_to_stream(k),
                      before=HeadOutputs(k))
        k.retire()
        ffn(k, "f0", 0, gains["ffn0"])
        k.retire()
        fox(k, gains)
        ffn(k, "f1", 1, gains["ffn1"])
        store_y(k)


_INS = ["x_prompt", "x_sample", "state_hgrn", "cache_k", "cache_v", "cache_logf", "page_table", "a_norm", "a_w_in", "a_lb",
        "a_onorm", "a_w_out", "kv_norm", "w_kvf", "b_f", "k_norm", "b_norm", "b_wq", "q_norm", "b_wo", "ffn_norm",
        "w_gate_up", "w_down"]


def kernel(**inputs):
    from concourse import bacc
    from concourse.bass_utils import run_bass_kernel_spmd

    nc = bacc.Bacc("TRN2", target_bir_lowering=False, num_devices=1)
    arrays = {n: np.ascontiguousarray(inputs[n]) for n in _INS}
    arrays.update(shape_constants())
    arrays["c_eps"] = np.full((P, 1), EPS, np.float32)
    aps = {n: nc.dram_tensor("in_" + n, v.shape, mybir.dt.from_np(v.dtype), kind="ExternalInput").ap()
           for n, v in arrays.items()}
    outs = {n: nc.dram_tensor("out_" + n, s, F32, kind="ExternalOutput").ap() for n, s in OUTS}
    program(nc, aps, outs)
    r = run_bass_kernel_spmd(nc, [{"in_" + n: v for n, v in arrays.items()}], core_ids=[0])
    return tuple(r.results[0]["out_" + n] for n, _ in OUTS)
```
